# Optimizing a Trainium2 kernel written in Bass

```python
import jax, jax.numpy as jnp
from jax import lax
import numpy as np

D_MODEL = 1024
BATCH = 1
SEQ = 1024
DEPTH = 1

PLE_DIM = 256
RWKV_WIDTH = 512
RWKV_HEAD = 64
RWKV_HEADS = RWKV_WIDTH // RWKV_HEAD
DECAY_LORA = 64
AAA_LORA = 64
GATE_LORA = 128
GMLP_WIDTH = D_MODEL - RWKV_WIDTH
GMLP_HEADS = 8
GMLP_HEAD = GMLP_WIDTH // GMLP_HEADS
CHUNK = 128
D_FF = 2816
RMS_EPS = 1e-6
LN_EPS = 1e-5
GN_EPS = 64e-5
RWKV_COLS = 3 * RWKV_WIDTH + DECAY_LORA + AAA_LORA + GATE_LORA
IN_COLS = RWKV_COLS + 2 * GMLP_WIDTH
RWKV_SPLITS = (RWKV_WIDTH, 2 * RWKV_WIDTH, 3 * RWKV_WIDTH,
               3 * RWKV_WIDTH + DECAY_LORA, 3 * RWKV_WIDTH + DECAY_LORA + AAA_LORA)

kernel_name = 'hybrid_rwkv7_chunked_gmlp_macaron_ple'

def rms_norm(x, g):
    xf = x.astype(jnp.float32)
    y = xf * lax.rsqrt(jnp.mean(xf * xf, axis=-1, keepdims=True) + RMS_EPS)
    return (y * g.astype(jnp.float32)).astype(x.dtype)

def layer_norm(x, g, b, eps):
    xf = x.astype(jnp.float32)
    mu = jnp.mean(xf, axis=-1, keepdims=True)
    var = jnp.mean(jnp.square(xf - mu), axis=-1, keepdims=True)
    y = (xf - mu) * lax.rsqrt(var + eps)
    return (y * g.astype(jnp.float32) + b.astype(jnp.float32)).astype(x.dtype)

def swiglu(x, w1, w3, w2):
    return (jax.nn.silu(x @ w1) * (x @ w3)) @ w2

def token_shift(z, mu):
    z_prev = jnp.pad(z[:, :-1], ((0, 0), (1, 0), (0, 0)))
    return z + (z_prev - z) * mu

def rwkv7_recurrence(r, decay, k, v, kk, a):
    B, T, H, N = r.shape

    def step(S, inp):
        r_t, d_t, k_t, v_t, kk_t, a_t = inp
        sa = jnp.einsum('bhvk,bhk->bhv', S, -kk_t)
        S = (S * d_t[:, :, None, :]
             + sa[..., None] * (kk_t * a_t)[:, :, None, :]
             + v_t[..., None] * k_t[:, :, None, :])
        y_t = jnp.einsum('bhvk,bhk->bhv', S, r_t)
        return S, y_t

    xs = (jnp.moveaxis(r, 1, 0), jnp.moveaxis(decay, 1, 0), jnp.moveaxis(k, 1, 0),
          jnp.moveaxis(v, 1, 0), jnp.moveaxis(kk, 1, 0), jnp.moveaxis(a, 1, 0))
    S0 = jnp.zeros((B, H, N, N), jnp.float32)
    _, y = lax.scan(step, S0, xs)
    return jnp.moveaxis(y, 0, 1)

def rwkv7_group(z, mu, w0, w_decay, a0, w_aaa, w_gate, k_k, k_a, r_k, gn_g, gn_b):
    B, T, _ = z.shape
    H, N = RWKV_HEADS, RWKV_HEAD
    z = token_shift(z, mu)
    r, k, v, zw, za, zg = jnp.split(z, RWKV_SPLITS, axis=-1)
    logw = -jax.nn.softplus(-(w0 + jnp.tanh(zw) @ w_decay)) - 0.5
    decay = jnp.exp(-jnp.exp(logw.astype(jnp.float32)))
    a = jax.nn.sigmoid(a0 + za @ w_aaa)
    g = jax.nn.sigmoid(zg) @ w_gate
    kk = (k * k_k).reshape(B, T, H, N).astype(jnp.float32)
    kk = kk / jnp.maximum(jnp.linalg.norm(kk, axis=-1, keepdims=True), 1e-12)
    k = k * (1.0 + (a - 1.0) * k_a)
    hd = lambda t: t.reshape(B, T, H, N).astype(jnp.float32)
    r4, k4, v4, a4, d4 = hd(r), hd(k), hd(v), hd(a), hd(decay)
    y = rwkv7_recurrence(r4, d4, k4, v4, kk, a4)
    y = layer_norm(y, gn_g.reshape(H, N), gn_b.reshape(H, N), GN_EPS)
    y = y + jnp.sum(r4 * k4 * r_k.astype(jnp.float32), axis=-1, keepdims=True) * v4
    return (y.reshape(B, T, RWKV_WIDTH) * g).astype(z.dtype)

def chunked_sgu_group(z, ln_g, ln_b, w_s, b_s):
    B, T, _ = z.shape
    u, v = jnp.split(jax.nn.gelu(z, approximate=False), 2, axis=-1)
    v = layer_norm(v, ln_g, ln_b, LN_EPS)
    v = v.reshape(B, T // CHUNK, CHUNK, GMLP_HEADS, GMLP_HEAD)
    causal = jnp.tril(jnp.ones((CHUNK, CHUNK), dtype=bool))
    ws = jnp.where(causal[None], w_s, jnp.zeros_like(w_s))
    mixed = jnp.einsum('hts,bcshd->bcthd', ws, v) + b_s.T[None, None, :, :, None]
    return u * mixed.reshape(B, T, GMLP_WIDTH)

def setup_inputs(seed: int = 0) -> dict:
    key = jax.random.key(seed)
    ks = jax.random.split(key, 40)
    L, D = DEPTH, D_MODEL

    def nrm(k, shape, scale):
        return jax.random.normal(k, shape, jnp.float32) * scale

    def gain(k, shape):
        return 1.0 + nrm(k, shape, 0.05)

    return {
        'x': nrm(ks[0], (BATCH, SEQ, D), 1.0),
        'p': nrm(ks[1], (DEPTH, BATCH, SEQ, PLE_DIM), 1.0),
        'norm_ffn1': gain(ks[2], (L, D)),
        'ffn1_w1': nrm(ks[3], (L, D, D_FF), D ** -0.5),
        'ffn1_w3': nrm(ks[4], (L, D, D_FF), D ** -0.5),
        'ffn1_w2': nrm(ks[5], (L, D_FF, D), D_FF ** -0.5),
        'norm_mix': gain(ks[6], (L, D)),
        'w_in': nrm(ks[7], (L, D, IN_COLS), D ** -0.5),
        'shift_mu': jax.random.uniform(ks[8], (L, RWKV_COLS), jnp.float32),
        'rwkv_w0': jax.random.uniform(ks[9], (L, RWKV_WIDTH), jnp.float32, -6.5, -1.5),
        'rwkv_w_decay': nrm(ks[10], (L, DECAY_LORA, RWKV_WIDTH), 0.1 * DECAY_LORA ** -0.5),
        'rwkv_a0': nrm(ks[11], (L, RWKV_WIDTH), 0.1),
        'rwkv_w_aaa': nrm(ks[12], (L, AAA_LORA, RWKV_WIDTH), AAA_LORA ** -0.5),
        'rwkv_w_gate': nrm(ks[13], (L, GATE_LORA, RWKV_WIDTH), GATE_LORA ** -0.5),
        'rwkv_k_k': 0.85 + nrm(ks[14], (L, RWKV_WIDTH), 0.05),
        'rwkv_k_a': 1.0 + nrm(ks[15], (L, RWKV_WIDTH), 0.05),
        'rwkv_r_k': nrm(ks[16], (L, RWKV_HEADS, RWKV_HEAD), 0.1),
        'rwkv_gn_g': gain(ks[17], (L, RWKV_WIDTH)),
        'rwkv_gn_b': nrm(ks[18], (L, RWKV_WIDTH), 0.02),
        'sgu_ln_g': gain(ks[19], (L, GMLP_WIDTH)),
        'sgu_ln_b': nrm(ks[20], (L, GMLP_WIDTH), 0.02),
        'sgu_w_s': nrm(ks[21], (L, GMLP_HEADS, CHUNK, CHUNK), 0.5 * CHUNK ** -0.5),
        'sgu_b_s': 1.0 + nrm(ks[22], (L, GMLP_HEADS, CHUNK), 0.1),
        'w_out': nrm(ks[23], (L, D, D), D ** -0.5),
        'norm_ffn2': gain(ks[24], (L, D)),
        'ffn2_w1': nrm(ks[25], (L, D, D_FF), D ** -0.5),
        'ffn2_w3': nrm(ks[26], (L, D, D_FF), D ** -0.5),
        'ffn2_w2': nrm(ks[27], (L, D_FF, D), D_FF ** -0.5),
        'norm_ple': gain(ks[28], (L, D)),
        'w_ple_gate': nrm(ks[29], (L, D, D), D ** -0.5),
        'w_ple': nrm(ks[30], (L, PLE_DIM, D), PLE_DIM ** -0.5),
        'norm_final': gain(ks[31], (D,)),
    }

def reference(x, p, norm_ffn1, ffn1_w1, ffn1_w3, ffn1_w2, norm_mix, w_in, shift_mu,
              rwkv_w0, rwkv_w_decay, rwkv_a0, rwkv_w_aaa, rwkv_w_gate, rwkv_k_k, rwkv_k_a,
              rwkv_r_k, rwkv_gn_g, rwkv_gn_b, sgu_ln_g, sgu_ln_b, sgu_w_s, sgu_b_s, w_out,
              norm_ffn2, ffn2_w1, ffn2_w3, ffn2_w2, norm_ple, w_ple_gate, w_ple, norm_final):
    h = x
    for i in range(DEPTH):
        h = h + 0.5 * swiglu(rms_norm(h, norm_ffn1[i]), ffn1_w1[i], ffn1_w3[i], ffn1_w2[i])
        n = rms_norm(h, norm_mix[i])
        z = n @ w_in[i]
        y_rwkv = rwkv7_group(z[..., :RWKV_COLS], shift_mu[i], rwkv_w0[i], rwkv_w_decay[i],
                             rwkv_a0[i], rwkv_w_aaa[i], rwkv_w_gate[i], rwkv_k_k[i],
                             rwkv_k_a[i], rwkv_r_k[i], rwkv_gn_g[i], rwkv_gn_b[i])
        y_sgu = chunked_sgu_group(z[..., RWKV_COLS:], sgu_ln_g[i], sgu_ln_b[i],
                                  sgu_w_s[i], sgu_b_s[i])
        y = jnp.concatenate([y_rwkv, y_sgu], axis=-1)
        h = h + y @ w_out[i]
        h = h + 0.5 * swiglu(rms_norm(h, norm_ffn2[i]), ffn2_w1[i], ffn2_w3[i], ffn2_w2[i])
        gate = jax.nn.sigmoid(rms_norm(h, norm_ple[i]) @ w_ple_gate[i])
        h = h + gate * (p[i] @ w_ple[i])
    return rms_norm(h, norm_final)


_drawn_inputs = setup_inputs


def setup_inputs(seed=0):
    import zlib

    import numpy as np

    out = dict(_drawn_inputs(seed))
    spreads = {}
    factors = {'rwkv_w_decay': 8.0,
     'rwkv_a0': 4.992,
     'rwkv_k_k': 3.709,
     'rwkv_k_a': 3.522,
     'rwkv_gn_g': 3.786,
     'rwkv_gn_b': 8.0,
     'sgu_ln_g': 8.0,
     'sgu_ln_b': 30.392,
     'norm_ffn2': 3.569,
     'norm_ple': 56.784}
    for name, (base, spread) in spreads.items():
        noise = np.random.default_rng([zlib.crc32(name.encode()), seed]).standard_normal(out[name].shape)
        drawn = base * np.exp(spread * noise) if base else spread * noise
        out[name] = __import__('jax').numpy.asarray(drawn.astype(out[name].dtype))
    for name, factor in factors.items():
        out[name] = (out[name] * factor).astype(out[name].dtype)
    return out
```

```python
from contextlib import ExitStack

import numpy as np

import concourse.bass as bass
from concourse import mybir

F32 = mybir.dt.float32
F32R = mybir.dt.float32r
U32 = mybir.dt.uint32
ALU = mybir.AluOpType
ACT = mybir.ActivationFunctionType
AX_X = mybir.AxisListType.X

P = 128
NB = 512
RAW_SLOTS = 3
SPLIT_SLOTS = 6
UNIT = 1024
STAGES = "full"
MIX_CONSTS = 12


class Stage:

    def __init__(self, name, iters, body, first_unit, ring, raw_ring, unit=UNIT):
        self.name, self.iters, self.body, self.first = name, iters, body, first_unit
        self.ring, self.raw_ring, self.unit = ring, raw_ring, unit
        self.end = first_unit + iters * body

    def raw_at(self, j):
        if self.raw_ring == RAW_SLOTS:
            return (j % RAW_SLOTS) * self.unit
        return RAW_SLOTS * UNIT - 2 * self.unit + (j % 2) * self.unit

    def split_at(self, j):
        if self.ring == SPLIT_SLOTS:
            return (j % SPLIT_SLOTS) * self.unit
        return SPLIT_SLOTS * UNIT - 2 * self.unit + (j % 2) * self.unit


def build(nc, io, out):
    x, p = io["x"], io["p"]
    T, D = x.shape[1], x.shape[2]
    F = io["ffn1_w1"].shape[2]
    KD = D // P
    HALVES = T // NB
    TT = T // P
    FT = F // P
    PLE = p.shape[3]
    KP = PLE // P
    IN_COLS = io["w_in"].shape[2]
    assert D == UNIT and HALVES == 2 and FT % 2 == 0 and IN_COLS % (2 * P) == 0

    SIM_ONLY_FFN = STAGES == "ffn"

    stages, unit = {}, 0
    for name, iters, body, ring, raw_ring, width in (
        ("ffn1", FT // 2, 6, SPLIT_SLOTS, RAW_SLOTS, UNIT),
        ("w_in", IN_COLS // P // 2, 2, 2, 2, UNIT),
        ("w_out", KD // 2, 2, 2, 2, UNIT),
        ("ffn2", FT // 2, 6, SPLIT_SLOTS, RAW_SLOTS, UNIT),
        ("gate", KD // 2, 2, 2, 2, UNIT + KP * P),
    ):
        if SIM_ONLY_FFN and name in ("w_in", "w_out"):
            continue
        stages[name] = Stage(name, iters, body, unit, ring, raw_ring, width)
        unit = stages[name].end

    G = RWKV_HEADS = io["rwkv_r_k"].shape[1]
    HD = io["rwkv_r_k"].shape[2]
    RW = RWKV_HEADS * HD
    KR = RW // P
    C = P
    CHUNKS = T // C
    SHIFTED = io["shift_mu"].shape[1] // P
    ZT = IN_COLS // P
    LORA, GATE = SHIFTED - 2, SHIFTED - 1
    LEVELS = 6
    assert HD == 64 and RW == NB and io["sgu_w_s"].shape[1] == 8 and CHUNKS % 2 == 0
    FULL = not SIM_ONLY_FFN

    with ExitStack() as ctx:
        def sb(name, shape, dt=F32, where=ctx):
            return where.enter_context(nc.sbuf_tensor(name, shape, dt))

        def sem(name):
            return ctx.enter_context(nc.semaphore(name))

        def here():
            return nc.sbuf_base

        hT = sb("hT", [P, KD, T])
        aH_at = here()
        aH = sb("aH", [P, KD, T], F32R)
        aL_at = here()
        aL = sb("aL", [P, KD, T], F32R)
        wH_at = here()
        wH = sb("wH", [P, SPLIT_SLOTS * UNIT], F32R)
        wL_at = here()
        wL = sb("wL", [P, SPLIT_SLOTS * UNIT], F32R)
        raw_at = here()
        raw = sb("raw", [P, RAW_SLOTS * UNIT])
        ident = sb("ident", [P, P])
        ones = sb("ones", [P, 1])
        NORMS = ("ffn1", "mix", "ffn2", "ple", "final")
        VECTORS = {}
        n_rows = 0
        for name in ("norm_ffn1", "norm_mix", "norm_ffn2", "norm_ple", "norm_final", "shift_mu",
                     "rwkv_a0", "rwkv_k_k", "rwkv_k_a", "rwkv_r_k"):
            VECTORS[name] = n_rows
            n_rows += int(np.prod(io[name].shape)) // P
        vec_rows = sb("vec_rows", [n_rows, P])
        vecs = sb("vecs", [P, n_rows])
        rms_eps = sb("rms_eps", [P, 1])
        zero = sb("zero", [P, 1])

        psum = ctx.enter_context(nc.psum_tensor("psum", [P, 8, NB], F32))

        sq_at = here()
        sq = sb("sq", [P, 4, NB])
        nrm = sb("nrm", [P, 2, NB])
        rms = sb("rms", [P, TT])
        rstd = sb("rstd", [P, TT])
        with ExitStack() as x_phase:
            xs = sb("xs", [P, TT, D], F32, x_phase)
        hid_at = nc.sbuf_base
        with ExitStack() as ffn_phase:
            hidH = sb("hidH", [P, 2, T], F32R, ffn_phase)
            hidL = sb("hidL", [P, 2, T], F32R, ffn_phase)
            silu = sb("silu", [P, 2, NB], F32, ffn_phase)
            hid = sb("hid", [P, 2, NB], F32, ffn_phase)
        with ExitStack() as ple_phase:
            pTH = sb("pTH", [P, KP, T], F32R, ple_phase)
            pTL = sb("pTL", [P, KP, T], F32R, ple_phase)
            p_rows = sb("p_rows", [P, TT, PLE], F32, ple_phase)
            gated = sb("gated", [P, 2, NB], F32, ple_phase)
            outs = sb("outs", [P, 2, D], F32, ple_phase)
        assert HALVES * NB == T

        KB = 1024
        spaces = [[hid_at, nc.sbuf_usable_end],
                  [wH_at, wH_at + 4 * UNIT * 4],
                  [wL_at, wL_at + 4 * UNIT * 4],
                  [sq_at, sq_at + 6 * NB * 4],
                  [aH_at, aH_at + KD * T * 4],
                  [raw_at, raw_at + UNIT * 4]]
        used = [(a + 31) // 32 * 32 for a, _ in spaces]
        placed = {}

        def over(name, shape, dt=F32, space=None):
            size = int(np.prod(shape[1:])) * (1 if dt == mybir.dt.uint8 else 4)
            size = (size + 31) // 32 * 32
            for n in (range(len(spaces)) if space is None else space):
                if used[n] + size <= spaces[n][1]:
                    at = used[n]
                    used[n] += size
                    placed[name] = at
                    return nc.alloc_sbuf_tensor_at(name, shape, dt, offset=at)
            raise AssertionError(f"no room for {name}: {[(b - u) for (a, b), u in zip(spaces, used)]}")

        def within(name, shape, other, offset):
            return nc.alloc_sbuf_tensor_at(name, shape, F32, offset=placed[other] + offset)

        if FULL:
            CONST = (1, 2, 0)
            WORK = (4, 3, 2, 1, 5, 0)
            zout = over("zout", [P, 2, T + 1], F32, (0,))
            shape_masks = over("shape_masks", [P, io["masks"].shape[1]], F32, CONST)
            w_lora = over("w_lora", [P, RW], F32, CONST)
            w_gate = over("w_gate", [P, RW], F32, CONST)
            w0_rows = over("w0_rows", [P, RW], F32, CONST)
            gn_g = over("gn_g", [P, RW], F32, CONST)
            gn_b = over("gn_b", [P, RW], F32, CONST)
            ln_g = over("ln_g", [P, NB], F32, CONST)
            ln_b = over("ln_b", [P, NB], F32, CONST)
            wsT = over("wsT", [P, 8, P], F32, CONST)
            b_s = over("b_s", [P, KR, P], F32, CONST)
            rk_heads = over("rk_heads", [P, KR, 2], F32, CONST)
            neg_half = over("neg_half", [P, 1], F32, CONST)
            ka_rest = over("ka_rest", [P, KR], F32, CONST)
            ws_rows = over("ws_rows", [P, 8, P], F32, (0,))
            used[0] = placed["zout"]
            y_out = nc.alloc_sbuf_tensor_at("y_out", [P, KD, T], F32, offset=aL_at)

            zc = over("zc", [P, SHIFTED, C + 1], F32, WORK)
            gc = over("gc", [P, 2 * KR, C], F32, WORK)
            zs = over("zs", [P, SHIFTED, C], F32, WORK)
            tanh_w = over("tanh_w", [P, C], F32, WORK)
            sig_g = over("sig_g", [P, C], F32, WORK)
            sig_w = over("sig_w", [P, RW], F32, WORK)
            e_in = over("e_in", [P, KR, C], F32, WORK)
            e_ex = over("e_ex", [P, KR, C], F32, WORK)
            e_neg = over("e_neg", [P, KR, C], F32, WORK)
            e_mid = over("e_mid", [P, 2, KR], F32, WORK)
            e_end = over("e_end", [P, 2, KR], F32, WORK)
            carry = over("carry", [P, KR], F32, WORK)
            aT = over("aT", [P, KR, C], F32, WORK)
            kkT = over("kkT", [P, KR, C], F32, WORK)
            tmpT = over("tmpT", [P, KR, C], F32, WORK)
            kpT = over("kpT", [P, KR, C], F32, WORK)
            rkT = over("rkT", [P, KR, C], F32, WORK)
            prT = [over(f"prT{b}", [P, KR, 2, C], F32, WORK) for b in range(2)]
            bT = over("bT", [P, KR, C], F32, WORK)
            kT = over("kT", [P, KR, C], F32, WORK)
            p_nat = over("p_nat", [P, RW], F32, WORK)
            b_nat = over("b_nat", [P, RW], F32, WORK)
            k_nat = over("k_nat", [P, RW], F32, WORK)
            v_nat = over("v_nat", [P, RW], F32, WORK)
            g_nat = [over(f"g_nat{b}", [P, RW], F32, WORK) for b in range(2)]
            bonus = over("bonus", [P, 2, G], F32, WORK)
            kk_rn = over("kk_rn", [P, G], F32, WORK)
            nT = over("nT", [P, G, C], F32, WORK)
            xq = over("xq", [P, G, 2, C], F32, WORK)
            mq = over("mq", [P, G, 2, C], F32, WORK)
            xT = over("xT", [P, G, C], F32, WORK)
            yb = over("yb", [P, G, C], F32, WORK)
            tpT = within("tpT", [P, KR, C], "xT", 0)
            gv = within("gv", [P, RW], "yb", 0)
            u_nat = within("u_nat", [P, RW], "yb", RW * 4)
            state = over("state", [P, KR, HD], F32, WORK)
            state_sum = over("state_sum", [P, KR, HD], F32, WORK)
            yc = over("yc", [P, RW], F32, WORK)
            ysq = over("ysq", [P, RW], F32, WORK)
            bv = over("bv", [P, RW], F32, WORK)
            mean = over("mean", [P, G], F32, WORK)
            var = over("var", [P, G], F32, WORK)
            v_stats = over("v_stats", [P, 6], F32, WORK)
            v_mv = over("v_mv", [P, 2], F32, WORK)
            v_rs = over("v_rs", [P, 1], F32, WORK)
            vn = over("vn", [P, NB], F32, WORK)
            mixed = over("mixed", [P, KR, C], F32, WORK)

            decay_sums = shape_masks[:, 0:2 * C]
            lower = shape_masks[:, 2 * C:3 * C]
            band_incl = shape_masks[:, 3 * C:5 * C]
            strict_incl = shape_masks[:, 5 * C:7 * C]
            head_cols = shape_masks[:, 7 * C:7 * C + 2]
            merge_masks = (shape_masks[:, 7 * C + 2:7 * C + 2 + LEVELS * P].bitcast(U32)
                           .rearrange("p (l c) -> p l c", c=P))

        raw_ready = {n: [sem(f"raw_ready_{n}{i}") for i in range(s.raw_ring)] for n, s in stages.items()}
        high_done = sem("high_done")
        w_split = sem("w_split")
        w_free = sem("w_free")

        const_ready = sem("const_ready")
        made = sem("made")
        x_ready = [sem(f"x_ready{i}") for i in range(TT // 2)]
        x_turned = sem("x_turned")
        vecs_turned = sem("vecs_turned")
        vecs_ready = sem("vecs_ready")
        x_used_act = sem("x_used_act")
        x_used_dve = sem("x_used_dve")
        tiles = HALVES * KD
        NORM_PER = dict(squared=tiles, sq_used=tiles, summed=HALVES, rooted=HALVES, inverted=HALVES,
                        spread=HALVES, scaled=tiles, high=tiles, ready=tiles)
        norm = {k: sem(f"norm_{k}") for k in NORM_PER}
        NORM_ORDER = [n for n in NORMS if not (SIM_ONLY_FFN and n == "mix")]

        def in_norm(name, k, count):
            return NORM_ORDER.index(name) * NORM_PER[k] + count

        ffn = {}
        for n in ("ffn1", "ffn2"):
            ffn[n] = {k: sem(f"{n}_{k}") for k in
                      ("up", "silued", "product", "high", "hid_ready", "down", "added")}
        pT = {k: sem(f"p_{k}") for k in ("loaded", "turned", "high", "ready")}
        gate = {k: sem(f"gate_{k}") for k in ("done", "sigmoid", "product", "added")}
        fin = {k: sem(f"result_{k}") for k in ("turned", "copied_act", "copied_dve", "stored0", "stored1")}

        if FULL:
            win = {k: sem(f"w_in_{k}") for k in ("done", "copied")}
            z_stored = [sem("z_stored0"), sem("z_stored1")]
            mix_consts = sem("mix_consts")
            mix_made = sem("mix_made")
            ws_turned = sem("ws_turned")
            ws_placed = sem("ws_placed")
            y_high = sem("y_high")
            delta_seen = sem("delta_seen")
            y_split = sem("y_split")
            w_out_done = sem("w_out_done")
            w_out_added = sem("w_out_added")
            z_scratch = nc.dram_tensor("z_scratch", (ZT * P, T + 1), F32, kind="Internal").ap()
            PER = dict(
                z_loaded=16, g_loaded=16, shifted=6, lora_in=2, w_raw=1, a_raw=1, g_raw=1, w_biased=1,
                w_sig=1, a_ready=1, g_ready=1, decays=1, exps=5, kk_raw=2, kk_sums=1, kk_clamped=1,
                kk_rn=1, kk_spread=1, kk_unit=1, pr_ready=2, kk_a=1, b_ready=1, kp=3, k_ready=1,
                rk=1, bonus_raw=1, bonus=1, gelu=1, v_turned=1, v_stats=1, v_mv=1, v_ve=1, v_rs=1,
                v_norm=1, v_affine=2, mixed=1, mixed_b=1, sgu=1,
                nat_turned=4, nat_act=2, nat_dve=2, gram=10, gram_used=10, x_init=2,
                xt=12, xt_copied=12, y=12, y_copied=12, delta=12, x_upd=12, bv=1,
                tp=1, tp_copied=1, gmk=1, gmk_copied=1, u=1, u_copied=1, s_new=1, y_raw=1,
                s_sum=1, carry=1, state=1, mean=2, yc=1, ysq=1, var=2, y_rs=1, y_fin=5,
                y_turned=1, y_placed=1)
            ev = {k: sem("c_" + k) for k in PER}

            def at(name, c, k=None):
                n = PER[name]
                return (c + 2) * n + (n if k is None else k)

        io_w = {"ffn1": ("ffn1_w1", "ffn1_w3", "ffn1_w2"), "ffn2": ("ffn2_w1", "ffn2_w3", "ffn2_w2")}

        def columns_of(w, m, k):
            return io[w][0].rearrange("(k p) c -> p k c", p=P)[:, :k, bass.ts(m, P)]

        def rows_of(w, m):
            return io[w][0][bass.ts(m, P), :]

        block = ctx.enter_context(nc.Block())

        @block.sync
        def _(sp):
            def tile_source(s, i, j):
                if s.name in io_w:
                    w1, w3, w2 = io_w[s.name]
                    m = i * 2 + (j // 2 if j < 4 else j - 4)
                    if j < 4:
                        return columns_of((w1, w3)[j % 2], m, KD)
                    return rows_of(w2, m)
                return columns_of({"w_in": "w_in", "w_out": "w_out", "gate": "w_ple_gate"}[s.name],
                                  i * 2 + j, KD)

            def load_chunk(c):
                sp.wait_ge(ev["shifted"], at("shifted", c - 1))
                sp.dma_start(zc[:], z_scratch[0:SHIFTED * P, bass.ds(c * C, C + 1)]
                             .rearrange("(k p) c -> p k c", p=P)).then_inc(ev["z_loaded"], 16)
                sp.wait_ge(ev["sgu"], at("sgu", c - 1))
                sp.dma_start(gc[:], z_scratch[SHIFTED * P:ZT * P, bass.ds(c * C + 1, C)]
                             .rearrange("(k p) c -> p k c", p=P)).then_inc(ev["g_loaded"], 16)

            for s in stages.values():
                if s.name == "w_out":
                    for j in range(2):
                        sp.wait_ge(z_stored[j], 16 * (1 + ZT // 2))
                    load_chunk(0)
                    with sp.Fori(1, CHUNKS) as c:
                        load_chunk(c)
                with sp.Fori(0, s.iters) as i:
                    for j in range(s.body):
                        u = i * s.body + (s.first + j)
                        sp.wait_ge(w_split, u + (1 + RAW_SLOTS - s.raw_ring))
                        slot = s.raw_at(j)
                        dst = raw[:, slot:slot + UNIT]
                        src = tile_source(s, i, j)
                        if len(src.shape) == 3:
                            dst = dst.rearrange("p (k c) -> p k c", c=P)
                        ready = raw_ready[s.name][j % s.raw_ring]
                        sp.dma_start(dst, src).then_inc(ready, 16)
                        if s.name == "gate":
                            sp.dma_start(
                                raw[:, slot + UNIT:slot + s.unit].rearrange("p (k c) -> p k c", c=P),
                                columns_of("w_ple", i * 2 + j, KP)).then_inc(ready, 16)

        @block.gpsimd
        def _(pool):
            pool.sem_inc(w_split, RAW_SLOTS)
            pool.memset(ident[:], 0.0).then_inc(made, 1)
            pool.memset(ones[:], 1.0).then_inc(made, 1)
            pool.memset(rms_eps[:], 1e-6).then_inc(made, 1)
            pool.memset(zero[:], 0.0).then_inc(made, 1)
            pool.wait_ge(made, 4)
            pool.affine_select(out=ident[:], in_=ident[:], compare_op=ALU.not_equal, fill=1.0,
                               base=0, pattern=[[-1, P]], channel_multiplier=1).then_inc(made, 1)
            if FULL:
                for k, n in PER.items():
                    pool.sem_inc(ev[k], 2 * n)

            def shift(c, tiles, k):
                n = tiles.stop - tiles.start
                mu0 = VECTORS["shift_mu"]
                mu = vecs[:, mu0 + tiles.start:mu0 + tiles.stop].unsqueeze(2).to_broadcast([P, n, C])
                pool.tensor_tensor(zs[:, tiles, :], zc[:, tiles, 0:C], zc[:, tiles, 1:C + 1],
                                   ALU.subtract).then_inc(ev["shifted"], 1)
                pool.wait_ge(ev["shifted"], at("shifted", c, k + 1))
                pool.tensor_tensor(zs[:, tiles, :], zs[:, tiles, :], mu, ALU.mult).then_inc(ev["shifted"], 1)
                pool.wait_ge(ev["shifted"], at("shifted", c, k + 2))
                pool.tensor_tensor(zs[:, tiles, :], zs[:, tiles, :], zc[:, tiles, 1:C + 1],
                                   ALU.add).then_inc(ev["shifted"], 1)

            def wide(name, k=KR):
                v = VECTORS[name]
                return vecs[:, v:v + k].unsqueeze(2).to_broadcast([P, k, C])

            def pool_front(c):
                pool.wait_ge(ev["z_loaded"], at("z_loaded", c))
                pool.wait_ge(ev["nat_turned"], at("nat_turned", c - 1))
                pool.wait_ge(ev["pr_ready"], at("pr_ready", c - 1))
                pool.wait_ge(ev["a_raw"], at("a_raw", c - 1))
                shift(c, slice(LORA, SHIFTED), 0)
                pool.wait_ge(ev["k_ready"], at("k_ready", c - 1))
                shift(c, slice(0, LORA), 3)
                pool.wait_ge(ev["shifted"], at("shifted", c))
                pool.wait_ge(ev["kk_unit"], at("kk_unit", c - 1))
                pool.wait_ge(ev["b_ready"], at("b_ready", c - 1))
                kz, rz = zs[:, KR:2 * KR, :], zs[:, 0:KR, :]
                pool.tensor_tensor(kkT[:], kz, wide("rwkv_k_k"), ALU.mult).then_inc(ev["kk_raw"], 1)
                pool.wait_ge(ev["kk_raw"], at("kk_raw", c, 1))
                pool.tensor_tensor(tmpT[:], kkT[:], kkT[:], ALU.mult).then_inc(ev["kk_raw"], 1)
                pool.wait_ge(ev["v_ve"], at("v_ve", c))
                pool.tensor_tensor(v_rs[:], v_mv[:, 1:2], neg_half[:], ALU.pow).then_inc(ev["v_rs"], 1)
                pool.wait_ge(ev["kk_clamped"], at("kk_clamped", c))
                pool.tensor_tensor(kk_rn[:], kk_rn[:], neg_half[:].to_broadcast([P, G]),
                                   ALU.pow).then_inc(ev["kk_rn"], 1)
                pool.wait_ge(ev["a_ready"], at("a_ready", c))
                pool.tensor_tensor(kpT[:], aT[:], wide("rwkv_k_a"), ALU.mult).then_inc(ev["kp"], 1)
                pool.wait_ge(ev["kp"], at("kp", c, 1))
                pool.tensor_tensor(kpT[:], kpT[:], ka_rest[:].unsqueeze(2).to_broadcast([P, KR, C]),
                                   ALU.add).then_inc(ev["kp"], 1)
                pool.wait_ge(ev["kp"], at("kp", c, 2))
                pool.tensor_tensor(kpT[:], kpT[:], kz, ALU.mult).then_inc(ev["kp"], 1)
                pool.wait_ge(ev["kp"], at("kp", c))
                pool.wait_ge(ev["bonus_raw"], at("bonus_raw", c - 1))
                pool.tensor_tensor(rkT[:], rz, kpT[:], ALU.mult).then_inc(ev["rk"], 1)
                pool.wait_ge(ev["v_norm"], at("v_norm", c))
                pool.tensor_tensor(vn[:], vn[:], ln_g[:], ALU.mult).then_inc(ev["v_affine"], 1)
                pool.wait_ge(ev["v_affine"], at("v_affine", c, 1))
                pool.tensor_tensor(vn[:], vn[:], ln_b[:], ALU.add).then_inc(ev["v_affine"], 1)

            def head_wide(x):
                return x.unsqueeze(2).to_broadcast([P, G, HD])

            def heads(x):
                return x.rearrange("p (h d) -> p h d", d=HD)

            def pool_tail(c, par):
                pool.wait_ge(ev["var"], at("var", c))
                pool.tensor_tensor(var[:], var[:], neg_half[:].to_broadcast([P, G]), ALU.pow).then_inc(ev["y_rs"], 1)
                pool.wait_ge(ev["y_rs"], at("y_rs", c))
                pool.tensor_tensor(heads(yc[:]), heads(yc[:]), head_wide(var[:]), ALU.mult).then_inc(ev["y_fin"], 1)
                for k, (op, other) in enumerate(((ALU.mult, gn_g), (ALU.add, gn_b), (ALU.add, bv),
                                                 (ALU.mult, g_nat[par]))):
                    pool.wait_ge(ev["y_fin"], at("y_fin", c, k + 1))
                    pool.tensor_tensor(yc[:], yc[:], other[:], op).then_inc(ev["y_fin"], 1)

            def pool_rest(c, par, first, last):
                for g in range(2):
                    pool.wait_ge(ev["gram_used"], at("gram_used", c, 2 * g + 2))
                    x = xq[:, 4 * g:4 * g + 4, 0, :]
                    pool.tensor_tensor(x, x, ident[:].unsqueeze(1).to_broadcast([P, 4, C]),
                                       ALU.add).then_inc(ev["x_init"], 1)
                if not first:
                    pool_tail(c - 1, 1 - par)
                pool.wait_ge(ev["bonus"], at("bonus", c))
                pool.wait_ge(ev["nat_dve"], at("nat_dve", c))
                if not first:
                    pool.wait_ge(ev["y_fin"], at("y_fin", c - 1))
                pool.tensor_tensor(heads(bv[:]), heads(v_nat[:]), head_wide(bonus[:, par, :]),
                                   ALU.mult).then_inc(ev["bv"], 1)
                if not last:
                    pool_front(c + 1)

            for s in stages.values():
                if s.name == "w_in":
                    pool.wait_ge(ffn["ffn1"]["added"], 4 + stages["ffn1"].iters * 2 * KD)
                    pool.memset(neg_half[:], -0.5).then_inc(mix_made, 1)
                    pool.memset(zout[:, :, 0:1], 0.0).then_inc(mix_made, 1)
                    pool.wait_ge(mix_consts, 16 * MIX_CONSTS)
                    rk = VECTORS["rwkv_r_k"]
                    pool.tensor_tensor(rk_heads[:], vecs[:, rk:rk + KR].unsqueeze(2).to_broadcast([P, KR, 2]),
                                       head_cols.unsqueeze(1).to_broadcast([P, KR, 2]),
                                       ALU.mult).then_inc(mix_made, 1)
                    ka = VECTORS["rwkv_k_a"]
                    pool.tensor_tensor(ka_rest[:], ones[:].to_broadcast([P, KR]), vecs[:, ka:ka + KR],
                                       ALU.subtract).then_inc(mix_made, 1)
                if s.name == "w_out":
                    pool.wait_ge(win["copied"], 4 + 2 * ZT)
                    for j in range(2):
                        pool.wait_ge(z_stored[j], 16 * (1 + ZT // 2))
                    pool.wait_ge(ws_placed, 2)
                    pool.memset(state[:], 0.0).then_inc(mix_made, 1)
                    pool_front(0)
                    pool_rest(0, 0, True, False)
                    with pool.Fori(0, CHUNKS // 2 - 1) as i:
                        for b in range(2):
                            pool_rest(i * 2 + (1 + b), 1 - b, False, False)
                    pool_rest(CHUNKS - 1, 1, False, True)
                    pool_tail(CHUNKS - 1, 1)
                per = 2 if s.name == "gate" else 1
                with pool.Fori(0, s.iters) as i:
                    for j in range(s.body):
                        u = i * s.body + (s.first + j)
                        turns = s.body // s.raw_ring
                        landed = (i * turns + (j // s.raw_ring + 1)) * (16 * per)
                        pool.wait_ge(raw_ready[s.name][j % s.raw_ring], landed)
                        pool.wait_ge(w_free, u + (1 + SPLIT_SLOTS - s.ring))
                        r, w = s.raw_at(j), s.split_at(j)
                        pool.tensor_tensor(wH[:, w:w + s.unit], raw[:, r:r + s.unit],
                                           zero[:].to_broadcast([P, s.unit]), ALU.add).then_inc(high_done, 1)
                        pool.wait_ge(high_done, u + 1)
                        pool.tensor_tensor(wL[:, w:w + s.unit], raw[:, r:r + s.unit],
                                           wH[:, w:w + s.unit].bitcast(F32),
                                           ALU.subtract).then_inc(w_split, 1)

        @block.tensor
        def _(pe):
            pe.sem_inc(w_free, SPLIT_SLOTS)

            def products(acc, wat, actH, actL, first, last):
                pe.matmul(acc, wH[:, wat:wat + P], actH, start=first, stop=False)
                pe.matmul(acc, wH[:, wat:wat + P], actL, start=False, stop=False)
                return pe.matmul(acc, wL[:, wat:wat + P], actH, start=False, stop=last)

            def half(h):
                return slice(h * NB, (h + 1) * NB)

            def turn_x():
                pe.wait_ge(made, 5)
                pe.wait_ge(const_ready, 16 * len(VECTORS))
                pe.transpose(psum[:, 4, 0:n_rows], vec_rows[:], ident[0:n_rows, 0:n_rows]).then_inc(vecs_turned, 1)
                for t in range(TT):
                    if t % 2 == 0:
                        pe.wait_ge(x_ready[t // 2], 16)
                    for q in range(2):
                        if t >= 2:
                            pe.wait_ge(x_used_dve if q == 0 else x_used_act, t - 1)
                        for k in range(4):
                            m = pe.transpose(psum[:, 2 * (t % 2) + q, k * P:(k + 1) * P],
                                             xs[:, t, (4 * q + k) * P:(4 * q + k + 1) * P], ident[:])
                        m.then_inc(x_turned, 1)

            def norm_sums(name):
                for h in range(HALVES):
                    bank = 3 * h
                    per = NB // P
                    for k in range(KD):
                        pe.wait_ge(norm["squared"], in_norm(name, "squared", h * KD + k + 1))
                        for t in range(per):
                            m = pe.matmul(psum[:, bank, k * per + t:k * per + t + 1],
                                          sq[:, k % 4, t * P:(t + 1) * P], ones[:], start=True, stop=True)
                        m.then_inc(norm["sq_used"], 1)
                    pe.wait_ge(norm["inverted"], in_norm(name, "inverted", h + 1))
                    for t in range(per):
                        c = h * per + t
                        m = pe.matmul(psum[:, bank, t * P:(t + 1) * P],
                                      rstd[:, c:c + 1].to_broadcast([P, P]), ident[:],
                                      start=True, stop=True)
                    m.then_inc(norm["spread"], 1)

            def ffn_products(name, st):
                s = ffn[name]
                pe.sem_inc(s["product"], 2)
                pe.sem_inc(s["added"], 4)
                with pe.Fori(0, st.iters) as i:
                    for f in range(2):
                        for h in range(HALVES):
                            for w in range(2):
                                u = 2 * f + w
                                if h == 0:
                                    pe.wait_ge(w_split, i * 6 + (st.first + u + 1 + RAW_SLOTS))
                                    if f == 0 and w == 0:
                                        pe.wait_ge(norm["ready"], in_norm(name, "ready", KD))
                                if h == 1 and f == 0 and w == 0:
                                    pe.wait_ge(norm["ready"], in_norm(name, "ready", 2 * KD))
                                bank = 2 * h + w
                                if w == 0:
                                    pe.wait_ge(s["product"], i * 4 + (2 * f + h + 1))
                                for k in range(KD):
                                    m = products(psum[:, bank, :], st.split_at(u) + k * P,
                                                 aH[:, k, half(h)], aL[:, k, half(h)],
                                                 k == 0, k == KD - 1)
                                if w == 1:
                                    m.then_inc(s["up"], 1)
                    for f in range(2):
                        pe.wait_ge(w_split, i * 6 + (st.first + 4 + f + 1 + RAW_SLOTS))
                    for h in range(HALVES):
                        pe.wait_ge(s["hid_ready"], i * 4 + (3 + h))
                        for d in range(KD):
                            bank = 4 + (h * KD + d) % 4
                            pe.wait_ge(s["added"], i * (2 * KD) + (h * KD + d + 1))
                            for f in range(2):
                                m = products(psum[:, bank, :], st.split_at(4 + f) + d * P,
                                             hidH[:, f, half(h)], hidL[:, f, half(h)],
                                             f == 0, f == 1)
                            m.then_inc(s["down"], 1)

            def turn_p():
                for t in range(TT):
                    if t == 0:
                        pe.wait_ge(pT["loaded"], 16)
                    if t >= 2:
                        pe.wait_ge(pT["ready"], t - 1)
                    for k in range(KP):
                        m = pe.transpose(psum[:, t % 2, k * P:(k + 1) * P],
                                         p_rows[:, t, k * P:(k + 1) * P], ident[:])
                    m.then_inc(pT["turned"], 1)

            def gate_products(st):
                pe.sem_inc(gate["added"], 2)
                with pe.Fori(0, st.iters) as i:
                    for j in range(2):
                        pe.wait_ge(w_split, i * 2 + (st.first + j + 1 + RAW_SLOTS))
                        for h in range(HALVES):
                            if j == 0:
                                pe.wait_ge(norm["ready"], in_norm("ple", "ready", (h + 1) * KD))
                            pe.wait_ge(gate["added"], i * 4 + (2 * j + h + 1))
                            w = st.split_at(j)
                            for k in range(KD):
                                products(psum[:, 2 * h, :], w + k * P, aH[:, k, half(h)],
                                         aL[:, k, half(h)], k == 0, k == KD - 1)
                            for k in range(KP):
                                m = products(psum[:, 2 * h + 1, :], w + UNIT + k * P,
                                             pTH[:, k, half(h)], pTL[:, k, half(h)],
                                             k == 0, k == KP - 1)
                            m.then_inc(gate["done"], 1)

            def turn_result():
                for t in range(TT):
                    if t % (NB // P) == 0:
                        pe.wait_ge(norm["ready"], in_norm("final", "ready", (t // (NB // P) + 1) * KD))
                    for q in range(2):
                        bank = 4 + (2 * t + q) % 4
                        if t >= 2:
                            pe.wait_ge(fin["copied_dve" if q == 0 else "copied_act"], t - 1)
                        for k in range(4):
                            m = pe.transpose(psum[:, bank, k * P:(k + 1) * P],
                                             hT[:, 4 * q + k, t * P:(t + 1) * P], ident[:])
                        m.then_inc(fin["turned"], 1)

            def w_in_products(st):
                pe.sem_inc(win["copied"], 4)
                with pe.Fori(0, st.iters) as i:
                    for j in range(2):
                        pe.wait_ge(w_split, i * 2 + (st.first + j + 1 + RAW_SLOTS))
                        for h in range(HALVES):
                            if j == 0:
                                pe.wait_ge(norm["ready"], in_norm("mix", "ready", (h + 1) * KD))
                            n = 2 * j + h
                            pe.wait_ge(win["copied"], i * 4 + (n + 1))
                            for k in range(KD):
                                m = products(psum[:, n, :], st.split_at(j) + k * P, aH[:, k, half(h)],
                                             aL[:, k, half(h)], k == 0, k == KD - 1)
                            m.then_inc(win["done"], 1)

            def w_out_products(st):
                pe.sem_inc(w_out_added, 4)
                with pe.Fori(0, st.iters) as i:
                    for j in range(2):
                        pe.wait_ge(w_split, i * 2 + (st.first + j + 1 + RAW_SLOTS))
                        for h in range(HALVES):
                            if j == 0:
                                pe.wait_ge(y_split, (h + 1) * KD)
                            n = 2 * j + h
                            pe.wait_ge(w_out_added, i * 4 + (n + 1))
                            for k in range(KD):
                                m = products(psum[:, n, :], st.split_at(j) + k * P, aH[:, k, half(h)],
                                             aL[:, k, half(h)], k == 0, k == KD - 1)
                            m.then_inc(w_out_done, 1)

            def turn_spatial():
                pe.wait_ge(mix_consts, 16 * MIX_CONSTS)
                for h in range(8):
                    m = pe.transpose(psum[:, 4 + h // 4, (h % 4) * P:(h % 4 + 1) * P], ws_rows[:, h, :], ident[:])
                    if h % 4 == 3:
                        m.then_inc(ws_turned, 1)

            def rows(h):
                return slice(HD * (h % 2), HD * (h % 2) + HD)

            def cols(h):
                return slice(HD * h, HD * h + HD)

            def head_at(slot):
                return 2 * (slot % 4) + slot // 4

            def mm(out, lhsT, rhs, start=True, stop=True):
                return pe.matmul(out, lhsT, rhs, start=start, stop=stop)

            def bank3(b):
                return psum[:, b, :].rearrange("p (k c) -> p k c", c=P)

            def pe_front(piece, c, par):
                if piece == 0:
                    pe.wait_ge(ev["lora_in"], at("lora_in", c, 1))
                    pe.wait_ge(ev["gram_used"], at("gram_used", c - 1, 9))
                    mm(psum[:, 4, :], tanh_w[0:64, :], w_lora[0:64, :]).then_inc(ev["w_raw"], 1)
                    pe.wait_ge(ev["gram_used"], at("gram_used", c - 1))
                    for k in range(KR):
                        m = mm(psum[:, 5, k * P:(k + 1) * P], w_lora[64:128, k * P:(k + 1) * P],
                               zs[64:128, LORA, :])
                    m.then_inc(ev["a_raw"], 1)
                    pe.wait_ge(ev["lora_in"], at("lora_in", c))
                    mm(psum[:, 6, :], sig_g[:], w_gate[:]).then_inc(ev["g_raw"], 1)
                if piece == 1:
                    pe.wait_ge(ev["gelu"], at("gelu", c))
                    pe.wait_ge(ev["sgu"], at("sgu", c - 1))
                    pe.wait_ge(ev["y_placed"], at("y_placed", c - 2))
                    for k in range(KR):
                        m = pe.transpose(psum[:, 7, k * P:(k + 1) * P], gc[:, KR + k, :], ident[:])
                    m.then_inc(ev["v_turned"], 1)
                    pe.wait_ge(ev["w_sig"], at("w_sig", c))
                    pe.wait_ge(ev["a_ready"], at("a_ready", c))
                    for k in range(KR):
                        m = mm(psum[:, 4 + k // 2, (k % 2) * 2 * C:(k % 2 + 1) * 2 * C],
                               sig_w[:, k * P:(k + 1) * P], decay_sums)
                    m.then_inc(ev["decays"], 1)
                if piece == 2:
                    pe.wait_ge(ev["kk_raw"], at("kk_raw", c))
                    pe.wait_ge(ev["g_ready"], at("g_ready", c))
                    for k in range(KR):
                        m = mm(psum[:, 6, 2 * k:2 * k + 2], tmpT[:, k, :], head_cols)
                    m.then_inc(ev["kk_sums"], 1)
                if piece == 3:
                    pe.wait_ge(ev["kk_rn"], at("kk_rn", c))
                    for h in range(G):
                        m = mm(psum[rows(h), 6, (h // 2) * P:(h // 2 + 1) * P],
                               kk_rn[:, h:h + 1].to_broadcast([P, HD]), ident[:])
                    m.then_inc(ev["kk_spread"], 1)
                if piece == 4:
                    pe.wait_ge(ev["v_affine"], at("v_affine", c))
                    for h in range(8):
                        m = mm(psum[rows(h), 7, (h // 2) * P:(h // 2 + 1) * P], vn[:, cols(h)], wsT[:, h, :])
                    m.then_inc(ev["mixed"], 1)
                if piece == 5:
                    pe.wait_ge(ev["rk"], at("rk", c))
                    pe.wait_ge(ev["kk_unit"], at("kk_unit", c))
                    for k in range(KR):
                        m = mm(psum[:, 6, 2 * k:2 * k + 2], rkT[:, k, :], rk_heads[:, k, :])
                    m.then_inc(ev["bonus_raw"], 1)

            def pe_turn_y(c):
                pe.wait_ge(ev["y_fin"], at("y_fin", c))
                for k in range(KR):
                    m = pe.transpose(psum[:, 7, k * P:(k + 1) * P], yc[:, k * P:(k + 1) * P], ident[:])
                m.then_inc(ev["y_turned"], 1)

            def pe_turn_x(c, n):
                g = n % 2
                for h in range(4):
                    m = pe.transpose(psum[:, 2 * g, h * P:(h + 1) * P], xq[:, 4 * g + h, 0, :], ident[:])
                m.then_inc(ev["xt"], 1)

            def pe_rest(c, par, first, last):
                pr = prT[par]
                pe.wait_ge(ev["pr_ready"], at("pr_ready", c))
                pe.wait_ge(ev["b_ready"], at("b_ready", c))
                pe.wait_ge(ev["k_ready"], at("k_ready", c))
                pe.wait_ge(ev["s_sum"], at("s_sum", c - 1))
                pe.wait_ge(ev["yc"], at("yc", c - 1))
                for n, src in enumerate((lambda k: pr[:, k, 0, :], lambda k: bT[:, k, :],
                                         lambda k: kT[:, k, :], lambda k: zs[:, 2 * KR + k, :])):
                    for k in range(KR):
                        m = pe.transpose(psum[:, n, k * P:(k + 1) * P], src(k), ident[:])
                    m.then_inc(ev["nat_turned"], 1)
                pe.wait_ge(ev["exps"], at("exps", c))
                pe.wait_ge(ev["bonus"], at("bonus", c))
                pe.wait_ge(ev["mixed_b"], at("mixed_b", c))
                for q in range(4):
                    for e in range(2):
                        h = head_at(2 * q + e)
                        m = mm(psum[:, 4 + q, e * 2 * C:(e + 1) * 2 * C], bT[rows(h), h // 2, :],
                               pr[rows(h), h // 2, :, :].rearrange("p a c -> p (a c)"))
                    m.then_inc(ev["gram"], 1)
                pe.wait_ge(ev["nat_act"], at("nat_act", c, 1))
                for q in range(2):
                    if q == 1:
                        pe.wait_ge(ev["nat_dve"], at("nat_dve", c, 1))
                    for e in range(4):
                        h = head_at(4 * q + e)
                        m = mm(psum[:, q, e * P:(e + 1) * P], pr[rows(h), h // 2, 0, :], bT[rows(h), h // 2, :])
                    m.then_inc(ev["gram"], 1)
                pe.wait_ge(ev["nat_act"], at("nat_act", c))
                pe.wait_ge(ev["nat_dve"], at("nat_dve", c))
                for q in range(4):
                    bank = 2 + q
                    if q >= 2:
                        pe.wait_ge(ev["gram_used"], at("gram_used", c, q - 1))
                    for e in range(2):
                        h = head_at(2 * q + e)
                        m = mm(psum[:, bank, e * 2 * C:(e + 1) * 2 * C], kT[rows(h), h // 2, :],
                               pr[rows(h), h // 2, :, :].rearrange("p a c -> p (a c)"))
                    m.then_inc(ev["gram"], 1)
                for g in range(2):
                    pe.wait_ge(ev["x_init"], at("x_init", c, g + 1))
                    pe.wait_ge(ev["gram_used"], at("gram_used", c, 5 if g == 0 else 7))
                    pe_turn_x(c, g)
                for lev in range(LEVELS):
                    for g in range(2):
                        n = 2 * lev + g
                        pe.wait_ge(ev["xt_copied"], at("xt_copied", c, n + 1))
                        if lev == 0:
                            pe.wait_ge(ev["gram_used"], at("gram_used", c, 6))
                        for e in range(4):
                            h = 4 * g + e
                            m = mm(psum[:, 2 * g, e * P:(e + 1) * P], nT[:, h, :], xq[:, h, 0, :])
                        m.then_inc(ev["y"], 1)
                    for g in range(2):
                        n = 2 * lev + g
                        pe.wait_ge(ev["y_copied"], at("y_copied", c, n + 1))
                        if lev == 0:
                            pe.wait_ge(ev["gram_used"], at("gram_used", c, 8))
                        for e in range(4):
                            h = 4 * g + e
                            m = mm(psum[:, 2 * g + 1, e * P:(e + 1) * P], xT[:, h, :], yb[:, h, :])
                        m.then_inc(ev["delta"], 1)
                    if lev == 1 and not first:
                        pe.wait_ge(ev["mixed_b"], at("mixed_b", c))
                        pe_turn_y(c - 1)
                    if not last:
                        pe_front(lev, c + 1, 1 - par)
                    for g in range(2):
                        n = 2 * lev + g
                        pe.wait_ge(ev["x_upd"], at("x_upd", c, n + 1))
                        if lev < LEVELS - 1:
                            pe_turn_x(c, n)
                for slot in range(G):
                    h = head_at(slot)
                    m = mm(psum[rows(h), 0, (h // 2) * P:(h // 2 + 1) * P], p_nat[:, cols(h)], xq[:, slot, 0, :])
                m.then_inc(ev["tp"], 1)
                pe.wait_ge(ev["gram_used"], at("gram_used", c))
                for slot in range(G):
                    h = head_at(slot)
                    m = mm(psum[:, 1, cols(h)], mq[:, slot, 0, :], v_nat[:, cols(h)])
                m.then_inc(ev["gmk"], 1)
                pe.wait_ge(ev["gmk_copied"], at("gmk_copied", c))
                pe.wait_ge(ev["tp_copied"], at("tp_copied", c))
                pe.wait_ge(ev["state"], at("state", c - 1))
                for slot in range(G):
                    h = head_at(slot)
                    o = psum[:, 2 + h % 2, cols(h // 2)]
                    mm(o, xq[:, slot, 0, :], gv[:, cols(h)], True, False)
                    m = mm(o, tpT[rows(h), h // 2, :], state[rows(h), h // 2, :], False, True)
                m.then_inc(ev["u"], 1)
                pe.wait_ge(ev["u_copied"], at("u_copied", c))
                for h in range(G):
                    o = psum[rows(h), 2, (h // 2) * HD:(h // 2 + 1) * HD]
                    mm(o, b_nat[:, cols(h)], u_nat[:, cols(h)], True, False)
                    m = mm(o, k_nat[:, cols(h)], v_nat[:, cols(h)], False, True)
                m.then_inc(ev["s_new"], 1)
                for slot in range(G):
                    h = head_at(slot)
                    o = psum[:, h % 2, cols(h // 2)]
                    mm(o, pr[rows(h), h // 2, 1, :], state[rows(h), h // 2, :], True, False)
                    mm(o, xq[:, slot, 1, :], u_nat[:, cols(h)], False, False)
                    m = mm(o, mq[:, slot, 1, :], v_nat[:, cols(h)], False, True)
                m.then_inc(ev["y_raw"], 1)

            def pe_mix():
                pe.wait_ge(mix_made, 5)
                for piece in range(6):
                    pe_front(piece, 0, 0)
                pe_rest(0, 0, True, False)
                with pe.Fori(0, CHUNKS // 2 - 1) as i:
                    for b in range(2):
                        pe_rest(i * 2 + (1 + b), 1 - b, False, False)
                pe_rest(CHUNKS - 1, 1, False, True)
                pe_turn_y(CHUNKS - 1)

            turn_x()
            pe.wait_ge(x_used_dve, TT)
            pe.wait_ge(x_used_act, TT)
            norm_sums("ffn1")
            ffn_products("ffn1", stages["ffn1"])
            if FULL:
                norm_sums("mix")
                w_in_products(stages["w_in"])
                turn_spatial()
                pe_mix()
                w_out_products(stages["w_out"])
                pe.wait_ge(w_out_added, 4 + 2 * KD)
            norm_sums("ffn2")
            ffn_products("ffn2", stages["ffn2"])
            turn_p()
            norm_sums("ple")
            gate_products(stages["gate"])
            norm_sums("final")
            turn_result()

        @block.scalar
        def _(act):
            def half(h):
                return slice(h * NB, (h + 1) * NB)

            def load_x():
                for c in range(TT // 2):
                    act.dma_start(xs[:, 2 * c:2 * c + 2, :],
                                  x[0, 2 * c * P:(2 * c + 2) * P, :].rearrange("(t q) c -> q t c", q=P)
                                  ).then_inc(x_ready[c], 16)
                for name, row in VECTORS.items():
                    v = io[name]
                    v = (v.rearrange("(k p) -> k p", p=P) if len(v.shape) == 1 else
                         v.rearrange("o (k p) -> (o k) p", p=P) if len(v.shape) == 2 else
                         v.rearrange("o (k a) c -> (o k) (a c)", a=2))
                    act.dma_start(vec_rows[row:row + v.shape[0], :], v).then_inc(const_ready, 16)
                for t in range(TT):
                    act.wait_ge(x_turned, 2 * t + 2)
                    act.activation(hT[:, 4:8, t * P:(t + 1) * P],
                                   psum[:, 2 * (t % 2) + 1, :].rearrange("p (k c) -> p k c", c=P),
                                   ACT.Copy).then_inc(x_used_act, 1)

            def squares(name, h, ready):
                for k in range(KD):
                    ready(h, k)
                    n = h * KD + k
                    if n >= 4:
                        act.wait_ge(norm["sq_used"], in_norm(name, "sq_used", n - 3))
                    act.activation(sq[:, k % 4, :], hT[:, k, half(h)], ACT.Square).then_inc(norm["squared"], 1)

            def root(name, h):
                act.wait_ge(norm["summed"], in_norm(name, "summed", h + 1))
                act.activation(rms[:, h * 4:h * 4 + 4], rms[:, h * 4:h * 4 + 4], ACT.Sqrt,
                               scale=1.0 / D, bias=rms_eps[:]).then_inc(norm["rooted"], 1)

            def highs(name, h):
                for k in range(KD):
                    act.wait_ge(norm["scaled"], in_norm(name, "scaled", h * KD + k + 1))
                    act.activation(aH[:, k, half(h)], nrm[:, k % 2, :], ACT.Copy).then_inc(norm["high"], 1)

            def norm_part(name, ready, split=True):
                for h in range(HALVES):
                    squares(name, h, ready)
                    root(name, h)
                    if split:
                        highs(name, h)

            def hidden(name, st):
                s = ffn[name]
                with act.Fori(0, st.iters) as i:
                    for f in range(2):
                        for h in range(HALVES):
                            n = 2 * f + h
                            act.wait_ge(s["up"], i * 4 + (n + 1))
                            act.activation(silu[:, h, :], psum[:, 2 * h, :], ACT.Silu).then_inc(s["silued"], 1)
                            if h == 1:
                                act.sem_inc(w_free, 2)
                            act.wait_ge(s["product"], i * 4 + (n + 3))
                            act.activation(hidH[:, f, half(h)], hid[:, h, :], ACT.Copy).then_inc(s["high"], 1)

            def after_adds(name, st):
                base = (st.iters - 1) * 2 * KD + 4
                return lambda h, k: act.wait_ge(ffn[name]["added"], base + h * KD + k + 1)

            def split_p():
                for t in range(TT):
                    act.wait_ge(pT["turned"], t + 1)
                    act.activation(pTH[:, :, t * P:(t + 1) * P],
                                   psum[:, t % 2, 0:PLE].rearrange("p (k c) -> p k c", c=P),
                                   ACT.Copy).then_inc(pT["high"], 1)

            def gate_sigmoid(st):
                with act.Fori(0, st.iters) as i:
                    for j in range(2):
                        for h in range(HALVES):
                            act.wait_ge(gate["done"], i * 4 + (2 * j + h + 1))
                            act.activation(silu[:, h, :], psum[:, 2 * h, :], ACT.Sigmoid).then_inc(gate["sigmoid"], 1)
                            if h == 1:
                                act.sem_inc(w_free, 1)

            def copy_result():
                for t in range(TT):
                    act.wait_ge(fin["turned"], 2 * t + 2)
                    if t >= 2:
                        act.wait_ge(fin[f"stored{t % 2}"], 16 * (t // 2))
                    act.activation(outs[:, t % 2, NB:D], psum[:, 4 + (2 * t + 1) % 4, :],
                                   ACT.Copy).then_inc(fin["copied_act"], 1)
                    act.wait_ge(fin["copied_act"], t + 1)
                    act.wait_ge(fin["copied_dve"], t + 1)
                    act.dma_start(out[0, t * P:(t + 1) * P, :],
                                  outs[:, t % 2, :]).then_inc(fin[f"stored{t % 2}"], 16)
                for j in range(2):
                    act.wait_ge(fin[f"stored{j}"], 16 * (TT // 2))

            def load_mix_consts():
                act.wait_ge(ffn["ffn1"]["added"], 4 + stages["ffn1"].iters * 2 * KD)
                loads = [(shape_masks[:], io["masks"]),
                         (w_lora[0:64, :], io["rwkv_w_decay"][0]), (w_lora[64:128, :], io["rwkv_w_aaa"][0]),
                         (w_gate[:], io["rwkv_w_gate"][0]),
                         (ws_rows[:], io["sgu_w_s"][0].rearrange("h t s -> t h s"))]
                for dst, name in ((w0_rows, "rwkv_w0"), (gn_g, "rwkv_gn_g"), (gn_b, "rwkv_gn_b"),
                                  (ln_g, "sgu_ln_g"), (ln_b, "sgu_ln_b")):
                    loads.append((dst[:], io[name][0:1, :].to_broadcast([P, NB])))
                for e in range(2):
                    loads.append((b_s[64 * e:64 * e + 64, :, :],
                                  io["sgu_b_s"].rearrange("o (k a) t -> a o k t", a=2)[e]
                                  .to_broadcast([64, KR, P])))
                assert len(loads) == MIX_CONSTS
                for dst, src in loads:
                    act.dma_start(dst, src).then_inc(mix_consts, 16)

            def store_z(st):
                for j in range(2):
                    act.sem_inc(z_stored[j], 16)
                act.wait_ge(mix_made, 2)
                with act.Fori(0, st.iters) as i:
                    for j in range(2):
                        act.wait_ge(z_stored[j], i * 16 + 16)
                        for h in range(HALVES):
                            n = 2 * j + h
                            act.wait_ge(win["done"], i * 4 + (n + 1))
                            if h == 1:
                                act.sem_inc(w_free, 1)
                            act.activation(zout[:, j, 1 + h * NB:1 + (h + 1) * NB], psum[:, n, :],
                                           ACT.Copy).then_inc(win["copied"], 1)
                        act.wait_ge(win["copied"], i * 4 + (4 + 2 * j + 2))
                        act.dma_start(z_scratch[bass.ds(i * 2 * P + j * P, P), :],
                                      zout[:, j, :]).then_inc(z_stored[j], 16)

            def act_front(piece, c, par):
                if piece == 0:
                    act.wait_ge(ev["shifted"], at("shifted", c, 3))
                    act.activation(tanh_w[0:64, :], zs[0:64, LORA, :], ACT.Tanh).then_inc(ev["lora_in"], 1)
                    act.activation(sig_g[:], zs[:, GATE, :], ACT.Sigmoid).then_inc(ev["lora_in"], 1)
                    act.wait_ge(ev["a_raw"], at("a_raw", c))
                    a0 = VECTORS["rwkv_a0"]
                    act.wait_ge(ev["kp"], at("kp", c - 1))
                    act.wait_ge(ev["kk_a"], at("kk_a", c - 1))
                    for k in range(KR):
                        m = act.activation(aT[:, k, :], psum[:, 5, k * P:(k + 1) * P], ACT.Sigmoid,
                                           bias=vecs[:, a0 + k:a0 + k + 1])
                    m.then_inc(ev["a_ready"], 1)
                    act.wait_ge(ev["w_biased"], at("w_biased", c))
                    act.activation(sig_w[:], sig_w[:], ACT.Sigmoid).then_inc(ev["w_sig"], 1)
                    act.wait_ge(ev["g_raw"], at("g_raw", c))
                    act.activation(g_nat[par][:], psum[:, 6, :], ACT.Copy).then_inc(ev["g_ready"], 1)
                    act.wait_ge(ev["g_loaded"], at("g_loaded", c))
                    act.activation(gc[:], gc[:], ACT.Gelu).then_inc(ev["gelu"], 1)
                if piece == 2:
                    act.wait_ge(ev["decays"], at("decays", c))
                    act.wait_ge(ev["pr_ready"], at("pr_ready", c - 1))
                    act.wait_ge(ev["b_ready"], at("b_ready", c - 1))
                    act.wait_ge(ev["k_ready"], at("k_ready", c - 1))
                    sums = psum[:, 4:6, :].rearrange("p b (k w t) -> p b k w t", w=2, t=C)
                    incl, excl = sums[:, :, :, 0, :], sums[:, :, :, 1, :]

                    def tiles(x):
                        return x.rearrange("p (b k) c -> p b k c", k=2)
                    act.activation(tiles(e_in[:]), incl, ACT.Exp).then_inc(ev["exps"], 1)
                    act.activation(tiles(e_ex[:]), excl, ACT.Exp).then_inc(ev["exps"], 1)
                    act.activation(tiles(e_neg[:]), incl, ACT.Exp, scale=-1.0).then_inc(ev["exps"], 1)
                    act.activation(e_mid[:, par, :].rearrange("p (b k) -> p b k", k=2),
                                   excl[:, :, :, 0], ACT.Exp, scale=-1.0).then_inc(ev["exps"], 1)
                    act.activation(e_end[:, par, :].rearrange("p (b k) -> p b k", k=2),
                                   incl[:, :, :, C - 1], ACT.Exp).then_inc(ev["exps"], 1)

            def by_parity(x):
                return x.rearrange("p (k e d) -> p e k d", e=2, d=HD)

            def parities(bank):
                return psum[:, bank:bank + 2, 0:NB // 2].rearrange("p e (k d) -> p e k d", d=HD)

            def act_place_y(c):
                act.wait_ge(ev["y_turned"], at("y_turned", c))
                act.activation(y_out[:, 0:KR, bass.ds(c * C, C)],
                               psum[:, 7, :].rearrange("p (k c) -> p k c", c=P),
                               ACT.Copy).then_inc(ev["y_placed"], 1)

            def act_copy_xt(c, n):
                g = n % 2
                act.wait_ge(ev["xt"], at("xt", c, n + 1))
                act.activation(xT[:, 4 * g:4 * g + 4, :], psum[:, 2 * g, :].rearrange("p (h c) -> p h c", c=P),
                               ACT.Copy).then_inc(ev["xt_copied"], 1)

            def act_rest(c, par, first, last):
                for n, (bank, dst) in enumerate(((0, p_nat), (2, k_nat))):
                    act.wait_ge(ev["nat_turned"], at("nat_turned", c, bank + 1))
                    act.activation(dst[:], psum[:, bank, :], ACT.Copy).then_inc(ev["nat_act"], 1)
                for g in range(2):
                    act_copy_xt(c, g)
                for lev in range(LEVELS):
                    for g in range(2):
                        n = 2 * lev + g
                        act.wait_ge(ev["y"], at("y", c, n + 1))
                        act.activation(yb[:, 4 * g:4 * g + 4, :],
                                       psum[:, 2 * g, :].rearrange("p (h c) -> p h c", c=P),
                                       ACT.Copy).then_inc(ev["y_copied"], 1)
                    if lev == 1 and not first:
                        act_place_y(c - 1)
                    if not last:
                        act_front(lev, c + 1, 1 - par)
                    if lev < LEVELS - 1:
                        for g in range(2):
                            act_copy_xt(c, 2 * lev + 2 + g)
                act.wait_ge(ev["tp"], at("tp", c))
                act.activation(tpT[:], psum[:, 0, :].rearrange("p (k c) -> p k c", c=P),
                               ACT.Copy).then_inc(ev["tp_copied"], 1)
                act.wait_ge(ev["u"], at("u", c))
                act.activation(by_parity(u_nat[:]), parities(2), ACT.Copy).then_inc(ev["u_copied"], 1)
                act.wait_ge(ev["yc"], at("yc", c))
                act.activation(ysq[:], yc[:], ACT.Square).then_inc(ev["ysq"], 1)

            def act_mix():
                for piece in range(6):
                    act_front(piece, 0, 0)
                act_rest(0, 0, True, False)
                with act.Fori(0, CHUNKS // 2 - 1) as i:
                    for b in range(2):
                        act_rest(i * 2 + (1 + b), 1 - b, False, False)
                act_rest(CHUNKS - 1, 1, False, True)
                act_place_y(CHUNKS - 1)
                for h in range(HALVES):
                    for k in range(KD):
                        if h == 0 and k == 0:
                            act.wait_ge(ev["y_placed"], at("y_placed", CHUNKS - 1))
                            act.wait_ge(ev["sgu"], at("sgu", CHUNKS - 1))
                            act.wait_ge(ev["y_turned"], at("y_turned", CHUNKS - 1))
                            act.wait_ge(ev["y_fin"], at("y_fin", CHUNKS - 1))
                        act.activation(aH[:, k, half(h)], y_out[:, k, half(h)], ACT.Copy).then_inc(y_high, 1)

            load_x()
            act.wait_ge(made, 5)

            def x_there(h, k):
                if k == 0:
                    act.wait_ge(x_used_dve, (h + 1) * (TT // 2))
                    act.wait_ge(x_used_act, (h + 1) * (TT // 2))
            norm_part("ffn1", x_there)
            hidden("ffn1", stages["ffn1"])
            if FULL:
                norm_part("mix", after_adds("ffn1", stages["ffn1"]))
                load_mix_consts()
                store_z(stages["w_in"])
                act_mix()
                norm_part("ffn2", lambda h, k: act.wait_ge(w_out_added, 4 + 2 * k + h + 1))
            else:
                norm_part("ffn2", after_adds("ffn1", stages["ffn1"]))
            hidden("ffn2", stages["ffn2"])
            act.wait_ge(ffn["ffn2"]["down"], stages["ffn2"].iters * 2 * KD)
            act.dma_start(p_rows[:], p[0, 0].rearrange("(t q) c -> q t c", q=P)).then_inc(pT["loaded"], 16)
            split_p()
            act.wait_ge(pT["ready"], TT)
            norm_part("ple", after_adds("ffn2", stages["ffn2"]))
            gate_sigmoid(stages["gate"])
            norm_part("final", lambda h, k: act.wait_ge(
                gate["added"], 2 + 2 * k + h + 1), split=False)
            copy_result()

        @block.vector
        def _(dve):
            def half(h):
                return slice(h * NB, (h + 1) * NB)

            def place_x():
                for t in range(TT):
                    dve.wait_ge(x_turned, 2 * t + 1)
                    dve.tensor_copy(hT[:, 0:4, t * P:(t + 1) * P],
                                    psum[:, 2 * (t % 2), :].rearrange("p (k c) -> p k c", c=P)
                                    ).then_inc(x_used_dve, 1)

            def norm_part(name, gain, split=True):
                per = NB // P
                for h in range(HALVES):
                    bank = 3 * h
                    dve.wait_ge(norm["sq_used"], in_norm(name, "sq_used", (h + 1) * KD))
                    dve.tensor_reduce(rms[:, h * per:(h + 1) * per],
                                      psum[:, bank, 0:KD * per].rearrange("p (k t) -> p t k", t=per),
                                      AX_X, ALU.add).then_inc(norm["summed"], 1)
                    dve.wait_ge(norm["rooted"], in_norm(name, "rooted", h + 1))
                    dve.reciprocal(rstd[:, h * per:(h + 1) * per],
                                   rms[:, h * per:(h + 1) * per]).then_inc(norm["inverted"], 1)
                    dve.wait_ge(norm["spread"], in_norm(name, "spread", h + 1))

                    def low(k):
                        dve.wait_ge(norm["high"], in_norm(name, "high", h * KD + k + 1))
                        dve.tensor_tensor(aL[:, k, half(h)], nrm[:, k % 2, :],
                                          aH[:, k, half(h)].bitcast(F32), ALU.subtract).then_inc(norm["ready"], 1)
                    for k in range(KD):
                        dst = nrm[:, k % 2, :] if split else hT[:, k, half(h)]
                        if split and h * KD + k >= 2:
                            dve.wait_ge(norm["ready"], in_norm(name, "ready", h * KD + k - 1))
                        dve.scalar_tensor_tensor(out=dst, in0=hT[:, k, half(h)], scalar=vecs[:, gain + k:gain + k + 1],
                                                 in1=psum[:, bank, :], op0=ALU.mult, op1=ALU.mult
                                                 ).then_inc(norm["scaled" if split else "ready"], 1)
                        if split and k >= 1:
                            low(k - 1)
                    if split:
                        low(KD - 1)

            def hidden_and_adds(name, st):
                s = ffn[name]
                with dve.Fori(0, st.iters) as i:
                    for f in range(2):
                        for h in range(HALVES):
                            n = 2 * f + h
                            dve.wait_ge(s["silued"], i * 4 + (n + 1))
                            dve.tensor_tensor(hid[:, h, :], silu[:, h, :], psum[:, 2 * h + 1, :],
                                              ALU.mult).then_inc(s["product"], 1)
                            dve.wait_ge(s["high"], i * 4 + (n + 1))
                            dve.tensor_tensor(hidL[:, f, half(h)], hid[:, h, :],
                                              hidH[:, f, half(h)].bitcast(F32),
                                              ALU.subtract).then_inc(s["hid_ready"], 1)
                    for h in range(HALVES):
                        for d in range(KD):
                            n = h * KD + d
                            dve.wait_ge(s["down"], i * (2 * KD) + (n + 1))
                            if n == 2 * KD - 1:
                                dve.sem_inc(w_free, 2)
                            dve.wait_ge(s["added"], i * (2 * KD) + (n + 1))
                            dve.scalar_tensor_tensor(out=hT[:, d, half(h)], in0=psum[:, 4 + n % 4, :],
                                                     scalar=0.5, in1=hT[:, d, half(h)],
                                                     op0=ALU.mult, op1=ALU.add).then_inc(s["added"], 1)

            def split_p():
                for t in range(TT):
                    dve.wait_ge(pT["high"], t + 1)
                    dve.tensor_tensor(pTL[:, :, t * P:(t + 1) * P],
                                      psum[:, t % 2, 0:PLE].rearrange("p (k c) -> p k c", c=P),
                                      pTH[:, :, t * P:(t + 1) * P].bitcast(F32), ALU.subtract).then_inc(pT["ready"], 1)

            def gate_adds(st):
                with dve.Fori(0, st.iters) as i:
                    for j in range(2):
                        for h in range(HALVES):
                            n = 2 * j + h
                            dve.wait_ge(gate["sigmoid"], i * 4 + (n + 1))
                            dve.tensor_tensor(gated[:, h, :], silu[:, h, :], psum[:, 2 * h + 1, :],
                                              ALU.mult).then_inc(gate["product"], 1)
                            dve.wait_ge(gate["product"], i * 4 + (n + 1))
                            hk = hT[:, bass.ds(i * 2 + j, 1), half(h)].rearrange("p a c -> p (a c)")
                            dve.tensor_tensor(hk, hk, gated[:, h, :], ALU.add).then_inc(gate["added"], 1)

            def copy_result():
                for t in range(TT):
                    dve.wait_ge(fin["turned"], 2 * t + 1)
                    if t >= 2:
                        dve.wait_ge(fin[f"stored{t % 2}"], 16 * (t // 2))
                    dve.tensor_copy(outs[:, t % 2, 0:NB],
                                    psum[:, 4 + (2 * t) % 4, :]).then_inc(fin["copied_dve"], 1)

            def place_spatial():
                for g in range(2):
                    dve.wait_ge(ws_turned, g + 1)
                    dve.tensor_tensor(wsT[:, 4 * g:4 * g + 4, :],
                                      psum[:, 4 + g, :].rearrange("p (h c) -> p h c", c=P),
                                      strict_incl[:, C:2 * C].unsqueeze(1).to_broadcast([P, 4, C]),
                                      ALU.mult).then_inc(ws_placed, 1)

            def dve_front(piece, c, par):
                kz, rz = zs[:, KR:2 * KR, :], zs[:, 0:KR, :]
                bank7 = psum[:, 7, :].rearrange("p (k c) -> p k c", c=P)
                if piece == 0:
                    dve.wait_ge(ev["w_raw"], at("w_raw", c))
                    dve.wait_ge(ev["decays"], at("decays", c - 1))
                    dve.tensor_tensor(sig_w[:], psum[:, 4, :], w0_rows[:], ALU.add).then_inc(ev["w_biased"], 1)
                if piece == 1:
                    dve.wait_ge(ev["v_turned"], at("v_turned", c))
                    dve.bn_stats(v_stats[:], psum[:, 7, :]).then_inc(ev["v_stats"], 1)
                    dve.wait_ge(mix_consts, 16 * MIX_CONSTS)
                    dve.wait_ge(ev["v_stats"], at("v_stats", c))
                    dve.bn_aggr(v_mv[:], v_stats[:]).then_inc(ev["v_mv"], 1)
                    dve.wait_ge(ev["v_mv"], at("v_mv", c))
                    dve.tensor_scalar(v_mv[:, 1:2], v_mv[:, 1:2], 1e-5, None, ALU.add).then_inc(ev["v_ve"], 1)
                if piece == 2:
                    dve.wait_ge(ev["kk_sums"], at("kk_sums", c))
                    dve.tensor_scalar(kk_rn[:], psum[:, 6, 0:G], 1e-24, None, ALU.max).then_inc(ev["kk_clamped"], 1)
                    dve.wait_ge(ev["v_rs"], at("v_rs", c))
                    dve.tensor_scalar(vn[:], psum[:, 7, :], v_mv[:, 0:1], v_rs[:], ALU.subtract,
                                      ALU.mult).then_inc(ev["v_norm"], 1)
                if piece == 3:
                    dve.wait_ge(ev["kk_spread"], at("kk_spread", c))
                    dve.tensor_tensor(kkT[:], kkT[:], psum[:, 6, :].rearrange("p (k c) -> p k c", c=P),
                                      ALU.mult).then_inc(ev["kk_unit"], 1)
                    dve.wait_ge(ev["exps"], at("exps", c, 3))
                    dve.tensor_tensor(prT[par][:, :, 1, :], rz, e_in[:], ALU.mult).then_inc(ev["pr_ready"], 1)
                    dve.wait_ge(ev["kk_unit"], at("kk_unit", c))
                    dve.tensor_tensor(prT[par][:, :, 0, :], kkT[:], e_ex[:], ALU.mult).then_inc(ev["pr_ready"], 1)
                    dve.tensor_tensor(tmpT[:], kkT[:], aT[:], ALU.mult).then_inc(ev["kk_a"], 1)
                if piece == 4:
                    dve.wait_ge(ev["kk_a"], at("kk_a", c))
                    dve.wait_ge(ev["gram"], at("gram", c - 1))
                    dve.scalar_tensor_tensor(out=bT[:], in0=tmpT[:], scalar=-1.0, in1=e_neg[:],
                                             op0=ALU.mult, op1=ALU.mult).then_inc(ev["b_ready"], 1)
                    dve.wait_ge(ev["kp"], at("kp", c))
                    dve.tensor_tensor(kT[:], kpT[:], e_neg[:], ALU.mult).then_inc(ev["k_ready"], 1)
                    dve.wait_ge(ev["mixed"], at("mixed", c))
                    dve.tensor_tensor(mixed[:], bank7, b_s[:], ALU.add).then_inc(ev["mixed_b"], 1)
                    dve.wait_ge(ev["mixed_b"], at("mixed_b", c))
                    dve.tensor_tensor(y_out[:, KR:2 * KR, bass.ds(c * C, C)], mixed[:], gc[:, 0:KR, :],
                                      ALU.mult).then_inc(ev["sgu"], 1)
                if piece == 5:
                    dve.wait_ge(ev["bonus_raw"], at("bonus_raw", c))
                    dve.tensor_copy(bonus[:, par, :], psum[:, 6, 0:G]).then_inc(ev["bonus"], 1)

            def dve_rest(c, par, first, last):
                for n, (bank, dst) in enumerate(((1, b_nat), (3, v_nat))):
                    dve.wait_ge(ev["nat_turned"], at("nat_turned", c, bank + 1))
                    if n == 1:
                        dve.wait_ge(ev["bv"], at("bv", c - 1))
                    dve.tensor_copy(dst[:], psum[:, bank, :]).then_inc(ev["nat_dve"], 1)
                k = 0
                for q in range(4):
                    k += 1
                    dve.wait_ge(ev["gram"], at("gram", c, k))
                    dve.tensor_tensor(xq[:, 2 * q:2 * q + 2, :, :].rearrange("p h a c -> p h (a c)"),
                                      psum[:, 4 + q, :].rearrange("p (h c) -> p h c", h=2),
                                      band_incl.unsqueeze(1).to_broadcast([P, 2, 2 * C]),
                                      ALU.mult).then_inc(ev["gram_used"], 1)
                for q in range(2):
                    k += 1
                    dve.wait_ge(ev["gram"], at("gram", c, k))
                    dve.tensor_tensor(nT[:, 4 * q:4 * q + 4, :], psum[:, q, :].rearrange("p (h c) -> p h c", c=P),
                                      lower.unsqueeze(1).to_broadcast([P, 4, C]),
                                      ALU.mult).then_inc(ev["gram_used"], 1)
                for q in range(4):
                    k += 1
                    dve.wait_ge(ev["gram"], at("gram", c, k))
                    dve.tensor_tensor(mq[:, 2 * q:2 * q + 2, :, :].rearrange("p h a c -> p h (a c)"),
                                      psum[:, 2 + q, :].rearrange("p (h c) -> p h c", h=2),
                                      strict_incl.unsqueeze(1).to_broadcast([P, 2, 2 * C]),
                                      ALU.mult).then_inc(ev["gram_used"], 1)
                for lev in range(LEVELS):
                    for g in range(2):
                        n = 2 * lev + g
                        dve.wait_ge(ev["delta"], at("delta", c, n + 1))
                        dve.sem_inc(delta_seen, 1)
                        dve.copy_predicated(xq[:, 4 * g:4 * g + 4, 0, :],
                                            merge_masks[:, lev, :].unsqueeze(1).to_broadcast([P, 4, C]),
                                            psum[:, 2 * g + 1, :].rearrange("p (h c) -> p h c", c=P)
                                            ).then_inc(ev["x_upd"], 1)
                    if not last:
                        dve_front(lev, c + 1, 1 - par)
                dve.wait_ge(ev["gmk"], at("gmk", c))
                dve.tensor_copy(gv[:], psum[:, 1, :]).then_inc(ev["gmk_copied"], 1)
                if not last:
                    dve.wait_ge(ev["exps"], at("exps", c + 1))
                    dve.tensor_tensor(carry[:], e_end[:, par, :], e_mid[:, 1 - par, :],
                                      ALU.mult).then_inc(ev["carry"], 1)
                dve.wait_ge(ev["s_new"], at("s_new", c))
                dve.tensor_tensor(state_sum[:], state[:], psum[:, 2, 0:KR * HD].rearrange("p (k d) -> p k d", d=HD),
                                  ALU.add).then_inc(ev["s_sum"], 1)
                dve.wait_ge(ev["y_raw"], at("y_raw", c))
                if not last:
                    dve.wait_ge(ev["s_sum"], at("s_sum", c))
                    dve.wait_ge(ev["carry"], at("carry", c))
                    dve.tensor_tensor(state[:], state_sum[:], carry[:].unsqueeze(2).to_broadcast([P, KR, HD]),
                                      ALU.mult).then_inc(ev["state"], 1)
                y4 = psum[:, 0:2, 0:NB // 2].rearrange("p e (k d) -> p e k d", d=HD)
                dve.tensor_reduce(mean[:].rearrange("p (e k) -> p e k", e=2), y4, AX_X,
                                  ALU.add).then_inc(ev["mean"], 1)
                dve.wait_ge(ev["mean"], at("mean", c, 1))
                dve.tensor_scalar(mean[:], mean[:], 1.0 / HD, None, ALU.mult).then_inc(ev["mean"], 1)
                dve.wait_ge(ev["mean"], at("mean", c))
                if not first:
                    dve.wait_ge(ev["y_turned"], at("y_turned", c - 1))
                for e in range(2):
                    m = dve.tensor_tensor(yc[:].rearrange("p (k e d) -> p e k d", e=2, d=HD)[:, e],
                                          psum[:, e, 0:NB // 2].rearrange("p (k d) -> p k d", d=HD),
                                          mean[:, e * KR:(e + 1) * KR].unsqueeze(2).to_broadcast([P, KR, HD]),
                                          ALU.subtract)
                m.then_inc(ev["yc"], 1)
                dve.wait_ge(ev["ysq"], at("ysq", c))
                dve.tensor_reduce(var[:], ysq[:].rearrange("p (h d) -> p h d", d=HD), AX_X, ALU.add
                                  ).then_inc(ev["var"], 1)
                dve.wait_ge(ev["var"], at("var", c, 1))
                dve.tensor_scalar(var[:], var[:], 1.0 / HD, 64e-5, ALU.mult, ALU.add).then_inc(ev["var"], 1)

            def dve_mix():
                for piece in range(6):
                    dve_front(piece, 0, 0)
                dve.wait_ge(mix_made, 5)
                dve_rest(0, 0, True, False)
                with dve.Fori(0, CHUNKS // 2 - 1) as i:
                    for b in range(2):
                        dve_rest(i * 2 + (1 + b), 1 - b, False, False)
                dve_rest(CHUNKS - 1, 1, False, True)
                for h in range(HALVES):
                    for k in range(KD):
                        dve.wait_ge(y_high, h * KD + k + 1)
                        dve.tensor_tensor(aL[:, k, half(h)], y_out[:, k, half(h)],
                                          aH[:, k, half(h)].bitcast(F32), ALU.subtract).then_inc(y_split, 1)

            def add_w_out(st):
                with dve.Fori(0, st.iters) as i:
                    for j in range(2):
                        for h in range(HALVES):
                            n = 2 * j + h
                            dve.wait_ge(w_out_done, i * 4 + (n + 1))
                            if h == 1:
                                dve.sem_inc(w_free, 1)
                            hk = hT[:, bass.ds(i * 2 + j, 1), half(h)].rearrange("p a c -> p (a c)")
                            dve.tensor_tensor(hk, hk, psum[:, n, :], ALU.add).then_inc(w_out_added, 1)

            place_x()
            dve.wait_ge(vecs_turned, 1)
            dve.tensor_copy(vecs[:], psum[:, 4, 0:n_rows]).then_inc(vecs_ready, 1)
            dve.wait_ge(vecs_ready, 1)
            norm_part("ffn1", VECTORS["norm_ffn1"])
            hidden_and_adds("ffn1", stages["ffn1"])
            if FULL:
                norm_part("mix", VECTORS["norm_mix"])
                place_spatial()
                dve_mix()
                add_w_out(stages["w_out"])
            norm_part("ffn2", VECTORS["norm_ffn2"])
            hidden_and_adds("ffn2", stages["ffn2"])
            split_p()
            norm_part("ple", VECTORS["norm_ple"])
            gate_adds(stages["gate"])
            norm_part("final", VECTORS["norm_final"], split=False)
            copy_result()


_INS = ['x', 'p', 'norm_ffn1', 'ffn1_w1', 'ffn1_w3', 'ffn1_w2', 'norm_mix', 'w_in', 'shift_mu',
        'rwkv_w0', 'rwkv_w_decay', 'rwkv_a0', 'rwkv_w_aaa', 'rwkv_w_gate', 'rwkv_k_k', 'rwkv_k_a',
        'rwkv_r_k', 'rwkv_gn_g', 'rwkv_gn_b', 'sgu_ln_g', 'sgu_ln_b', 'sgu_w_s', 'sgu_b_s', 'w_out',
        'norm_ffn2', 'ffn2_w1', 'ffn2_w3', 'ffn2_w2', 'norm_ple', 'w_ple_gate', 'w_ple', 'norm_final']


def shape_constants(P=128, levels=6):
    row, col = np.arange(P)[:, None], np.arange(P)[None, :]
    mid = row <= P // 2 - 1
    unit = -np.exp(np.float32(-0.5))
    incl, excl = (row <= col), (row < col)
    pairs = (row // 2 == col // 2) & excl
    head = np.stack([np.arange(P) < P // 2, np.arange(P) >= P // 2], axis=1)
    parts = [unit * (incl.astype(np.float32) - mid), unit * (excl.astype(np.float32) - mid),
             row > col, pairs, incl, excl, incl, head]
    for n in range(1, levels + 1):
        b = 2 ** n
        parts.append((row // (2 * b) == col // (2 * b)) & (row % (2 * b) < b) & (col % (2 * b) >= b))
    return np.ascontiguousarray(np.concatenate([a.astype(np.float32) for a in parts], axis=1))


def kernel(**inputs):
    import concourse.bacc as bacc
    from concourse.bass_utils import run_bass_kernel_spmd

    nc = bacc.Bacc("TRN2", target_bir_lowering=False, num_devices=1,
                   dynamic_dma_scratch_size=1024)
    arrays, io = {}, {}
    for name in _INS:
        a = np.ascontiguousarray(inputs[name])
        arrays[f"in_{name}"] = a
        io[name] = nc.dram_tensor(f"in_{name}", a.shape, mybir.dt.from_np(a.dtype), kind="ExternalInput").ap()
    arrays["in_masks"] = shape_constants()
    io["masks"] = nc.dram_tensor("in_masks", arrays["in_masks"].shape, F32, kind="ExternalInput").ap()
    out = nc.dram_tensor("out", inputs["x"].shape, F32, kind="ExternalOutput").ap()
    build(nc, io, out)
    return run_bass_kernel_spmd(nc, [arrays], core_ids=[0]).results[0]["out"]
```

```python
from contextlib import ExitStack

import numpy as np

import concourse.bass as bass
from concourse import mybir

F32 = mybir.dt.float32
F32R = mybir.dt.float32r
U32 = mybir.dt.uint32
ALU = mybir.AluOpType
ACT = mybir.ActivationFunctionType
AX_X = mybir.AxisListType.X

P = 128
NB = 512
RAW_SLOTS = 3
SPLIT_SLOTS = 6
UNIT = 1024
STAGES = "full"
MIX_CONSTS = 12


class Stage:

    def __init__(self, name, iters, body, first_unit, ring, start, raw_ring, unit=UNIT):
        self.name, self.iters, self.body, self.first = name, iters, body, first_unit
        self.ring, self.start, self.raw_ring, self.unit = ring, start, raw_ring, unit
        self.end = first_unit + iters * body

    def raw_at(self, j):
        if self.raw_ring == RAW_SLOTS:
            return (j % RAW_SLOTS) * self.unit
        return RAW_SLOTS * UNIT - 2 * self.unit + (j % 2) * self.unit

    def split_at(self, j):
        if self.ring == SPLIT_SLOTS:
            return ((self.start + j) % SPLIT_SLOTS) * self.unit
        return self.start * UNIT + (j % 2) * self.unit


def build(nc, io, out):
    x, p = io["x"], io["p"]
    T, D = x.shape[1], x.shape[2]
    F = io["ffn1_w1"].shape[2]
    KD = D // P
    HALVES = T // NB
    TT = T // P
    FT = F // P
    PLE = p.shape[3]
    KP = PLE // P
    IN_COLS = io["w_in"].shape[2]
    assert D == UNIT and HALVES == 2 and FT % 2 == 0 and IN_COLS % (2 * P) == 0

    stages, unit = {}, 0
    for name, iters, body, ring, start, raw_ring, width in (
        ("ffn1", FT // 2, 6, SPLIT_SLOTS, 0, RAW_SLOTS, UNIT),
        ("w_in", IN_COLS // P // 2, 2, 2, 0, 2, UNIT),
        ("w_out", KD // 2, 2, 2, 0, 2, UNIT),
        ("ffn2", FT // 2, 6, SPLIT_SLOTS, 2, RAW_SLOTS, UNIT),
        ("gate", KD // 2, 2, 2, 2, 2, UNIT + KP * P),
    ):
        stages[name] = Stage(name, iters, body, unit, ring, start, raw_ring, width)
        unit = stages[name].end

    G = RWKV_HEADS = io["rwkv_r_k"].shape[1]
    HD = io["rwkv_r_k"].shape[2]
    RW = RWKV_HEADS * HD
    KR = RW // P
    C = P
    CHUNKS = T // C
    SHIFTED = io["shift_mu"].shape[1] // P
    ZT = IN_COLS // P
    LORA, GATE = SHIFTED - 2, SHIFTED - 1
    LEVELS = 6
    assert HD == 64 and RW == NB and io["sgu_w_s"].shape[1] == 8 and CHUNKS % 2 == 0

    with ExitStack() as ctx:
        def sb(name, shape, dt=F32, where=ctx):
            return where.enter_context(nc.sbuf_tensor(name, shape, dt))

        def sem(name):
            return ctx.enter_context(nc.semaphore(name))

        def here():
            return nc.sbuf_base

        hT = sb("hT", [P, KD, T])
        aH_at = here()
        aH = sb("aH", [P, KD, T], F32R)
        aL_at = here()
        aL = sb("aL", [P, KD, T], F32R)
        wH_at = here()
        wH = sb("wH", [P, SPLIT_SLOTS * UNIT], F32R)
        wL_at = here()
        wL = sb("wL", [P, SPLIT_SLOTS * UNIT], F32R)
        raw_at = here()
        raw = sb("raw", [P, RAW_SLOTS * UNIT])
        ident = sb("ident", [P, P])
        ones = sb("ones", [P, 1])
        NORMS = ("ffn1", "mix", "ffn2", "ple", "final")
        VECTORS = {}
        n_rows = 0
        for name in ("norm_ffn1", "norm_mix", "norm_ffn2", "norm_ple", "norm_final", "shift_mu",
                     "rwkv_a0", "rwkv_k_k", "rwkv_k_a", "rwkv_r_k"):
            VECTORS[name] = n_rows
            n_rows += int(np.prod(io[name].shape)) // P
        vec_rows = sb("vec_rows", [n_rows, P])
        vecs = sb("vecs", [P, n_rows])
        inv_width = sb("inv_width", [P, 1])
        zero = sb("zero", [P, 1])
        neg_half = sb("neg_half", [P, 1])
        rms_eps = sb("rms_eps", [P, 1])

        psum = ctx.enter_context(nc.psum_tensor("psum", [P, 8, NB], F32))

        sq_at = here()
        sq = sb("sq", [P, 4, NB])
        sums = sb("sums", [P, 2, NB])
        rs = sb("rs", [P, 2, NB])
        rstd = sb("rstd", [P, TT])
        with ExitStack() as x_phase:
            xs = sb("xs", [P, TT, D], F32, x_phase)
        hid_at = nc.sbuf_base
        with ExitStack() as ffn_phase:
            hidH = sb("hidH", [P, 2, T], F32R, ffn_phase)
            hidL = sb("hidL", [P, 2, T], F32R, ffn_phase)
            silu = sb("silu", [P, 2, NB], F32, ffn_phase)
            hid = sb("hid", [P, 2, NB], F32, ffn_phase)
            p_at = nc.sbuf_base
        with ExitStack() as result_phase:
            outs = sb("outs", [P, 4, D], F32, result_phase)
        gain_rows = nc.alloc_sbuf_tensor_at("gain_rows", [P, D], F32, offset=p_at - 2 * NB * 4)
        pTH = nc.alloc_sbuf_tensor_at("pTH", [P, KP, T], F32R, offset=p_at)
        pTL = nc.alloc_sbuf_tensor_at("pTL", [P, KP, T], F32R, offset=p_at + KP * T * 4)
        p_rows = nc.alloc_sbuf_tensor_at("p_rows", [P, TT, PLE], F32, offset=hid_at)
        assert HALVES * NB == T

        KB = 1024
        spaces = [[hid_at, nc.sbuf_usable_end],
                  [wH_at + 2 * UNIT * 4, wH_at + 6 * UNIT * 4],
                  [wL_at + 2 * UNIT * 4, wL_at + 6 * UNIT * 4],
                  [sq_at, sq_at + 8 * NB * 4],
                  [aH_at, aH_at + KD * T * 4],
                  [raw_at, raw_at + UNIT * 4]]
        used = [(a + 31) // 32 * 32 for a, _ in spaces]
        placed = {}

        def over(name, shape, dt=F32, space=None):
            size = int(np.prod(shape[1:])) * (1 if dt == mybir.dt.uint8 else 4)
            size = (size + 31) // 32 * 32
            for n in (range(len(spaces)) if space is None else space):
                if used[n] + size <= spaces[n][1]:
                    at = used[n]
                    used[n] += size
                    placed[name] = at
                    return nc.alloc_sbuf_tensor_at(name, shape, dt, offset=at)
            raise AssertionError(f"no room for {name}: {[(b - u) for (a, b), u in zip(spaces, used)]}")

        def within(name, shape, other, offset):
            return nc.alloc_sbuf_tensor_at(name, shape, F32, offset=placed[other] + offset)

        if True:
            CONST = (1, 2, 0)
            WORK = (4, 3, 2, 1, 5, 0)
            zout = over("zout", [P, 2, T + 1], F32, (0,))
            shape_masks = over("shape_masks", [P, io["masks"].shape[1]], F32, CONST)
            w_lora = over("w_lora", [P, RW], F32, CONST)
            w_gate = over("w_gate", [P, RW], F32, CONST)
            w0_rows = over("w0_rows", [P, RW], F32, CONST)
            gn_g = over("gn_g", [P, RW], F32, CONST)
            gn_b = over("gn_b", [P, RW], F32, CONST)
            ln_g = over("ln_g", [P, NB], F32, CONST)
            ln_b = over("ln_b", [P, NB], F32, CONST)
            wsT = over("wsT", [P, 8, P], F32, CONST)
            b_s = over("b_s", [P, KR, P], F32, CONST)
            rk_heads = over("rk_heads", [P, KR, 2], F32, CONST)
            ka_rest = over("ka_rest", [P, KR], F32, CONST)
            ws_rows = over("ws_rows", [P, 8, P], F32, (0,))
            used[0] = placed["zout"]
            y_out = nc.alloc_sbuf_tensor_at("y_out", [P, KD, T], F32, offset=aL_at)

            zc = over("zc", [P, SHIFTED, C + 1], F32, WORK)
            gc = over("gc", [P, 2 * KR, C], F32, WORK)
            zs = over("zs", [P, SHIFTED, C], F32, WORK)
            tanh_w = over("tanh_w", [P, C], F32, WORK)
            sig_g = over("sig_g", [P, C], F32, WORK)
            sig_w = over("sig_w", [P, RW], F32, WORK)
            e_in = over("e_in", [P, KR, C], F32, WORK)
            e_ex = over("e_ex", [P, KR, C], F32, WORK)
            e_neg = over("e_neg", [P, KR, C], F32, WORK)
            e_mid = over("e_mid", [P, 2, KR], F32, WORK)
            e_end = over("e_end", [P, 2, KR], F32, WORK)
            carry = over("carry", [P, KR], F32, WORK)
            aT = over("aT", [P, KR, C], F32, WORK)
            kkT = over("kkT", [P, KR, C], F32, WORK)
            tmpT = over("tmpT", [P, KR, C], F32, WORK)
            kpT = over("kpT", [P, KR, C], F32, WORK)
            rkT = over("rkT", [P, KR, C], F32, WORK)
            prT = [over(f"prT{b}", [P, KR, 2, C], F32, WORK) for b in range(2)]
            bT = over("bT", [P, KR, C], F32, WORK)
            kT = over("kT", [P, KR, C], F32, WORK)
            p_nat = over("p_nat", [P, RW], F32, WORK)
            b_nat = over("b_nat", [P, RW], F32, WORK)
            k_nat = over("k_nat", [P, RW], F32, WORK)
            v_nat = over("v_nat", [P, RW], F32, WORK)
            g_nat = [over(f"g_nat{b}", [P, RW], F32, WORK) for b in range(2)]
            bonus = over("bonus", [P, 2, G], F32, WORK)
            kk_rn = over("kk_rn", [P, G], F32, WORK)
            nT = over("nT", [P, G, C], F32, WORK)
            xq = over("xq", [P, G, 2, C], F32, WORK)
            mq = over("mq", [P, G, 2, C], F32, WORK)
            xT = over("xT", [P, G, C], F32, WORK)
            yb = over("yb", [P, G, C], F32, WORK)
            tpT = within("tpT", [P, KR, C], "xT", 0)
            gv = within("gv", [P, RW], "yb", 0)
            u_nat = within("u_nat", [P, RW], "yb", RW * 4)
            state = over("state", [P, KR, HD], F32, WORK)
            state_sum = over("state_sum", [P, KR, HD], F32, WORK)
            yc = over("yc", [P, RW], F32, WORK)
            ysq = over("ysq", [P, RW], F32, WORK)
            bv = over("bv", [P, RW], F32, WORK)
            mean = over("mean", [P, G], F32, WORK)
            var = over("var", [P, G], F32, WORK)
            v_stats = over("v_stats", [P, 6], F32, WORK)
            v_mv = over("v_mv", [P, 2], F32, WORK)
            v_rs = over("v_rs", [P, 1], F32, WORK)
            vn = over("vn", [P, NB], F32, WORK)
            mixed = over("mixed", [P, KR, C], F32, WORK)

            decay_sums = shape_masks[:, 0:2 * C]
            lower = shape_masks[:, 2 * C:3 * C]
            band_incl = shape_masks[:, 3 * C:5 * C]
            strict_incl = shape_masks[:, 5 * C:7 * C]
            head_cols = shape_masks[:, 7 * C:7 * C + 2]
            merge_masks = (shape_masks[:, 7 * C + 2:7 * C + 2 + LEVELS * P].bitcast(U32)
                           .rearrange("p (l c) -> p l c", c=P))

        raw_ready = {n: [sem(f"raw_ready_{n}{i}") for i in range(s.raw_ring)] for n, s in stages.items()}
        high_done = sem("high_done")
        w_split = sem("w_split")
        w_free = sem("w_free")

        const_ready = sem("const_ready")
        made = sem("made")
        x_ready = [sem(f"x_ready{i}") for i in range(TT // 2)]
        x_turned = sem("x_turned")
        vecs_turned = sem("vecs_turned")
        vecs_ready = sem("vecs_ready")
        x_used_act = sem("x_used_act")
        x_used_dve = sem("x_used_dve")
        tiles = HALVES * KD
        SUMMED_BY_POOL = ("ffn1", "mix", "ple")
        NORM_PER = dict(squared=tiles, summed=tiles, spread=HALVES, rooted=HALVES, inverted=HALVES,
                        high=tiles, ready=tiles)
        norm = {k: sem(f"norm_{k}") for k in NORM_PER}
        tile_squared = sem("tile_squared")
        tile_summed = sem("tile_summed")

        def in_tiles(name, count):
            return ("ffn2", "final").index(name) * tiles + count

        def in_norm(name, k, count):
            order = SUMMED_BY_POOL if k in ("squared", "summed") else NORMS
            return order.index(name) * NORM_PER[k] + count

        ffn = {}
        for n in ("ffn1", "ffn2"):
            ffn[n] = {k: sem(f"{n}_{k}") for k in
                      ("up", "scaled", "silued", "banks_free", "product", "high", "hid_ready", "down", "added")}
        pT = {k: sem(f"p_{k}") for k in ("loaded", "turned", "high", "ready")}
        gate = {k: sem(f"gate_{k}") for k in ("done", "scaled", "sigmoid", "product", "added")}
        gain_ready = sem("gain_ready")
        fin = {k: sem(f"result_{k}") for k in ("turned", "copied", "stored0", "stored1", "stored2", "stored3")}

        def items(last):
            return [(0, 0), (1, 0), (0, 1), (1, 1)] if last else [(0, 0), (0, 1), (1, 0), (1, 1)]

        def frees(m, last):
            return (2 if m == 3 else 0) if last else m % 2

        if True:
            win = {k: sem(f"w_in_{k}") for k in ("done", "copied")}
            z_stored = [sem("z_stored0"), sem("z_stored1")]
            mix_consts = sem("mix_consts")
            mix_made = sem("mix_made")
            ws_turned = sem("ws_turned")
            ws_placed = sem("ws_placed")
            y_high = sem("y_high")
            delta_seen = sem("delta_seen")
            y_split = sem("y_split")
            w_out_done = sem("w_out_done")
            w_out_added = sem("w_out_added")
            zout_free = sem("zout_free")
            z_scratch = nc.dram_tensor("z_scratch", (ZT * P, T + 1), F32, kind="Internal").ap()
            PER = dict(
                z_loaded=16, g_loaded=16, shifted=6, lora_in=2, w_raw=1, a_raw=1, g_raw=1, w_biased=1,
                w_sig=1, a_ready=1, g_ready=1, decays=1, exps=5, kk_raw=2, kk_sums=1, kk_clamped=1,
                kk_rn=1, kk_spread=1, kk_unit=1, pr_ready=2, kk_a=1, b_ready=1, kp=3, k_ready=1,
                rk=1, bonus_raw=1, bonus=1, gelu=1, v_turned=1, v_stats=1, v_mv=1, v_ve=1, v_rs=1,
                v_norm=1, v_affine=2, mixed=1, mixed_b=1, sgu=1,
                nat_turned=4, nat_act=2, nat_dve=2, gram=10, gram_used=10, x_init=2,
                xt=12, xt_copied=12, y=12, y_copied=12, delta=12, x_upd=12, bv=1,
                tp=1, tp_copied=1, gmk=1, gmk_copied=1, u=1, u_copied=1, s_new=1, y_raw=1,
                s_sum=1, carry=1, state=1, mean=2, yc=1, ysq=1, var=2, y_rs=1, y_fin=5,
                y_turned=1, y_placed=1)
            ev = {k: sem("c_" + k) for k in PER}

            def at(name, c, k=None):
                n = PER[name]
                return (c + 2) * n + (n if k is None else k)

        io_w = {"ffn1": ("ffn1_w1", "ffn1_w3", "ffn1_w2"), "ffn2": ("ffn2_w1", "ffn2_w3", "ffn2_w2")}

        def columns_of(w, m, k):
            return io[w][0].rearrange("(k p) c -> p k c", p=P)[:, :k, bass.ts(m, P)]

        def rows_of(w, m):
            return io[w][0][bass.ts(m, P), :]

        def store_result(engine, t):
            engine.wait_ge(fin["copied"], 2 * t + 2)
            engine.dma_start(out[0, t * P:(t + 1) * P, :], outs[:, t % 4, :]).then_inc(fin[f"stored{t % 4}"], 16)

        block = ctx.enter_context(nc.Block())

        @block.sync
        def _(sp):
            def tile_source(s, i, j):
                if s.name in io_w:
                    w1, w3, w2 = io_w[s.name]
                    m = i * 2 + (j // 2 if j < 4 else j - 4)
                    if j < 4:
                        return columns_of((w1, w3)[j % 2], m, KD)
                    return rows_of(w2, m)
                return columns_of({"w_in": "w_in", "w_out": "w_out", "gate": "w_ple_gate"}[s.name],
                                  i * 2 + j, KD)

            def load_chunk(c):
                sp.wait_ge(ev["shifted"], at("shifted", c - 1))
                sp.dma_start(zc[:], z_scratch[0:SHIFTED * P, bass.ds(c * C, C + 1)]
                             .rearrange("(k p) c -> p k c", p=P)).then_inc(ev["z_loaded"], 16)
                sp.wait_ge(ev["sgu"], at("sgu", c - 1))
                sp.dma_start(gc[:], z_scratch[SHIFTED * P:ZT * P, bass.ds(c * C + 1, C)]
                             .rearrange("(k p) c -> p k c", p=P)).then_inc(ev["g_loaded"], 16)

            for s in stages.values():
                if s.name == "w_out":
                    for j in range(2):
                        sp.wait_ge(z_stored[j], 16 * (1 + ZT // 2))
                    load_chunk(0)
                    with sp.Fori(1, CHUNKS) as c:
                        load_chunk(c)
                with sp.Fori(0, s.iters) as i:
                    for j in range(s.body):
                        u = i * s.body + (s.first + j)
                        sp.wait_ge(w_split, u + (1 + RAW_SLOTS - s.raw_ring))
                        slot = s.raw_at(j)
                        dst = raw[:, slot:slot + UNIT]
                        src = tile_source(s, i, j)
                        if len(src.shape) == 3:
                            dst = dst.rearrange("p (k c) -> p k c", c=P)
                        ready = raw_ready[s.name][j % s.raw_ring]
                        sp.dma_start(dst, src).then_inc(ready, 16)
                        if s.name == "gate":
                            sp.dma_start(
                                raw[:, slot + UNIT:slot + s.unit].rearrange("p (k c) -> p k c", c=P),
                                columns_of("w_ple", i * 2 + j, KP)).then_inc(ready, 16)
            for t in range(0, TT, 2):
                store_result(sp, t)
            for t in range(4):
                sp.wait_ge(fin[f"stored{t}"], 16 * (TT // 4))

        @block.gpsimd
        def _(pool):
            pool.sem_inc(w_split, RAW_SLOTS)
            pool.memset(ident[:], 0.0).then_inc(made, 1)
            pool.memset(ones[:], 1.0).then_inc(made, 1)
            pool.memset(inv_width[:], 1.0 / D).then_inc(made, 1)
            pool.memset(zero[:], 0.0).then_inc(made, 1)
            pool.memset(neg_half[:], -0.5).then_inc(made, 1)
            pool.memset(rms_eps[:], 1e-6).then_inc(made, 1)
            pool.wait_ge(made, 6)
            pool.affine_select(out=ident[:], in_=ident[:], compare_op=ALU.not_equal, fill=1.0,
                               base=0, pattern=[[-1, P]], channel_multiplier=1).then_inc(made, 1)
            if True:
                for k, n in PER.items():
                    pool.sem_inc(ev[k], 2 * n)

            NORM_OF = {"ffn1": "ffn1", "w_in": "mix", "gate": "ple"}

            def norm_part(name):
                for h in range(HALVES):
                    for k in range(KD):
                        n = h * KD + k
                        pool.wait_ge(norm["squared"], in_norm(name, "squared", n + 1))
                        if k == 0:
                            pool.tensor_copy(sums[:, h, :], sq[:, n % 4, :]).then_inc(norm["summed"], 1)
                        else:
                            pool.wait_ge(norm["summed"], in_norm(name, "summed", n))
                            pool.tensor_tensor(sums[:, h, :], sums[:, h, :], sq[:, n % 4, :],
                                               ALU.add).then_inc(norm["summed"], 1)
            def mix_constants():
                pool.wait_ge(ffn["ffn1"]["added"], 4 + stages["ffn1"].iters * 2 * KD)
                pool.memset(zout[:, :, 0:1], 0.0).then_inc(mix_made, 1)
                pool.wait_ge(mix_consts, 16 * MIX_CONSTS)
                rk = VECTORS["rwkv_r_k"]
                pool.tensor_tensor(rk_heads[:], vecs[:, rk:rk + KR].unsqueeze(2).to_broadcast([P, KR, 2]),
                                   head_cols.unsqueeze(1).to_broadcast([P, KR, 2]),
                                   ALU.mult).then_inc(mix_made, 1)
                ka = VECTORS["rwkv_k_a"]
                pool.tensor_tensor(ka_rest[:], ones[:].to_broadcast([P, KR]), vecs[:, ka:ka + KR],
                                   ALU.subtract).then_inc(mix_made, 1)

            def shift(c, tiles, k):
                n = tiles.stop - tiles.start
                mu0 = VECTORS["shift_mu"]
                mu = vecs[:, mu0 + tiles.start:mu0 + tiles.stop].unsqueeze(2).to_broadcast([P, n, C])
                pool.tensor_tensor(zs[:, tiles, :], zc[:, tiles, 0:C], zc[:, tiles, 1:C + 1],
                                   ALU.subtract).then_inc(ev["shifted"], 1)
                pool.wait_ge(ev["shifted"], at("shifted", c, k + 1))
                pool.tensor_tensor(zs[:, tiles, :], zs[:, tiles, :], mu, ALU.mult).then_inc(ev["shifted"], 1)
                pool.wait_ge(ev["shifted"], at("shifted", c, k + 2))
                pool.tensor_tensor(zs[:, tiles, :], zs[:, tiles, :], zc[:, tiles, 1:C + 1],
                                   ALU.add).then_inc(ev["shifted"], 1)

            def wide(name, k=KR):
                v = VECTORS[name]
                return vecs[:, v:v + k].unsqueeze(2).to_broadcast([P, k, C])

            def pool_front(c):
                pool.wait_ge(ev["z_loaded"], at("z_loaded", c))
                pool.wait_ge(ev["nat_turned"], at("nat_turned", c - 1))
                pool.wait_ge(ev["pr_ready"], at("pr_ready", c - 1))
                pool.wait_ge(ev["a_raw"], at("a_raw", c - 1))
                shift(c, slice(LORA, SHIFTED), 0)
                pool.wait_ge(ev["k_ready"], at("k_ready", c - 1))
                shift(c, slice(0, LORA), 3)
                pool.wait_ge(ev["shifted"], at("shifted", c))
                pool.wait_ge(ev["kk_unit"], at("kk_unit", c - 1))
                pool.wait_ge(ev["b_ready"], at("b_ready", c - 1))
                kz, rz = zs[:, KR:2 * KR, :], zs[:, 0:KR, :]
                pool.tensor_tensor(kkT[:], kz, wide("rwkv_k_k"), ALU.mult).then_inc(ev["kk_raw"], 1)
                pool.wait_ge(ev["kk_raw"], at("kk_raw", c, 1))
                pool.tensor_tensor(tmpT[:], kkT[:], kkT[:], ALU.mult).then_inc(ev["kk_raw"], 1)
                pool.wait_ge(ev["v_ve"], at("v_ve", c))
                pool.tensor_tensor(v_rs[:], v_mv[:, 1:2], neg_half[:], ALU.pow).then_inc(ev["v_rs"], 1)
                pool.wait_ge(ev["kk_clamped"], at("kk_clamped", c))
                pool.tensor_tensor(kk_rn[:], kk_rn[:], neg_half[:].to_broadcast([P, G]),
                                   ALU.pow).then_inc(ev["kk_rn"], 1)
                pool.wait_ge(ev["a_ready"], at("a_ready", c))
                pool.tensor_tensor(kpT[:], aT[:], wide("rwkv_k_a"), ALU.mult).then_inc(ev["kp"], 1)
                pool.wait_ge(ev["kp"], at("kp", c, 1))
                pool.tensor_tensor(kpT[:], kpT[:], ka_rest[:].unsqueeze(2).to_broadcast([P, KR, C]),
                                   ALU.add).then_inc(ev["kp"], 1)
                pool.wait_ge(ev["kp"], at("kp", c, 2))
                pool.tensor_tensor(kpT[:], kpT[:], kz, ALU.mult).then_inc(ev["kp"], 1)
                pool.wait_ge(ev["kp"], at("kp", c))
                pool.wait_ge(ev["bonus_raw"], at("bonus_raw", c - 1))
                pool.tensor_tensor(rkT[:], rz, kpT[:], ALU.mult).then_inc(ev["rk"], 1)
                pool.wait_ge(ev["v_norm"], at("v_norm", c))
                pool.tensor_tensor(vn[:], vn[:], ln_g[:], ALU.mult).then_inc(ev["v_affine"], 1)
                pool.wait_ge(ev["v_affine"], at("v_affine", c, 1))
                pool.tensor_tensor(vn[:], vn[:], ln_b[:], ALU.add).then_inc(ev["v_affine"], 1)

            def head_wide(x):
                return x.unsqueeze(2).to_broadcast([P, G, HD])

            def heads(x):
                return x.rearrange("p (h d) -> p h d", d=HD)

            def pool_tail(c, par):
                pool.wait_ge(ev["var"], at("var", c))
                pool.tensor_tensor(var[:], var[:], neg_half[:].to_broadcast([P, G]), ALU.pow).then_inc(ev["y_rs"], 1)
                pool.wait_ge(ev["y_rs"], at("y_rs", c))
                pool.tensor_tensor(heads(yc[:]), heads(yc[:]), head_wide(var[:]), ALU.mult).then_inc(ev["y_fin"], 1)
                for k, (op, other) in enumerate(((ALU.mult, gn_g), (ALU.add, gn_b), (ALU.add, bv),
                                                 (ALU.mult, g_nat[par]))):
                    pool.wait_ge(ev["y_fin"], at("y_fin", c, k + 1))
                    pool.tensor_tensor(yc[:], yc[:], other[:], op).then_inc(ev["y_fin"], 1)

            def pool_rest(c, par, first, last):
                for g in range(2):
                    pool.wait_ge(ev["gram_used"], at("gram_used", c, 2 * g + 2))
                    x = xq[:, 4 * g:4 * g + 4, 0, :]
                    pool.tensor_tensor(x, x, ident[:].unsqueeze(1).to_broadcast([P, 4, C]),
                                       ALU.add).then_inc(ev["x_init"], 1)
                if not first:
                    pool_tail(c - 1, 1 - par)
                pool.wait_ge(ev["bonus"], at("bonus", c))
                pool.wait_ge(ev["nat_dve"], at("nat_dve", c))
                if not first:
                    pool.wait_ge(ev["y_fin"], at("y_fin", c - 1))
                pool.tensor_tensor(heads(bv[:]), heads(v_nat[:]), head_wide(bonus[:, par, :]),
                                   ALU.mult).then_inc(ev["bv"], 1)
                if not last:
                    pool_front(c + 1)

            for s in stages.values():
                if s.name == "w_out":
                    pool.wait_ge(win["copied"], 4 + 2 * ZT)
                    for j in range(2):
                        pool.wait_ge(z_stored[j], 16 * (1 + ZT // 2))
                    pool.wait_ge(ws_placed, 2)
                    pool.memset(state[:], 0.0).then_inc(mix_made, 1)
                    pool_front(0)
                    pool_rest(0, 0, True, False)
                    with pool.Fori(0, CHUNKS // 2 - 1) as i:
                        for b in range(2):
                            pool_rest(i * 2 + (1 + b), 1 - b, False, False)
                    pool_rest(CHUNKS - 1, 1, False, True)
                    pool_tail(CHUNKS - 1, 1)
                per = 2 if s.name == "gate" else 1

                def split_tile(i, j, freed):
                    u = i * s.body + (s.first + j)
                    turns = s.body // s.raw_ring
                    landed = (i * turns + (j // s.raw_ring + 1)) * (16 * per)
                    pool.wait_ge(raw_ready[s.name][j % s.raw_ring], landed)
                    pool.wait_ge(w_free, freed)
                    r, w = s.raw_at(j), s.split_at(j)
                    pool.tensor_tensor(wH[:, w:w + s.unit], raw[:, r:r + s.unit],
                                       zero[:].to_broadcast([P, s.unit]), ALU.add).then_inc(high_done, 1)
                    pool.wait_ge(high_done, u + 1)
                    pool.tensor_tensor(wL[:, w:w + s.unit], raw[:, r:r + s.unit],
                                       wH[:, w:w + s.unit].bitcast(F32),
                                       ALU.subtract).then_inc(w_split, 1)

                ahead = 4 if s.ring == SPLIT_SLOTS else 2
                for j in range(ahead):
                    u = s.first + j
                    split_tile(0, j, {"w_in": u + 1, "gate": s.first + 3}.get(
                        s.name, u + 1 + SPLIT_SLOTS - s.ring))
                if s.name in NORM_OF:
                    norm_part(NORM_OF[s.name])
                for j in range(ahead, s.body):
                    split_tile(0, j, s.first + j + 1)
                if s.name == "w_in":
                    mix_constants()
                with pool.Fori(1, s.iters) as i:
                    for j in range(s.body):
                        split_tile(i, j, i * s.body + (s.first + j) + (1 + SPLIT_SLOTS - s.ring))

        @block.tensor
        def _(pe):
            pe.sem_inc(w_free, SPLIT_SLOTS)

            def products(acc, wat, actH, actL, first, last):
                pe.matmul(acc, wH[:, wat:wat + P], actH, start=first, stop=False)
                pe.matmul(acc, wH[:, wat:wat + P], actL, start=False, stop=False)
                return pe.matmul(acc, wL[:, wat:wat + P], actH, start=False, stop=last)

            def half(h):
                return slice(h * NB, (h + 1) * NB)

            def turn_vecs():
                pe.wait_ge(made, 7)
                pe.wait_ge(const_ready, 16 * len(VECTORS))
                pe.transpose(psum[:, 0, 0:n_rows], vec_rows[:], ident[0:n_rows, 0:n_rows]).then_inc(vecs_turned, 1)

            def turn_x(h):
                for t in range(h * (TT // 2), (h + 1) * (TT // 2)):
                    if t % 2 == 0:
                        pe.wait_ge(x_ready[t // 2], 16)
                    for q in range(2):
                        if t >= 2:
                            pe.wait_ge(x_used_dve if q == 0 else x_used_act, t - 1)
                        for k in range(4):
                            m = pe.transpose(psum[:, 4 + 2 * (t % 2) + q, k * P:(k + 1) * P],
                                             xs[:, t, (4 * q + k) * P:(4 * q + k + 1) * P], ident[:])
                        m.then_inc(x_turned, 1)

            def spread_sums(name, h):
                if name == "ffn1" and h == 0:
                    turn_x(1)
                    pe.wait_ge(x_used_dve, TT)
                    pe.wait_ge(x_used_act, TT)
                if name in ("mix", "ple"):
                    s = ffn["ffn1" if name == "mix" else "ffn2"]
                    pe.wait_ge(s["added"], 4 + FT // 2 * 2 * KD)
                if name == "ffn2":
                    pe.wait_ge(tile_summed, in_tiles(name, tiles))
                else:
                    pe.wait_ge(norm["summed"], in_norm(name, "summed", (h + 1) * KD))
                pe.matmul(psum[:, 4 + h, :], inv_width[:].to_broadcast([P, P]), sums[:, h, :],
                          start=True, stop=True).then_inc(norm["spread"], 1)

            def ready(name, h, k):
                pe.wait_ge(norm["ready"], in_norm(name, "ready", h * KD + k + 1))

            def ffn_products(name, st):
                s = ffn[name]
                pe.sem_inc(s["banks_free"], 2)
                pe.sem_inc(s["added"], 4)

                def group(i, first):
                    for f in range(2):
                        for h in range(HALVES):
                            for w in range(2):
                                u = 2 * f + w
                                if h == 0:
                                    pe.wait_ge(w_split, i * 6 + (st.first + u + 1 + RAW_SLOTS))
                                bank = 2 * h + w
                                if w == 0:
                                    pe.wait_ge(s["banks_free"], i * 4 + (2 * f + h + 1))
                                for k in range(KD):
                                    if first and f == 0 and w == 0:
                                        ready(name, h, k)
                                    m = products(psum[:, bank, :], st.split_at(u) + k * P,
                                                 aH[:, k, half(h)], aL[:, k, half(h)],
                                                 k == 0, k == KD - 1)
                                if w == 1:
                                    m.then_inc(s["up"], 1)
                            if first and f == 0:
                                spread_sums(name, h)
                    for f in range(2):
                        pe.wait_ge(w_split, i * 6 + (st.first + 4 + f + 1 + RAW_SLOTS))
                    for h in range(HALVES):
                        pe.wait_ge(s["hid_ready"], i * 4 + (3 + h))
                        for d in range(KD):
                            bank = 4 + (h * KD + d) % 4
                            pe.wait_ge(s["added"], i * (2 * KD) + (h * KD + d + 1))
                            for f in range(2):
                                m = products(psum[:, bank, :], st.split_at(4 + f) + d * P,
                                             hidH[:, f, half(h)], hidL[:, f, half(h)],
                                             f == 0, f == 1)
                            m.then_inc(s["down"], 1)

                group(0, True)
                with pe.Fori(1, st.iters) as i:
                    group(i, False)

            def turn_p():
                pe.wait_ge(pT["loaded"], 16)
                for t in range(TT):
                    if t >= 2:
                        pe.wait_ge(pT["ready"], t - 1)
                    for k in range(KP):
                        m = pe.transpose(psum[:, 6 + t % 2, k * P:(k + 1) * P],
                                         p_rows[:, t, k * P:(k + 1) * P], ident[:])
                    m.then_inc(pT["turned"], 1)

            def gate_products(st):
                pe.sem_inc(gate["added"], 2)

                def group(i, first, last):
                    for m, (j, h) in enumerate(items(last)):
                        pe.wait_ge(w_split, i * 2 + (st.first + j + 1 + RAW_SLOTS))
                        pe.wait_ge(gate["added"], i * 4 + (m + 1))
                        w = st.split_at(j)
                        for k in range(KD):
                            if first and j == 0:
                                ready("ple", h, k)
                            products(psum[:, 2 * (m % 2), :], w + k * P, aH[:, k, half(h)],
                                     aL[:, k, half(h)], k == 0, k == KD - 1)
                        for k in range(KP):
                            mm_ = products(psum[:, 2 * (m % 2) + 1, :], w + UNIT + k * P,
                                           pTH[:, k, half(h)], pTL[:, k, half(h)],
                                           k == 0, k == KP - 1)
                        mm_.then_inc(gate["done"], 1)
                        if first and j == 0:
                            spread_sums("ple", h)
                        if last and m == 2:
                            result_sums(0)

                group(0, True, False)
                with pe.Fori(1, st.iters - 1) as i:
                    group(i, False, False)
                group(st.iters - 1, False, True)

            def result_sums(h):
                pe.wait_ge(tile_summed, in_tiles("final", tiles - (2 if h == 0 else 0)))
                for t in range(TT // 2):
                    m = pe.matmul(psum[:, 4 if h == 0 else 0, t:t + 1], sums[:, h, t * P:(t + 1) * P],
                                  inv_width[:], start=True, stop=True)
                m.then_inc(norm["spread"], 1)

            def turn_result():
                pe.wait_ge(norm["rooted"], in_norm("final", "rooted", 1))
                for t in range(TT):
                    if t == TT // 2:
                        result_sums(1)
                    for q in range(2):
                        bank = 4 + (2 * t + q) % 4
                        if t >= 2:
                            pe.wait_ge(fin["copied"], 2 * t + q - 3)
                        for k in range(4):
                            m = pe.transpose(psum[:, bank, k * P:(k + 1) * P],
                                             hT[:, 4 * q + k, t * P:(t + 1) * P], ident[:])
                        m.then_inc(fin["turned"], 1)

            def w_in_products(st):
                pe.sem_inc(win["copied"], 4)

                def group(i, first):
                    for j in range(2):
                        pe.wait_ge(w_split, i * 2 + (st.first + j + 1 + RAW_SLOTS))
                        for h in range(HALVES):
                            n = 2 * j + h
                            pe.wait_ge(win["copied"], i * 4 + (n + 1))
                            for k in range(KD):
                                if first and j == 0:
                                    ready("mix", h, k)
                                m = products(psum[:, n, :], st.split_at(j) + k * P, aH[:, k, half(h)],
                                             aL[:, k, half(h)], k == 0, k == KD - 1)
                            m.then_inc(win["done"], 1)
                            if first and j == 0:
                                spread_sums("mix", h)

                group(0, True)
                with pe.Fori(1, st.iters) as i:
                    group(i, False)

            def w_out_products(st):
                pe.sem_inc(w_out_added, 4)

                def group(i, first, last):
                    for n, (j, h) in enumerate(items(last)):
                        pe.wait_ge(w_split, i * 2 + (st.first + j + 1 + RAW_SLOTS))
                        pe.wait_ge(w_out_added, i * 4 + (n + 1))
                        for k in range(KD):
                            if first and j == 0:
                                pe.wait_ge(y_split, h * KD + k + 1)
                            m = products(psum[:, n, :], st.split_at(j) + k * P, aH[:, k, half(h)],
                                         aL[:, k, half(h)], k == 0, k == KD - 1)
                        m.then_inc(w_out_done, 1)

                group(0, True, False)
                with pe.Fori(1, st.iters - 1) as i:
                    group(i, False, False)
                turn_p()
                group(st.iters - 1, False, True)

            def turn_spatial():
                pe.wait_ge(mix_consts, 16 * MIX_CONSTS)
                for h in range(8):
                    m = pe.transpose(psum[:, 4 + h // 4, (h % 4) * P:(h % 4 + 1) * P], ws_rows[:, h, :], ident[:])
                    if h % 4 == 3:
                        m.then_inc(ws_turned, 1)

            def rows(h):
                return slice(HD * (h % 2), HD * (h % 2) + HD)

            def cols(h):
                return slice(HD * h, HD * h + HD)

            def head_at(slot):
                return 2 * (slot % 4) + slot // 4

            def mm(out, lhsT, rhs, start=True, stop=True):
                return pe.matmul(out, lhsT, rhs, start=start, stop=stop)

            def bank3(b):
                return psum[:, b, :].rearrange("p (k c) -> p k c", c=P)

            def pe_front(piece, c, par):
                if piece == 0:
                    pe.wait_ge(ev["lora_in"], at("lora_in", c, 1))
                    pe.wait_ge(ev["gram_used"], at("gram_used", c - 1, 9))
                    mm(psum[:, 4, :], tanh_w[0:64, :], w_lora[0:64, :]).then_inc(ev["w_raw"], 1)
                    pe.wait_ge(ev["gram_used"], at("gram_used", c - 1))
                    for k in range(KR):
                        m = mm(psum[:, 5, k * P:(k + 1) * P], w_lora[64:128, k * P:(k + 1) * P],
                               zs[64:128, LORA, :])
                    m.then_inc(ev["a_raw"], 1)
                    pe.wait_ge(ev["lora_in"], at("lora_in", c))
                    mm(psum[:, 6, :], sig_g[:], w_gate[:]).then_inc(ev["g_raw"], 1)
                if piece == 1:
                    pe.wait_ge(ev["gelu"], at("gelu", c))
                    pe.wait_ge(ev["sgu"], at("sgu", c - 1))
                    pe.wait_ge(ev["y_placed"], at("y_placed", c - 2))
                    for k in range(KR):
                        m = pe.transpose(psum[:, 7, k * P:(k + 1) * P], gc[:, KR + k, :], ident[:])
                    m.then_inc(ev["v_turned"], 1)
                    pe.wait_ge(ev["w_sig"], at("w_sig", c))
                    pe.wait_ge(ev["a_ready"], at("a_ready", c))
                    for k in range(KR):
                        m = mm(psum[:, 4 + k // 2, (k % 2) * 2 * C:(k % 2 + 1) * 2 * C],
                               sig_w[:, k * P:(k + 1) * P], decay_sums)
                    m.then_inc(ev["decays"], 1)
                if piece == 2:
                    pe.wait_ge(ev["kk_raw"], at("kk_raw", c))
                    pe.wait_ge(ev["g_ready"], at("g_ready", c))
                    for k in range(KR):
                        m = mm(psum[:, 6, 2 * k:2 * k + 2], tmpT[:, k, :], head_cols)
                    m.then_inc(ev["kk_sums"], 1)
                if piece == 3:
                    pe.wait_ge(ev["kk_rn"], at("kk_rn", c))
                    for h in range(G):
                        m = mm(psum[rows(h), 6, (h // 2) * P:(h // 2 + 1) * P],
                               kk_rn[:, h:h + 1].to_broadcast([P, HD]), ident[:])
                    m.then_inc(ev["kk_spread"], 1)
                if piece == 4:
                    pe.wait_ge(ev["v_affine"], at("v_affine", c))
                    for h in range(8):
                        m = mm(psum[rows(h), 7, (h // 2) * P:(h // 2 + 1) * P], vn[:, cols(h)], wsT[:, h, :])
                    m.then_inc(ev["mixed"], 1)
                if piece == 5:
                    pe.wait_ge(ev["rk"], at("rk", c))
                    pe.wait_ge(ev["kk_unit"], at("kk_unit", c))
                    for k in range(KR):
                        m = mm(psum[:, 6, 2 * k:2 * k + 2], rkT[:, k, :], rk_heads[:, k, :])
                    m.then_inc(ev["bonus_raw"], 1)

            def pe_turn_y(c):
                pe.wait_ge(ev["y_fin"], at("y_fin", c))
                for k in range(KR):
                    m = pe.transpose(psum[:, 7, k * P:(k + 1) * P], yc[:, k * P:(k + 1) * P], ident[:])
                m.then_inc(ev["y_turned"], 1)

            def pe_turn_x(c, n):
                g = n % 2
                for h in range(4):
                    m = pe.transpose(psum[:, 2 * g, h * P:(h + 1) * P], xq[:, 4 * g + h, 0, :], ident[:])
                m.then_inc(ev["xt"], 1)

            def pe_rest(c, par, first, last):
                pr = prT[par]
                pe.wait_ge(ev["pr_ready"], at("pr_ready", c))
                pe.wait_ge(ev["b_ready"], at("b_ready", c))
                pe.wait_ge(ev["k_ready"], at("k_ready", c))
                pe.wait_ge(ev["s_sum"], at("s_sum", c - 1))
                pe.wait_ge(ev["yc"], at("yc", c - 1))
                for n, src in enumerate((lambda k: pr[:, k, 0, :], lambda k: bT[:, k, :],
                                         lambda k: kT[:, k, :], lambda k: zs[:, 2 * KR + k, :])):
                    for k in range(KR):
                        m = pe.transpose(psum[:, n, k * P:(k + 1) * P], src(k), ident[:])
                    m.then_inc(ev["nat_turned"], 1)
                pe.wait_ge(ev["exps"], at("exps", c))
                pe.wait_ge(ev["bonus"], at("bonus", c))
                pe.wait_ge(ev["mixed_b"], at("mixed_b", c))
                for q in range(4):
                    for e in range(2):
                        h = head_at(2 * q + e)
                        m = mm(psum[:, 4 + q, e * 2 * C:(e + 1) * 2 * C], bT[rows(h), h // 2, :],
                               pr[rows(h), h // 2, :, :].rearrange("p a c -> p (a c)"))
                    m.then_inc(ev["gram"], 1)
                pe.wait_ge(ev["nat_act"], at("nat_act", c, 1))
                for q in range(2):
                    if q == 1:
                        pe.wait_ge(ev["nat_dve"], at("nat_dve", c, 1))
                    for e in range(4):
                        h = head_at(4 * q + e)
                        m = mm(psum[:, q, e * P:(e + 1) * P], pr[rows(h), h // 2, 0, :], bT[rows(h), h // 2, :])
                    m.then_inc(ev["gram"], 1)
                pe.wait_ge(ev["nat_act"], at("nat_act", c))
                pe.wait_ge(ev["nat_dve"], at("nat_dve", c))
                for q in range(4):
                    bank = 2 + q
                    if q >= 2:
                        pe.wait_ge(ev["gram_used"], at("gram_used", c, q - 1))
                    for e in range(2):
                        h = head_at(2 * q + e)
                        m = mm(psum[:, bank, e * 2 * C:(e + 1) * 2 * C], kT[rows(h), h // 2, :],
                               pr[rows(h), h // 2, :, :].rearrange("p a c -> p (a c)"))
                    m.then_inc(ev["gram"], 1)
                for g in range(2):
                    pe.wait_ge(ev["x_init"], at("x_init", c, g + 1))
                    pe.wait_ge(ev["gram_used"], at("gram_used", c, 5 if g == 0 else 7))
                    pe_turn_x(c, g)
                for lev in range(LEVELS):
                    for g in range(2):
                        n = 2 * lev + g
                        pe.wait_ge(ev["xt_copied"], at("xt_copied", c, n + 1))
                        if lev == 0:
                            pe.wait_ge(ev["gram_used"], at("gram_used", c, 6))
                        for e in range(4):
                            h = 4 * g + e
                            m = mm(psum[:, 2 * g, e * P:(e + 1) * P], nT[:, h, :], xq[:, h, 0, :])
                        m.then_inc(ev["y"], 1)
                    for g in range(2):
                        n = 2 * lev + g
                        pe.wait_ge(ev["y_copied"], at("y_copied", c, n + 1))
                        if lev == 0:
                            pe.wait_ge(ev["gram_used"], at("gram_used", c, 8))
                        for e in range(4):
                            h = 4 * g + e
                            m = mm(psum[:, 2 * g + 1, e * P:(e + 1) * P], xT[:, h, :], yb[:, h, :])
                        m.then_inc(ev["delta"], 1)
                    if lev == 1 and not first:
                        pe.wait_ge(ev["mixed_b"], at("mixed_b", c))
                        pe_turn_y(c - 1)
                    if not last:
                        pe_front(lev, c + 1, 1 - par)
                    for g in range(2):
                        n = 2 * lev + g
                        pe.wait_ge(ev["x_upd"], at("x_upd", c, n + 1))
                        if lev < LEVELS - 1:
                            pe_turn_x(c, n)
                for slot in range(G):
                    h = head_at(slot)
                    m = mm(psum[rows(h), 0, (h // 2) * P:(h // 2 + 1) * P], p_nat[:, cols(h)], xq[:, slot, 0, :])
                m.then_inc(ev["tp"], 1)
                pe.wait_ge(ev["gram_used"], at("gram_used", c))
                for slot in range(G):
                    h = head_at(slot)
                    m = mm(psum[:, 1, cols(h)], mq[:, slot, 0, :], v_nat[:, cols(h)])
                m.then_inc(ev["gmk"], 1)
                pe.wait_ge(ev["gmk_copied"], at("gmk_copied", c))
                pe.wait_ge(ev["tp_copied"], at("tp_copied", c))
                pe.wait_ge(ev["state"], at("state", c - 1))
                for slot in range(G):
                    h = head_at(slot)
                    o = psum[:, 2 + h % 2, cols(h // 2)]
                    mm(o, xq[:, slot, 0, :], gv[:, cols(h)], True, False)
                    m = mm(o, tpT[rows(h), h // 2, :], state[rows(h), h // 2, :], False, True)
                m.then_inc(ev["u"], 1)
                pe.wait_ge(ev["u_copied"], at("u_copied", c))
                for h in range(G):
                    o = psum[rows(h), 2, (h // 2) * HD:(h // 2 + 1) * HD]
                    mm(o, b_nat[:, cols(h)], u_nat[:, cols(h)], True, False)
                    m = mm(o, k_nat[:, cols(h)], v_nat[:, cols(h)], False, True)
                m.then_inc(ev["s_new"], 1)
                for slot in range(G):
                    h = head_at(slot)
                    o = psum[:, h % 2, cols(h // 2)]
                    mm(o, pr[rows(h), h // 2, 1, :], state[rows(h), h // 2, :], True, False)
                    mm(o, xq[:, slot, 1, :], u_nat[:, cols(h)], False, False)
                    m = mm(o, mq[:, slot, 1, :], v_nat[:, cols(h)], False, True)
                m.then_inc(ev["y_raw"], 1)

            def pe_mix():
                pe.wait_ge(mix_made, 4)
                for piece in range(6):
                    pe_front(piece, 0, 0)
                pe_rest(0, 0, True, False)
                with pe.Fori(0, CHUNKS // 2 - 1) as i:
                    for b in range(2):
                        pe_rest(i * 2 + (1 + b), 1 - b, False, False)
                pe_rest(CHUNKS - 1, 1, False, True)
                pe_turn_y(CHUNKS - 1)

            turn_vecs()
            turn_x(0)
            ffn_products("ffn1", stages["ffn1"])
            w_in_products(stages["w_in"])
            turn_spatial()
            pe_mix()
            w_out_products(stages["w_out"])
            ffn_products("ffn2", stages["ffn2"])
            gate_products(stages["gate"])
            turn_result()

        @block.scalar
        def _(act):
            def half(h):
                return slice(h * NB, (h + 1) * NB)

            def load_x():
                for c in range(TT // 2):
                    act.dma_start(xs[:, 2 * c:2 * c + 2, :],
                                  x[0, 2 * c * P:(2 * c + 2) * P, :].rearrange("(t q) c -> q t c", q=P)
                                  ).then_inc(x_ready[c], 16)
                for name, row in VECTORS.items():
                    v = io[name]
                    v = (v.rearrange("(k p) -> k p", p=P) if len(v.shape) == 1 else
                         v.rearrange("o (k p) -> (o k) p", p=P) if len(v.shape) == 2 else
                         v.rearrange("o (k a) c -> (o k) (a c)", a=2))
                    act.dma_start(vec_rows[row:row + v.shape[0], :], v).then_inc(const_ready, 16)

            def place_x(h):
                for t in range(h * (TT // 2), (h + 1) * (TT // 2)):
                    act.wait_ge(x_turned, 2 * t + 2)
                    act.activation(hT[:, 4:8, t * P:(t + 1) * P],
                                   psum[:, 4 + 2 * (t % 2) + 1, :].rearrange("p (k c) -> p k c", c=P),
                                   ACT.Copy).then_inc(x_used_act, 1)

            def highs(name, gain, h, final, square=True):
                for k in range(KD):
                    final(h, k)
                    n = h * KD + k
                    act.activation(aH[:, k, half(h)], hT[:, k, half(h)], ACT.Copy,
                                   scale=vecs[:, gain + k:gain + k + 1]).then_inc(norm["high"], 1)
                    if square:
                        if n >= 4:
                            act.wait_ge(norm["summed"], in_norm(name, "summed", n - 3))
                        act.activation(sq[:, n % 4, :], hT[:, k, half(h)], ACT.Square).then_inc(norm["squared"], 1)

            def root(name, h):
                act.wait_ge(norm["spread"], in_norm(name, "spread", h + 1))
                act.activation(rs[:, h, :], psum[:, 4 + h, :], ACT.Sqrt, bias=rms_eps[:]).then_inc(norm["rooted"], 1)

            def hidden(name, st):
                s = ffn[name]

                def group(i, first):
                    for f in range(2):
                        for h in range(HALVES):
                            n = 2 * f + h
                            if first and f == 0:
                                root(name, h)
                            act.wait_ge(s["scaled"], i * 4 + (n + 1))
                            act.activation(silu[:, h, :], silu[:, h, :], ACT.Silu).then_inc(s["silued"], 1)
                            act.wait_ge(s["product"], i * 4 + (n + 1))
                            act.activation(hidH[:, f, half(h)], hid[:, h, :], ACT.Copy).then_inc(s["high"], 1)

                group(0, True)
                with act.Fori(1, st.iters) as i:
                    group(i, False)

            def after_adds(name, st):
                base = (st.iters - 1) * 2 * KD + 4
                return lambda h, k: act.wait_ge(ffn[name]["added"], base + h * KD + k + 1)

            def split_p():
                for t in range(TT):
                    act.wait_ge(pT["turned"], t + 1)
                    act.activation(pTH[:, :, t * P:(t + 1) * P],
                                   psum[:, 6 + t % 2, 0:PLE].rearrange("p (k c) -> p k c", c=P),
                                   ACT.Copy).then_inc(pT["high"], 1)

            def gate_sigmoid(st):
                act.wait_ge(ffn["ffn2"]["added"], 4 + st_ffn2.iters * 2 * KD)
                act.dma_start(gain_rows[:], io["norm_final"].unsqueeze(0).to_broadcast([P, D])
                              ).then_inc(gain_ready, 16)

                def group(i, first):
                    for m in range(4):
                        if first and m < 2:
                            root("ple", m)
                        act.wait_ge(gate["scaled"], i * 4 + (m + 1))
                        act.activation(silu[:, m % 2, :], silu[:, m % 2, :],
                                       ACT.Sigmoid).then_inc(gate["sigmoid"], 1)

                group(0, True)
                with act.Fori(1, st.iters) as i:
                    group(i, False)

            def load_mix_consts():
                act.wait_ge(ffn["ffn1"]["added"], 4 + stages["ffn1"].iters * 2 * KD)
                loads = [(shape_masks[:], io["masks"]),
                         (w_lora[0:64, :], io["rwkv_w_decay"][0]), (w_lora[64:128, :], io["rwkv_w_aaa"][0]),
                         (w_gate[:], io["rwkv_w_gate"][0]),
                         (ws_rows[:], io["sgu_w_s"][0].rearrange("h t s -> t h s"))]
                for dst, name in ((w0_rows, "rwkv_w0"), (gn_g, "rwkv_gn_g"), (gn_b, "rwkv_gn_b"),
                                  (ln_g, "sgu_ln_g"), (ln_b, "sgu_ln_b")):
                    loads.append((dst[:], io[name][0:1, :].to_broadcast([P, NB])))
                for e in range(2):
                    loads.append((b_s[64 * e:64 * e + 64, :, :],
                                  io["sgu_b_s"].rearrange("o (k a) t -> a o k t", a=2)[e]
                                  .to_broadcast([64, KR, P])))
                assert len(loads) == MIX_CONSTS
                for dst, src in loads:
                    act.dma_start(dst, src).then_inc(mix_consts, 16)

            def store_z(st):
                for j in range(2):
                    act.sem_inc(z_stored[j], 16)
                act.wait_ge(mix_made, 1)
                with act.Fori(0, st.iters) as i:
                    for j in range(2):
                        act.wait_ge(z_stored[j], i * 16 + 16)
                        act.sem_inc(zout_free, 1)
                        act.wait_ge(win["copied"], i * 4 + (4 + 2 * j + 2))
                        act.dma_start(z_scratch[bass.ds(i * 2 * P + j * P, P), :],
                                      zout[:, j, :]).then_inc(z_stored[j], 16)

            def act_front(piece, c, par):
                if piece == 0:
                    act.wait_ge(ev["shifted"], at("shifted", c, 3))
                    act.activation(tanh_w[0:64, :], zs[0:64, LORA, :], ACT.Tanh).then_inc(ev["lora_in"], 1)
                    act.activation(sig_g[:], zs[:, GATE, :], ACT.Sigmoid).then_inc(ev["lora_in"], 1)
                    act.wait_ge(ev["a_raw"], at("a_raw", c))
                    a0 = VECTORS["rwkv_a0"]
                    act.wait_ge(ev["kp"], at("kp", c - 1))
                    act.wait_ge(ev["kk_a"], at("kk_a", c - 1))
                    for k in range(KR):
                        m = act.activation(aT[:, k, :], psum[:, 5, k * P:(k + 1) * P], ACT.Sigmoid,
                                           bias=vecs[:, a0 + k:a0 + k + 1])
                    m.then_inc(ev["a_ready"], 1)
                    act.wait_ge(ev["w_biased"], at("w_biased", c))
                    act.activation(sig_w[:], sig_w[:], ACT.Sigmoid).then_inc(ev["w_sig"], 1)
                    act.wait_ge(ev["g_raw"], at("g_raw", c))
                    act.activation(g_nat[par][:], psum[:, 6, :], ACT.Copy).then_inc(ev["g_ready"], 1)
                    act.wait_ge(ev["g_loaded"], at("g_loaded", c))
                    act.activation(gc[:], gc[:], ACT.Gelu).then_inc(ev["gelu"], 1)
                if piece == 2:
                    act.wait_ge(ev["decays"], at("decays", c))
                    act.wait_ge(ev["pr_ready"], at("pr_ready", c - 1))
                    act.wait_ge(ev["b_ready"], at("b_ready", c - 1))
                    act.wait_ge(ev["k_ready"], at("k_ready", c - 1))
                    sums = psum[:, 4:6, :].rearrange("p b (k w t) -> p b k w t", w=2, t=C)
                    incl, excl = sums[:, :, :, 0, :], sums[:, :, :, 1, :]

                    def tiles(x):
                        return x.rearrange("p (b k) c -> p b k c", k=2)
                    act.activation(tiles(e_in[:]), incl, ACT.Exp).then_inc(ev["exps"], 1)
                    act.activation(tiles(e_ex[:]), excl, ACT.Exp).then_inc(ev["exps"], 1)
                    act.activation(tiles(e_neg[:]), incl, ACT.Exp, scale=-1.0).then_inc(ev["exps"], 1)
                    act.activation(e_mid[:, par, :].rearrange("p (b k) -> p b k", k=2),
                                   excl[:, :, :, 0], ACT.Exp, scale=-1.0).then_inc(ev["exps"], 1)
                    act.activation(e_end[:, par, :].rearrange("p (b k) -> p b k", k=2),
                                   incl[:, :, :, C - 1], ACT.Exp).then_inc(ev["exps"], 1)

            def by_parity(x):
                return x.rearrange("p (k e d) -> p e k d", e=2, d=HD)

            def parities(bank):
                return psum[:, bank:bank + 2, 0:NB // 2].rearrange("p e (k d) -> p e k d", d=HD)

            def act_place_y(c):
                act.wait_ge(ev["y_turned"], at("y_turned", c))
                act.activation(y_out[:, 0:KR, bass.ds(c * C, C)],
                               psum[:, 7, :].rearrange("p (k c) -> p k c", c=P),
                               ACT.Copy).then_inc(ev["y_placed"], 1)

            def act_copy_xt(c, n):
                g = n % 2
                act.wait_ge(ev["xt"], at("xt", c, n + 1))
                act.activation(xT[:, 4 * g:4 * g + 4, :], psum[:, 2 * g, :].rearrange("p (h c) -> p h c", c=P),
                               ACT.Copy).then_inc(ev["xt_copied"], 1)

            def act_rest(c, par, first, last):
                for n, (bank, dst) in enumerate(((0, p_nat), (2, k_nat))):
                    act.wait_ge(ev["nat_turned"], at("nat_turned", c, bank + 1))
                    act.activation(dst[:], psum[:, bank, :], ACT.Copy).then_inc(ev["nat_act"], 1)
                for g in range(2):
                    act_copy_xt(c, g)
                for lev in range(LEVELS):
                    for g in range(2):
                        n = 2 * lev + g
                        act.wait_ge(ev["y"], at("y", c, n + 1))
                        act.activation(yb[:, 4 * g:4 * g + 4, :],
                                       psum[:, 2 * g, :].rearrange("p (h c) -> p h c", c=P),
                                       ACT.Copy).then_inc(ev["y_copied"], 1)
                    if lev == 1 and not first:
                        act_place_y(c - 1)
                    if not last:
                        act_front(lev, c + 1, 1 - par)
                    if lev < LEVELS - 1:
                        for g in range(2):
                            act_copy_xt(c, 2 * lev + 2 + g)
                act.wait_ge(ev["tp"], at("tp", c))
                act.activation(tpT[:], psum[:, 0, :].rearrange("p (k c) -> p k c", c=P),
                               ACT.Copy).then_inc(ev["tp_copied"], 1)
                act.wait_ge(ev["u"], at("u", c))
                act.activation(by_parity(u_nat[:]), parities(2), ACT.Copy).then_inc(ev["u_copied"], 1)
                act.wait_ge(ev["yc"], at("yc", c))
                act.activation(ysq[:], yc[:], ACT.Square).then_inc(ev["ysq"], 1)

            def act_mix():
                for piece in range(6):
                    act_front(piece, 0, 0)
                act_rest(0, 0, True, False)
                with act.Fori(0, CHUNKS // 2 - 1) as i:
                    for b in range(2):
                        act_rest(i * 2 + (1 + b), 1 - b, False, False)
                act_rest(CHUNKS - 1, 1, False, True)
                act_place_y(CHUNKS - 1)
                for h in range(HALVES):
                    for k in range(KD):
                        if h == 0 and k == 0:
                            act.wait_ge(ev["y_placed"], at("y_placed", CHUNKS - 1))
                            act.wait_ge(ev["sgu"], at("sgu", CHUNKS - 1))
                            act.wait_ge(ev["y_turned"], at("y_turned", CHUNKS - 1))
                            act.wait_ge(ev["y_fin"], at("y_fin", CHUNKS - 1))
                        act.activation(aH[:, k, half(h)], y_out[:, k, half(h)], ACT.Copy).then_inc(y_high, 1)

            load_x()
            act.wait_ge(made, 7)
            g = VECTORS["norm_ffn1"]
            for h in range(HALVES):
                place_x(h)
                if h == 0:
                    act.wait_ge(vecs_ready, 1)
                highs("ffn1", g, h, lambda h, k: k == 0 and (
                    act.wait_ge(x_used_dve, (h + 1) * (TT // 2)), act.wait_ge(x_used_act, (h + 1) * (TT // 2))))
            hidden("ffn1", stages["ffn1"])
            for h in range(HALVES):
                highs("mix", VECTORS["norm_mix"], h, after_adds("ffn1", stages["ffn1"]))
            load_mix_consts()
            for h in range(HALVES):
                root("mix", h)
            store_z(stages["w_in"])
            act_mix()
            act.dma_start(p_rows[:], p[0, 0].rearrange("(t q) c -> q t c", q=P)).then_inc(pT["loaded"], 16)
            split_p()
            n = 4 * (stages["w_out"].iters - 1) + 4
            for h in range(HALVES):
                highs("ffn2", VECTORS["norm_ffn2"], h,
                      lambda h, k: k == 0 and act.wait_ge(w_out_added, n + 2 * h + 2), square=False)
            hidden("ffn2", stages["ffn2"])
            st_ffn2 = stages["ffn2"]
            for h in range(HALVES):
                highs("ple", VECTORS["norm_ple"], h, after_adds("ffn2", st_ffn2))
            gate_sigmoid(stages["gate"])
            for h in range(HALVES):
                act.wait_ge(norm["spread"], in_norm("final", "spread", h + 1))
                c = h * (TT // 2)
                act.activation(rstd[:, c:c + TT // 2], psum[:, 4 if h == 0 else 0, 0:TT // 2], ACT.Sqrt,
                               bias=rms_eps[:]).then_inc(norm["rooted"], 1)
            for t in range(1, TT, 2):
                store_result(act, t)

        @block.vector
        def _(dve):
            def half(h):
                return slice(h * NB, (h + 1) * NB)

            def place_x(h):
                for t in range(h * (TT // 2), (h + 1) * (TT // 2)):
                    dve.wait_ge(x_turned, 2 * t + 1)
                    dve.tensor_copy(hT[:, 0:4, t * P:(t + 1) * P],
                                    psum[:, 4 + 2 * (t % 2), :].rearrange("p (k c) -> p k c", c=P)
                                    ).then_inc(x_used_dve, 1)

            def low(name, h, k):
                gain = VECTORS["norm_" + name] + k
                dve.wait_ge(norm["high"], in_norm(name, "high", h * KD + k + 1))
                dve.scalar_tensor_tensor(out=aL[:, k, half(h)], in0=hT[:, k, half(h)],
                                         scalar=vecs[:, gain:gain + 1], in1=aH[:, k, half(h)].bitcast(F32),
                                         op0=ALU.mult, op1=ALU.subtract).then_inc(norm["ready"], 1)

            def sum_square(name, n, hk, slot, h, first):
                if first:
                    dve.sem_inc(tile_squared, 1)
                    dve.tensor_tensor(sums[:, h, :], hk, hk, ALU.mult).then_inc(tile_summed, 1)
                    return
                dve.tensor_tensor(sq[:, slot, :], hk, hk, ALU.mult).then_inc(tile_squared, 1)
                dve.wait_ge(tile_squared, n + in_tiles(name, 0))
                dve.wait_ge(tile_summed, n + in_tiles(name, -1))
                dve.tensor_tensor(sums[:, h, :], sums[:, h, :], sq[:, slot, :], ALU.add).then_inc(tile_summed, 1)

            def invert(name, h):
                dve.wait_ge(norm["rooted"], in_norm(name, "rooted", h + 1))
                dve.reciprocal(rs[:, h, :], rs[:, h, :]).then_inc(norm["inverted"], 1)
                dve.wait_ge(norm["inverted"], in_norm(name, "inverted", h + 1))

            def hidden_and_adds(name, st, next_norm):
                s = ffn[name]

                def group(i, first, last):
                    for f in range(2):
                        for h in range(HALVES):
                            n = 2 * f + h
                            dve.wait_ge(s["up"], i * 4 + (n + 1))
                            if first and f == 0:
                                invert(name, h)
                            dve.tensor_tensor(silu[:, h, :], psum[:, 2 * h, :], rs[:, h, :],
                                              ALU.mult).then_inc(s["scaled"], 1)
                            if h == 1:
                                dve.sem_inc(w_free, 2)
                            dve.tensor_tensor(hid[:, h, :], psum[:, 2 * h + 1, :], rs[:, h, :],
                                              ALU.mult).then_inc(s["banks_free"], 1)
                            dve.wait_ge(s["banks_free"], i * 4 + (n + 3))
                            dve.wait_ge(s["silued"], i * 4 + (n + 1))
                            dve.tensor_tensor(hid[:, h, :], silu[:, h, :], hid[:, h, :],
                                              ALU.mult).then_inc(s["product"], 1)
                            dve.wait_ge(s["high"], i * 4 + (n + 1))
                            dve.tensor_tensor(hidL[:, f, half(h)], hid[:, h, :],
                                              hidH[:, f, half(h)].bitcast(F32),
                                              ALU.subtract).then_inc(s["hid_ready"], 1)
                    for h in range(HALVES):
                        for d in range(KD):
                            n = h * KD + d
                            dve.wait_ge(s["down"], i * (2 * KD) + (n + 1))
                            if n == 2 * KD - 1:
                                dve.sem_inc(w_free, 2)
                            dve.wait_ge(s["added"], i * (2 * KD) + (n + 1))
                            dve.scalar_tensor_tensor(out=hT[:, d, half(h)], in0=psum[:, 4 + n % 4, :],
                                                     scalar=0.5, in1=hT[:, d, half(h)],
                                                     op0=ALU.mult, op1=ALU.add).then_inc(s["added"], 1)
                            if last and n >= 1:
                                low(next_norm, (n - 1) // KD, (n - 1) % KD)
                    if last:
                        low(next_norm, 1, KD - 1)

                group(0, True, False)
                with dve.Fori(1, st.iters - 1) as i:
                    group(i, False, False)
                group(st.iters - 1, False, True)

            def scale_z(st):
                def group(i, first):
                    for j in range(2):
                        dve.wait_ge(zout_free, i * 2 + (j + 1))
                        for h in range(HALVES):
                            n = 2 * j + h
                            dve.wait_ge(win["done"], i * 4 + (n + 1))
                            if h == 1:
                                dve.sem_inc(w_free, 1)
                            if first and j == 0:
                                invert("mix", h)
                            dve.tensor_tensor(zout[:, j, 1 + h * NB:1 + (h + 1) * NB], psum[:, n, :],
                                              rs[:, h, :], ALU.mult).then_inc(win["copied"], 1)

                group(0, True)
                with dve.Fori(1, st.iters) as i:
                    group(i, False)

            def split_p():
                for t in range(TT):
                    dve.wait_ge(pT["high"], t + 1)
                    dve.tensor_tensor(pTL[:, :, t * P:(t + 1) * P],
                                      psum[:, 6 + t % 2, 0:PLE].rearrange("p (k c) -> p k c", c=P),
                                      pTH[:, :, t * P:(t + 1) * P].bitcast(F32), ALU.subtract).then_inc(pT["ready"], 1)

            def gate_adds(st):
                def group(i, first, last):
                    for m, (j, h) in enumerate(items(last)):
                        s = silu[:, m % 2, :]
                        dve.wait_ge(gate["done"], i * 4 + (m + 1))
                        if frees(m, last):
                            dve.sem_inc(w_free, frees(m, last))
                        if first and j == 0:
                            invert("ple", h)
                        dve.tensor_tensor(s, psum[:, 2 * (m % 2), :], rs[:, h, :],
                                          ALU.mult).then_inc(gate["scaled"], 1)
                        dve.wait_ge(gate["sigmoid"], i * 4 + (m + 1))
                        dve.tensor_tensor(s, s, psum[:, 2 * (m % 2) + 1, :], ALU.mult).then_inc(gate["product"], 1)
                        dve.wait_ge(gate["product"], i * 4 + (m + 1))
                        hk = hT[:, bass.ds(i * 2 + j, 1), half(h)].rearrange("p a c -> p (a c)")
                        dve.tensor_tensor(hk, hk, s, ALU.add).then_inc(gate["added"], 1)
                        dve.wait_ge(gate["added"], i * 4 + (m + 3))
                        sum_square("final", i * 4 + (m + 1), hk, m, h, first and j == 0)

                group(0, True, False)
                with dve.Fori(1, st.iters - 1) as i:
                    group(i, False, False)
                group(st.iters - 1, False, True)

            def scale_result():
                dve.wait_ge(gain_ready, 16)
                for t in range(TT):
                    if t % (TT // 2) == 0:
                        n = 1 + t // (TT // 2)
                        dve.wait_ge(norm["rooted"], in_norm("final", "rooted", n))
                        dve.reciprocal(rstd[:, t:t + TT // 2], rstd[:, t:t + TT // 2]).then_inc(norm["inverted"], 1)
                        dve.wait_ge(norm["inverted"], in_norm("final", "inverted", n))
                    if t >= 4:
                        dve.wait_ge(fin[f"stored{t % 4}"], 16 * (t // 4))
                    for q in range(2):
                        dve.wait_ge(fin["turned"], 2 * t + q + 1)
                        dve.scalar_tensor_tensor(out=outs[:, t % 4, q * NB:(q + 1) * NB],
                                                 in0=psum[:, 4 + (2 * t + q) % 4, :], scalar=rstd[:, t:t + 1],
                                                 in1=gain_rows[:, q * NB:(q + 1) * NB],
                                                 op0=ALU.mult, op1=ALU.mult).then_inc(fin["copied"], 1)

            def place_spatial():
                for g in range(2):
                    dve.wait_ge(ws_turned, g + 1)
                    dve.tensor_tensor(wsT[:, 4 * g:4 * g + 4, :],
                                      psum[:, 4 + g, :].rearrange("p (h c) -> p h c", c=P),
                                      strict_incl[:, C:2 * C].unsqueeze(1).to_broadcast([P, 4, C]),
                                      ALU.mult).then_inc(ws_placed, 1)

            def dve_front(piece, c, par):
                kz, rz = zs[:, KR:2 * KR, :], zs[:, 0:KR, :]
                bank7 = psum[:, 7, :].rearrange("p (k c) -> p k c", c=P)
                if piece == 0:
                    dve.wait_ge(ev["w_raw"], at("w_raw", c))
                    dve.wait_ge(ev["decays"], at("decays", c - 1))
                    dve.tensor_tensor(sig_w[:], psum[:, 4, :], w0_rows[:], ALU.add).then_inc(ev["w_biased"], 1)
                if piece == 1:
                    dve.wait_ge(ev["v_turned"], at("v_turned", c))
                    dve.bn_stats(v_stats[:], psum[:, 7, :]).then_inc(ev["v_stats"], 1)
                    dve.wait_ge(mix_consts, 16 * MIX_CONSTS)
                    dve.wait_ge(ev["v_stats"], at("v_stats", c))
                    dve.bn_aggr(v_mv[:], v_stats[:]).then_inc(ev["v_mv"], 1)
                    dve.wait_ge(ev["v_mv"], at("v_mv", c))
                    dve.tensor_scalar(v_mv[:, 1:2], v_mv[:, 1:2], 1e-5, None, ALU.add).then_inc(ev["v_ve"], 1)
                if piece == 2:
                    dve.wait_ge(ev["kk_sums"], at("kk_sums", c))
                    dve.tensor_scalar(kk_rn[:], psum[:, 6, 0:G], 1e-24, None, ALU.max).then_inc(ev["kk_clamped"], 1)
                    dve.wait_ge(ev["v_rs"], at("v_rs", c))
                    dve.tensor_scalar(vn[:], psum[:, 7, :], v_mv[:, 0:1], v_rs[:], ALU.subtract,
                                      ALU.mult).then_inc(ev["v_norm"], 1)
                if piece == 3:
                    dve.wait_ge(ev["kk_spread"], at("kk_spread", c))
                    dve.tensor_tensor(kkT[:], kkT[:], psum[:, 6, :].rearrange("p (k c) -> p k c", c=P),
                                      ALU.mult).then_inc(ev["kk_unit"], 1)
                    dve.wait_ge(ev["exps"], at("exps", c, 3))
                    dve.tensor_tensor(prT[par][:, :, 1, :], rz, e_in[:], ALU.mult).then_inc(ev["pr_ready"], 1)
                    dve.wait_ge(ev["kk_unit"], at("kk_unit", c))
                    dve.tensor_tensor(prT[par][:, :, 0, :], kkT[:], e_ex[:], ALU.mult).then_inc(ev["pr_ready"], 1)
                    dve.tensor_tensor(tmpT[:], kkT[:], aT[:], ALU.mult).then_inc(ev["kk_a"], 1)
                if piece == 4:
                    dve.wait_ge(ev["kk_a"], at("kk_a", c))
                    dve.wait_ge(ev["gram"], at("gram", c - 1))
                    dve.scalar_tensor_tensor(out=bT[:], in0=tmpT[:], scalar=-1.0, in1=e_neg[:],
                                             op0=ALU.mult, op1=ALU.mult).then_inc(ev["b_ready"], 1)
                    dve.wait_ge(ev["kp"], at("kp", c))
                    dve.tensor_tensor(kT[:], kpT[:], e_neg[:], ALU.mult).then_inc(ev["k_ready"], 1)
                    dve.wait_ge(ev["mixed"], at("mixed", c))
                    dve.tensor_tensor(mixed[:], bank7, b_s[:], ALU.add).then_inc(ev["mixed_b"], 1)
                    dve.wait_ge(ev["mixed_b"], at("mixed_b", c))
                    dve.tensor_tensor(y_out[:, KR:2 * KR, bass.ds(c * C, C)], mixed[:], gc[:, 0:KR, :],
                                      ALU.mult).then_inc(ev["sgu"], 1)
                if piece == 5:
                    dve.wait_ge(ev["bonus_raw"], at("bonus_raw", c))
                    dve.tensor_copy(bonus[:, par, :], psum[:, 6, 0:G]).then_inc(ev["bonus"], 1)

            def dve_rest(c, par, first, last):
                for n, (bank, dst) in enumerate(((1, b_nat), (3, v_nat))):
                    dve.wait_ge(ev["nat_turned"], at("nat_turned", c, bank + 1))
                    if n == 1:
                        dve.wait_ge(ev["bv"], at("bv", c - 1))
                    dve.tensor_copy(dst[:], psum[:, bank, :]).then_inc(ev["nat_dve"], 1)
                k = 0
                for q in range(4):
                    k += 1
                    dve.wait_ge(ev["gram"], at("gram", c, k))
                    dve.tensor_tensor(xq[:, 2 * q:2 * q + 2, :, :].rearrange("p h a c -> p h (a c)"),
                                      psum[:, 4 + q, :].rearrange("p (h c) -> p h c", h=2),
                                      band_incl.unsqueeze(1).to_broadcast([P, 2, 2 * C]),
                                      ALU.mult).then_inc(ev["gram_used"], 1)
                for q in range(2):
                    k += 1
                    dve.wait_ge(ev["gram"], at("gram", c, k))
                    dve.tensor_tensor(nT[:, 4 * q:4 * q + 4, :], psum[:, q, :].rearrange("p (h c) -> p h c", c=P),
                                      lower.unsqueeze(1).to_broadcast([P, 4, C]),
                                      ALU.mult).then_inc(ev["gram_used"], 1)
                for q in range(4):
                    k += 1
                    dve.wait_ge(ev["gram"], at("gram", c, k))
                    dve.tensor_tensor(mq[:, 2 * q:2 * q + 2, :, :].rearrange("p h a c -> p h (a c)"),
                                      psum[:, 2 + q, :].rearrange("p (h c) -> p h c", h=2),
                                      strict_incl.unsqueeze(1).to_broadcast([P, 2, 2 * C]),
                                      ALU.mult).then_inc(ev["gram_used"], 1)
                for lev in range(LEVELS):
                    for g in range(2):
                        n = 2 * lev + g
                        dve.wait_ge(ev["delta"], at("delta", c, n + 1))
                        dve.sem_inc(delta_seen, 1)
                        dve.copy_predicated(xq[:, 4 * g:4 * g + 4, 0, :],
                                            merge_masks[:, lev, :].unsqueeze(1).to_broadcast([P, 4, C]),
                                            psum[:, 2 * g + 1, :].rearrange("p (h c) -> p h c", c=P)
                                            ).then_inc(ev["x_upd"], 1)
                    if not last:
                        dve_front(lev, c + 1, 1 - par)
                dve.wait_ge(ev["gmk"], at("gmk", c))
                dve.tensor_copy(gv[:], psum[:, 1, :]).then_inc(ev["gmk_copied"], 1)
                if not last:
                    dve.wait_ge(ev["exps"], at("exps", c + 1))
                    dve.tensor_tensor(carry[:], e_end[:, par, :], e_mid[:, 1 - par, :],
                                      ALU.mult).then_inc(ev["carry"], 1)
                dve.wait_ge(ev["s_new"], at("s_new", c))
                dve.tensor_tensor(state_sum[:], state[:], psum[:, 2, 0:KR * HD].rearrange("p (k d) -> p k d", d=HD),
                                  ALU.add).then_inc(ev["s_sum"], 1)
                dve.wait_ge(ev["y_raw"], at("y_raw", c))
                if not last:
                    dve.wait_ge(ev["s_sum"], at("s_sum", c))
                    dve.wait_ge(ev["carry"], at("carry", c))
                    dve.tensor_tensor(state[:], state_sum[:], carry[:].unsqueeze(2).to_broadcast([P, KR, HD]),
                                      ALU.mult).then_inc(ev["state"], 1)
                y4 = psum[:, 0:2, 0:NB // 2].rearrange("p e (k d) -> p e k d", d=HD)
                dve.tensor_reduce(mean[:].rearrange("p (e k) -> p e k", e=2), y4, AX_X,
                                  ALU.add).then_inc(ev["mean"], 1)
                dve.wait_ge(ev["mean"], at("mean", c, 1))
                dve.tensor_scalar(mean[:], mean[:], 1.0 / HD, None, ALU.mult).then_inc(ev["mean"], 1)
                dve.wait_ge(ev["mean"], at("mean", c))
                if not first:
                    dve.wait_ge(ev["y_turned"], at("y_turned", c - 1))
                for e in range(2):
                    m = dve.tensor_tensor(yc[:].rearrange("p (k e d) -> p e k d", e=2, d=HD)[:, e],
                                          psum[:, e, 0:NB // 2].rearrange("p (k d) -> p k d", d=HD),
                                          mean[:, e * KR:(e + 1) * KR].unsqueeze(2).to_broadcast([P, KR, HD]),
                                          ALU.subtract)
                m.then_inc(ev["yc"], 1)
                dve.wait_ge(ev["ysq"], at("ysq", c))
                dve.tensor_reduce(var[:], ysq[:].rearrange("p (h d) -> p h d", d=HD), AX_X, ALU.add
                                  ).then_inc(ev["var"], 1)
                dve.wait_ge(ev["var"], at("var", c, 1))
                dve.tensor_scalar(var[:], var[:], 1.0 / HD, 64e-5, ALU.mult, ALU.add).then_inc(ev["var"], 1)

            def dve_mix():
                for piece in range(6):
                    dve_front(piece, 0, 0)
                dve.wait_ge(mix_made, 4)
                dve_rest(0, 0, True, False)
                with dve.Fori(0, CHUNKS // 2 - 1) as i:
                    for b in range(2):
                        dve_rest(i * 2 + (1 + b), 1 - b, False, False)
                dve_rest(CHUNKS - 1, 1, False, True)
                for h in range(HALVES):
                    for k in range(KD):
                        dve.wait_ge(y_high, h * KD + k + 1)
                        dve.tensor_tensor(aL[:, k, half(h)], y_out[:, k, half(h)],
                                          aH[:, k, half(h)].bitcast(F32), ALU.subtract).then_inc(y_split, 1)

            def add_w_out(st):
                def group(i, first, last):
                    for n, (j, h) in enumerate(items(last)):
                        dve.wait_ge(w_out_done, i * 4 + (n + 1))
                        if frees(n, last):
                            dve.sem_inc(w_free, frees(n, last))
                        hk = hT[:, bass.ds(i * 2 + j, 1), half(h)].rearrange("p a c -> p (a c)")
                        dve.tensor_tensor(hk, hk, psum[:, n, :], ALU.add).then_inc(w_out_added, 1)
                        dve.wait_ge(w_out_added, i * 4 + (n + 5))
                        sum_square("ffn2", i * 4 + (n + 1), hk, n, h, first and j == 0)
                        if last and n == 1:
                            for k in range(KD):
                                low("ffn2", 0, k)

                group(0, True, False)
                with dve.Fori(1, st.iters - 1) as i:
                    group(i, False, False)
                split_p()
                group(st.iters - 1, False, True)
                for k in range(KD):
                    low("ffn2", 1, k)

            dve.wait_ge(vecs_turned, 1)
            dve.tensor_copy(vecs[:], psum[:, 0, 0:n_rows]).then_inc(vecs_ready, 1)
            dve.wait_ge(vecs_ready, 1)
            for h in range(HALVES):
                place_x(h)
                dve.wait_ge(x_used_act, (h + 1) * (TT // 2))
                for k in range(KD):
                    low("ffn1", h, k)
            hidden_and_adds("ffn1", stages["ffn1"], "mix")
            scale_z(stages["w_in"])
            place_spatial()
            dve_mix()
            add_w_out(stages["w_out"])
            hidden_and_adds("ffn2", stages["ffn2"], "ple")
            gate_adds(stages["gate"])
            scale_result()


_INS = ['x', 'p', 'norm_ffn1', 'ffn1_w1', 'ffn1_w3', 'ffn1_w2', 'norm_mix', 'w_in', 'shift_mu',
        'rwkv_w0', 'rwkv_w_decay', 'rwkv_a0', 'rwkv_w_aaa', 'rwkv_w_gate', 'rwkv_k_k', 'rwkv_k_a',
        'rwkv_r_k', 'rwkv_gn_g', 'rwkv_gn_b', 'sgu_ln_g', 'sgu_ln_b', 'sgu_w_s', 'sgu_b_s', 'w_out',
        'norm_ffn2', 'ffn2_w1', 'ffn2_w3', 'ffn2_w2', 'norm_ple', 'w_ple_gate', 'w_ple', 'norm_final']


def shape_constants(P=128, levels=6):
    row, col = np.arange(P)[:, None], np.arange(P)[None, :]
    mid = row <= P // 2 - 1
    unit = -np.exp(np.float32(-0.5))
    incl, excl = (row <= col), (row < col)
    pairs = (row // 2 == col // 2) & excl
    head = np.stack([np.arange(P) < P // 2, np.arange(P) >= P // 2], axis=1)
    parts = [unit * (incl.astype(np.float32) - mid), unit * (excl.astype(np.float32) - mid),
             row > col, pairs, incl, excl, incl, head]
    for n in range(1, levels + 1):
        b = 2 ** n
        parts.append((row // (2 * b) == col // (2 * b)) & (row % (2 * b) < b) & (col % (2 * b) >= b))
    return np.ascontiguousarray(np.concatenate([a.astype(np.float32) for a in parts], axis=1))


def kernel(**inputs):
    import concourse.bacc as bacc
    from concourse.bass_utils import run_bass_kernel_spmd

    nc = bacc.Bacc("TRN2", target_bir_lowering=False, num_devices=1,
                   dynamic_dma_scratch_size=1024)
    arrays, io = {}, {}
    for name in _INS:
        a = np.ascontiguousarray(inputs[name])
        arrays[f"in_{name}"] = a
        io[name] = nc.dram_tensor(f"in_{name}", a.shape, mybir.dt.from_np(a.dtype), kind="ExternalInput").ap()
    arrays["in_masks"] = shape_constants()
    io["masks"] = nc.dram_tensor("in_masks", arrays["in_masks"].shape, F32, kind="ExternalInput").ap()
    out = nc.dram_tensor("out", inputs["x"].shape, F32, kind="ExternalOutput").ap()
    build(nc, io, out)
    return run_bass_kernel_spmd(nc, [arrays], core_ids=[0]).results[0]["out"]
```

```python
from contextlib import ExitStack

import numpy as np

import concourse.bass as bass
from concourse import mybir

F32 = mybir.dt.float32
F32R = mybir.dt.float32r
U32 = mybir.dt.uint32
ALU = mybir.AluOpType
ACT = mybir.ActivationFunctionType
AX_X = mybir.AxisListType.X

P = 128
NB = 512
RAW_SLOTS = 3
SPLIT_SLOTS = 6
UNIT = 1024
MIX_CONSTS = 12


class Stage:

    def __init__(self, name, iters, body, first_unit, ring, start, raw_ring, unit=UNIT):
        self.name, self.iters, self.body, self.first = name, iters, body, first_unit
        self.ring, self.start, self.raw_ring, self.unit = ring, start, raw_ring, unit
        self.end = first_unit + iters * body

    def raw_at(self, j):
        if self.raw_ring == RAW_SLOTS:
            return (j % RAW_SLOTS) * self.unit
        return RAW_SLOTS * UNIT - 2 * self.unit + (j % 2) * self.unit

    def split_at(self, j):
        if self.ring == SPLIT_SLOTS:
            return ((self.start + j) % SPLIT_SLOTS) * self.unit
        if self.ring == 4:
            return (self.start * UNIT + j * self.unit) if j < 3 else 0
        return self.start * UNIT + (j % 2) * self.unit


def build(nc, io, out):
    x, p = io["x"], io["p"]
    T, D = x.shape[1], x.shape[2]
    F = io["ffn1_w1"].shape[2]
    KD = D // P
    HALVES = T // NB
    TT = T // P
    FT = F // P
    PLE = p.shape[3]
    KP = PLE // P
    IN_COLS = io["w_in"].shape[2]
    assert D == UNIT and HALVES == 2 and FT % 2 == 0 and IN_COLS % (2 * P) == 0

    stages, unit = {}, 0
    for name, iters, body, ring, start, raw_ring, width in (
        ("ffn1", FT // 2, 6, SPLIT_SLOTS, 0, RAW_SLOTS, UNIT),
        ("w_in", IN_COLS // P // 2, 2, 2, 0, 2, UNIT),
        ("w_out", KD // 2, 2, 2, 0, 2, UNIT),
        ("ffn2", FT // 2, 6, SPLIT_SLOTS, 2, RAW_SLOTS, UNIT),
        ("gate", KD // 4, 4, 4, 2, 2, UNIT + KP * P),
    ):
        stages[name] = Stage(name, iters, body, unit, ring, start, raw_ring, width)
        unit = stages[name].end

    G = RWKV_HEADS = io["rwkv_r_k"].shape[1]
    HD = io["rwkv_r_k"].shape[2]
    RW = RWKV_HEADS * HD
    KR = RW // P
    C = P
    CHUNKS = T // C
    SHIFTED = io["shift_mu"].shape[1] // P
    ZT = IN_COLS // P
    LORA, GATE = SHIFTED - 2, SHIFTED - 1
    LEVELS = 6
    assert HD == 64 and RW == NB and io["sgu_w_s"].shape[1] == 8 and CHUNKS % 2 == 0

    with ExitStack() as ctx:
        def sb(name, shape, dt=F32, where=ctx):
            return where.enter_context(nc.sbuf_tensor(name, shape, dt))

        def sem(name):
            return ctx.enter_context(nc.semaphore(name))

        hT = sb("hT", [P, KD, T])
        aH_at = nc.sbuf_base
        aH = sb("aH", [P, KD, T], F32R)
        aL_at = nc.sbuf_base
        aL = sb("aL", [P, KD, T], F32R)
        wH_at = nc.sbuf_base
        wH = sb("wH", [P, SPLIT_SLOTS * UNIT], F32R)
        wL_at = nc.sbuf_base
        wL = sb("wL", [P, SPLIT_SLOTS * UNIT], F32R)
        raw_at = nc.sbuf_base
        raw = sb("raw", [P, RAW_SLOTS * UNIT])
        ident = sb("ident", [P, P])
        ones = sb("ones", [P, 1])
        NORMS = ("ffn1", "mix", "ffn2", "ple", "final")
        VECTORS = {}
        n_rows = 0
        for name in ("norm_ffn1", "norm_mix", "norm_ffn2", "norm_ple", "norm_final", "shift_mu",
                     "rwkv_a0", "rwkv_k_k", "rwkv_k_a", "rwkv_r_k"):
            VECTORS[name] = n_rows
            n_rows += int(np.prod(io[name].shape)) // P
        vec_rows = sb("vec_rows", [n_rows, P])
        vecs = sb("vecs", [P, n_rows])
        inv_width = sb("inv_width", [P, 1])
        zero = sb("zero", [P, 1])
        neg_half = sb("neg_half", [P, 1])
        rms_eps = sb("rms_eps", [P, 1])

        psum = ctx.enter_context(nc.psum_tensor("psum", [P, 8, NB], F32))

        sq_at = nc.sbuf_base
        sq = sb("sq", [P, 4, NB])
        sums = sb("sums", [P, 2, NB])
        rs = sb("rs", [P, 2, NB])
        rstd = sb("rstd", [P, TT])
        with ExitStack() as x_phase:
            xs = sb("xs", [P, TT, D], F32, x_phase)
        hid_at = nc.sbuf_base
        with ExitStack() as ffn_phase:
            hidH = sb("hidH", [P, 2, T], F32R, ffn_phase)
            hidL = sb("hidL", [P, 2, T], F32R, ffn_phase)
            silu = sb("silu", [P, 2, NB], F32, ffn_phase)
            hid = sb("hid", [P, 2, NB], F32, ffn_phase)
            p_at = nc.sbuf_base
        with ExitStack() as result_phase:
            outs = sb("outs", [P, 4, D], F32, result_phase)
        gain_rows = nc.alloc_sbuf_tensor_at("gain_rows", [P, D], F32, offset=p_at - 2 * NB * 4)
        pTH = nc.alloc_sbuf_tensor_at("pTH", [P, KP, T], F32R, offset=p_at)
        pTL = nc.alloc_sbuf_tensor_at("pTL", [P, KP, T], F32R, offset=p_at + KP * T * 4)
        p_rows = nc.alloc_sbuf_tensor_at("p_rows", [P, TT, PLE], F32, offset=hid_at)
        assert HALVES * NB == T

        spaces = [[hid_at, nc.sbuf_usable_end],
                  [wH_at + 2 * UNIT * 4, wH_at + 6 * UNIT * 4],
                  [wL_at + 2 * UNIT * 4, wL_at + 6 * UNIT * 4],
                  [sq_at, sq_at + 8 * NB * 4],
                  [aH_at, aH_at + KD * T * 4],
                  [raw_at, raw_at + UNIT * 4]]
        used = [(a + 31) // 32 * 32 for a, _ in spaces]
        placed = {}

        def over(name, shape, dt=F32, space=None):
            size = int(np.prod(shape[1:])) * (1 if dt == mybir.dt.uint8 else 4)
            size = (size + 31) // 32 * 32
            for n in (range(len(spaces)) if space is None else space):
                if used[n] + size <= spaces[n][1]:
                    at = used[n]
                    used[n] += size
                    placed[name] = at
                    return nc.alloc_sbuf_tensor_at(name, shape, dt, offset=at)
            raise AssertionError(f"no room for {name}: {[(b - u) for (a, b), u in zip(spaces, used)]}")

        def within(name, shape, other, offset):
            return nc.alloc_sbuf_tensor_at(name, shape, F32, offset=placed[other] + offset)

        CONST = (1, 2, 0)
        WORK = (4, 3, 2, 1, 5, 6, 0)
        LATE = (3, 2, 1, 5, 6, 0)
        zout = over("zout", [P, 2, T + 1], F32, (0,))
        shape_masks = over("shape_masks", [P, io["masks"].shape[1]], F32, CONST)
        w_lora = over("w_lora", [P, RW], F32, CONST)
        w_gate = over("w_gate", [P, RW], F32, CONST)
        w0_rows = over("w0_rows", [P, RW], F32, CONST)
        gn_g = over("gn_g", [P, RW], F32, CONST)
        gn_b = over("gn_b", [P, RW], F32, CONST)
        ln_g = over("ln_g", [P, NB], F32, CONST)
        ln_b = over("ln_b", [P, NB], F32, CONST)
        wsT = over("wsT", [P, 8, P], F32, CONST)
        b_s = over("b_s", [P, KR, P], F32, CONST)
        rk_heads = over("rk_heads", [P, KR, 2], F32, CONST)
        ka_rest = over("ka_rest", [P, KR], F32, CONST)
        ws_rows = over("ws_rows", [P, 8, P], F32, (0,))
        zs = over("zs", [P, SHIFTED, C], F32, (0,))
        spaces.append([used[0], spaces[0][1]])
        used.append(used[0])
        spaces[0][1] = placed["zs"]
        used[0] = placed["zout"]
        y_out = nc.alloc_sbuf_tensor_at("y_out", [P, KD, T], F32, offset=aL_at)

        EARLY = (2, 1, 5)
        zc = over("zc", [P, SHIFTED, C + 1], F32, (3,))
        gc = over("gc", [P, 2 * KR, C], F32, WORK)
        tanh_w = over("tanh_w", [P, C], F32, EARLY)
        sig_g = over("sig_g", [P, C], F32, EARLY)
        sig_w = over("sig_w", [P, RW], F32, WORK)
        e_in = over("e_in", [P, KR, C], F32, WORK)
        e_ex = over("e_ex", [P, KR, C], F32, WORK)
        e_neg = over("e_neg", [P, KR, C], F32, WORK)
        e_mid = over("e_mid", [P, 2, KR], F32, WORK)
        e_end = over("e_end", [P, 2, KR], F32, WORK)
        carry = over("carry", [P, KR], F32, WORK)
        aT = over("aT", [P, KR, C], F32, WORK)
        kkT = over("kkT", [P, KR, C], F32, WORK)
        tmpT = over("tmpT", [P, KR, C], F32, WORK)
        kpT = over("kpT", [P, KR, C], F32, WORK)
        rkT = over("rkT", [P, KR, C], F32, WORK)
        prT = [over(f"prT{b}", [P, KR, 2, C], F32, WORK) for b in range(2)]
        bT = over("bT", [P, KR, C], F32, WORK)
        kT = over("kT", [P, KR, C], F32, WORK)
        gv = over("gv", [P, RW], F32, WORK)
        b_nat = over("b_nat", [P, RW], F32, WORK)
        k_nat = over("k_nat", [P, RW], F32, WORK)
        v_nat = over("v_nat", [P, RW], F32, WORK)
        g_nat = [over(f"g_nat{b}", [P, RW], F32, LATE) for b in range(2)]
        bonus = over("bonus", [P, 2, G], F32, WORK)
        kk_rn = over("kk_rn", [P, G], F32, WORK)
        nT = over("nT", [P, G, C], F32, WORK)
        xq = over("xq", [P, G, 2, C], F32, WORK)
        mq = over("mq", [P, G, 2, C], F32, WORK)
        xT = over("xT", [P, G, C], F32, WORK)
        yb = over("yb", [P, G, C], F32, WORK)
        u_nat = within("u_nat", [P, RW], "yb", RW * 4)
        state = over("state", [P, KR, HD], F32, WORK)
        state_sum = over("state_sum", [P, KR, HD], F32, WORK)
        yc = over("yc", [P, RW], F32, LATE)
        ysq = over("ysq", [P, RW], F32, LATE)
        bv = over("bv", [P, RW], F32, LATE)
        mean = over("mean", [P, G], F32, LATE)
        var = over("var", [P, G], F32, LATE)
        v_stats = over("v_stats", [P, 6], F32, WORK)
        v_mv = over("v_mv", [P, 2], F32, WORK)
        v_rs = over("v_rs", [P, 1], F32, WORK)
        vn = over("vn", [P, NB], F32, WORK)
        mixed = over("mixed", [P, KR, C], F32, WORK)

        decay_sums = shape_masks[:, 0:2 * C]
        lower = shape_masks[:, 2 * C:3 * C]
        band_incl = shape_masks[:, 3 * C:5 * C]
        strict_incl = shape_masks[:, 5 * C:7 * C]
        head_cols = shape_masks[:, 7 * C:7 * C + 2]
        merge_masks = (shape_masks[:, 7 * C + 2:7 * C + 2 + LEVELS * P].bitcast(U32)
                       .rearrange("p (l c) -> p l c", c=P))

        raw_ready = {n: [sem(f"raw_ready_{n}{i}") for i in range(s.raw_ring)] for n, s in stages.items()}
        high_done = sem("high_done")
        w_split = sem("w_split")
        w_free = sem("w_free")

        const_ready = sem("const_ready")
        made = sem("made")
        x_ready = [sem(f"x_ready{i}") for i in range(TT // 2)]
        x_turned = sem("x_turned")
        vecs_turned = sem("vecs_turned")
        vecs_ready = sem("vecs_ready")
        x_used_act = sem("x_used_act")
        x_used_dve = sem("x_used_dve")
        tiles = HALVES * KD
        SUMMED_BY_POOL = ("ffn1", "mix", "ple")
        NORM_PER = dict(squared=tiles, summed=tiles, spread=HALVES, rooted=HALVES, inverted=HALVES,
                        high=tiles, ready=tiles)
        norm = {k: sem(f"norm_{k}") for k in NORM_PER}
        tile_squared = sem("tile_squared")
        tile_summed = sem("tile_summed")

        def in_tiles(name, count):
            return {"ffn1": 0, "ffn2": KD, "final": KD + tiles}[name] + count

        def in_norm(name, k, count):
            if k in ("squared", "summed"):
                return max(SUMMED_BY_POOL.index(name) * tiles - KD, 0) + count
            return NORMS.index(name) * NORM_PER[k] + count

        ffn = {}
        for n in ("ffn1", "ffn2"):
            ffn[n] = {k: sem(f"{n}_{k}") for k in
                      ("up", "scaled", "silued", "banks_free", "product", "high", "hid_ready", "down", "added")}
        pT = {k: sem(f"p_{k}") for k in ("loaded", "turned", "high", "ready")}
        gate = {k: sem(f"gate_{k}") for k in ("done", "scaled", "sigmoid", "product", "added")}
        gain_ready = sem("gain_ready")
        fin = {k: sem(f"result_{k}") for k in ("turned", "copied", "stored0", "stored1", "stored2", "stored3")}

        def gate_items(last):
            return [(j, h) for h in range(HALVES) for j in range(4)] if last else \
                   [(j, h) for j in range(4) for h in range(HALVES)]

        def items(last):
            return [(0, 0), (1, 0), (0, 1), (1, 1)] if last else [(0, 0), (0, 1), (1, 0), (1, 1)]

        def frees(m, last):
            return (1 if m >= 2 else 0) if last else m % 2

        win = {k: sem(f"w_in_{k}") for k in ("done", "copied")}
        z_stored = [sem("z_stored0"), sem("z_stored1")]
        mix_consts = sem("mix_consts")
        mix_made = sem("mix_made")
        ws_turned = sem("ws_turned")
        ws_placed = sem("ws_placed")
        y_high = sem("y_high")
        delta_seen = sem("delta_seen")
        y_split = sem("y_split")
        w_out_done = sem("w_out_done")
        w_out_added = sem("w_out_added")
        zout_free = sem("zout_free")
        z_scratch = nc.dram_tensor("z_scratch", (ZT * P, T + 1), F32, kind="Internal").ap()
        PER = dict(
            z_loaded=16, g_loaded=16, shifted=6, lora_in=2, w_raw=1, a_raw=1, g_raw=1, w_biased=1,
            w_sig=1, a_ready=1, g_ready=1, decays=1, exps=5, kk_raw=2, kk_sums=1, kk_clamped=1,
            kk_rn=1, kk_spread=1, kk_unit=1, pr_ready=2, kk_a=1, b_ready=1, kp=3, k_ready=1,
            rk=1, bonus_raw=1, bonus=1, gelu=1, v_turned=1, v_stats=1, v_mv=1, v_ve=1, v_rs=1,
            v_norm=1, v_affine=2, mixed=1, mixed_b=1, sgu=1,
            nat_turned=3, nat_copied=3, gram=10, gram_used=10, x_init=2,
            xt=12, xt_copied=12, y=12, y_copied=12, delta=12, x_upd=12, bv=1,
            gmk=1, gmk_copied=1, u=1, u_copied=1, s_new=1, y_raw=1,
            s_sum=1, carry=1, state=1, mean=2, yc=1, ysq=1, var=2, y_rs=1, y_fin=5,
            y_turned=1, y_placed=1)
        ev = {k: sem("c_" + k) for k in PER}

        def at(name, c, k=None):
            n = PER[name]
            return (c + 2) * n + (n if k is None else k)

        io_w = {"ffn1": ("ffn1_w1", "ffn1_w3", "ffn1_w2"), "ffn2": ("ffn2_w1", "ffn2_w3", "ffn2_w2")}

        def columns_of(w, m, k):
            return io[w][0].rearrange("(k p) c -> p k c", p=P)[:, :k, bass.ts(m, P)]

        def rows_of(w, m):
            return io[w][0][bass.ts(m, P), :]

        def store_result(engine, t):
            engine.wait_ge(fin["copied"], 2 * t + 2)
            engine.dma_start(out[0, t * P:(t + 1) * P, :], outs[:, t % 4, :]).then_inc(fin[f"stored{t % 4}"], 16)

        block = ctx.enter_context(nc.Block())

        @block.sync
        def _(sp):
            def tile_source(s, i, j):
                if s.name in io_w:
                    w1, w3, w2 = io_w[s.name]
                    m = i * 2 + (j // 2 if j < 4 else j - 4)
                    if j < 4:
                        return columns_of((w1, w3)[j % 2], m, KD)
                    return rows_of(w2, m)
                return columns_of({"w_in": "w_in", "w_out": "w_out", "gate": "w_ple_gate"}[s.name],
                                  i * s.body + j, KD)

            def load_u_and_v(c):
                sp.dma_start(gc[:], z_scratch[SHIFTED * P:ZT * P, bass.ds(c * C + 1, C)]
                             .rearrange("(k p) c -> p k c", p=P)).then_inc(ev["g_loaded"], 16)

            def load_chunk(c):
                sp.wait_ge(ev["shifted"], at("shifted", c - 1))
                sp.dma_start(zc[:], z_scratch[0:SHIFTED * P, bass.ds(c * C, C + 1)]
                             .rearrange("(k p) c -> p k c", p=P)).then_inc(ev["z_loaded"], 16)
                if isinstance(c, int):
                    for j in range(2):
                        sp.wait_ge(z_stored[j], 16 * (1 + ZT // 2))
                sp.wait_ge(ev["sgu"], at("sgu", c - 1))
                load_u_and_v(c)

            for s in stages.values():
                if s.name == "w_out":
                    for j in range(2):
                        sp.wait_ge(z_stored[j], 16 * (1 + SHIFTED // 2))
                    load_chunk(0)
                    with sp.Fori(1, CHUNKS) as c:
                        load_chunk(c)
                with sp.Fori(0, s.iters) as i:
                    for j in range(s.body):
                        u = i * s.body + (s.first + j)
                        sp.wait_ge(w_split, u + (1 + RAW_SLOTS - s.raw_ring))
                        slot = s.raw_at(j)
                        dst = raw[:, slot:slot + UNIT]
                        src = tile_source(s, i, j)
                        if len(src.shape) == 3:
                            dst = dst.rearrange("p (k c) -> p k c", c=P)
                        ready = raw_ready[s.name][j % s.raw_ring]
                        sp.dma_start(dst, src).then_inc(ready, 16)
                        if s.name == "gate":
                            sp.dma_start(
                                raw[:, slot + UNIT:slot + s.unit].rearrange("p (k c) -> p k c", c=P),
                                columns_of("w_ple", i * s.body + j, KP)).then_inc(ready, 16)
            for t in range(TT):
                store_result(sp, t)
            for t in range(4):
                sp.wait_ge(fin[f"stored{t}"], 16 * (TT // 4))

        @block.gpsimd
        def _(pool):
            pool.sem_inc(w_split, RAW_SLOTS)
            pool.memset(ident[:], 0.0).then_inc(made, 1)
            pool.memset(ones[:], 1.0).then_inc(made, 1)
            pool.memset(inv_width[:], 1.0 / D).then_inc(made, 1)
            pool.memset(zero[:], 0.0).then_inc(made, 1)
            pool.memset(neg_half[:], -0.5).then_inc(made, 1)
            pool.memset(rms_eps[:], 1e-6).then_inc(made, 1)
            pool.wait_ge(made, 6)
            pool.affine_select(out=ident[:], in_=ident[:], compare_op=ALU.not_equal, fill=1.0,
                               base=0, pattern=[[-1, P]], channel_multiplier=1).then_inc(made, 1)
            for k, n in PER.items():
                pool.sem_inc(ev[k], 2 * n)

            NORM_OF = {"ffn1": "ffn1", "w_in": "mix", "gate": "ple"}

            def norm_part(name):
                for h in range(HALVES):
                    for k in range(KD):
                        n = h * KD + k
                        if name == "ffn1" and h == 1:
                            continue
                        pool.wait_ge(norm["squared"], in_norm(name, "squared", n + 1))
                        if k == 0:
                            pool.tensor_copy(sums[:, h, :], sq[:, n % 4, :]).then_inc(norm["summed"], 1)
                        else:
                            pool.wait_ge(norm["summed"], in_norm(name, "summed", n))
                            pool.tensor_tensor(sums[:, h, :], sums[:, h, :], sq[:, n % 4, :],
                                               ALU.add).then_inc(norm["summed"], 1)
            def mix_constants():
                pool.wait_ge(ffn["ffn1"]["added"], 4 + stages["ffn1"].iters * 2 * KD)
                pool.memset(zout[:, :, 0:1], 0.0).then_inc(mix_made, 1)
                pool.wait_ge(mix_consts, 16 * MIX_CONSTS)
                rk = VECTORS["rwkv_r_k"]
                pool.tensor_tensor(rk_heads[:], vecs[:, rk:rk + KR].unsqueeze(2).to_broadcast([P, KR, 2]),
                                   head_cols.unsqueeze(1).to_broadcast([P, KR, 2]),
                                   ALU.mult).then_inc(mix_made, 1)
                ka = VECTORS["rwkv_k_a"]
                pool.tensor_tensor(ka_rest[:], ones[:].to_broadcast([P, KR]), vecs[:, ka:ka + KR],
                                   ALU.subtract).then_inc(mix_made, 1)

            def shift(c, tiles, k):
                n = tiles.stop - tiles.start
                mu0 = VECTORS["shift_mu"]
                mu = vecs[:, mu0 + tiles.start:mu0 + tiles.stop].unsqueeze(2).to_broadcast([P, n, C])
                pool.tensor_tensor(zs[:, tiles, :], zc[:, tiles, 0:C], zc[:, tiles, 1:C + 1],
                                   ALU.subtract).then_inc(ev["shifted"], 1)
                pool.wait_ge(ev["shifted"], at("shifted", c, k + 1))
                pool.tensor_tensor(zs[:, tiles, :], zs[:, tiles, :], mu, ALU.mult).then_inc(ev["shifted"], 1)
                pool.wait_ge(ev["shifted"], at("shifted", c, k + 2))
                pool.tensor_tensor(zs[:, tiles, :], zs[:, tiles, :], zc[:, tiles, 1:C + 1],
                                   ALU.add).then_inc(ev["shifted"], 1)

            def wide(name, k=KR):
                v = VECTORS[name]
                return vecs[:, v:v + k].unsqueeze(2).to_broadcast([P, k, C])

            def pool_lora(c):
                pool.wait_ge(ev["z_loaded"], at("z_loaded", c))
                pool.wait_ge(ev["a_raw"], at("a_raw", c - 1))
                shift(c, slice(LORA, SHIFTED), 0)

            def pool_v_rs(c):
                pool.wait_ge(ev["v_ve"], at("v_ve", c))
                pool.tensor_tensor(v_rs[:], v_mv[:, 1:2], neg_half[:], ALU.pow).then_inc(ev["v_rs"], 1)

            def pool_front(c, first=False):
                pool.wait_ge(ev["nat_turned"], at("nat_turned", c - 1))
                pool.wait_ge(ev["pr_ready"], at("pr_ready", c - 1))
                pool.wait_ge(ev["k_ready"], at("k_ready", c - 1))
                shift(c, slice(0, LORA), 3)
                pool.wait_ge(ev["shifted"], at("shifted", c))
                if first:
                    pool.wait_ge(win["copied"], 4 + 2 * ZT)
                pool.wait_ge(ev["kk_unit"], at("kk_unit", c - 1))
                pool.wait_ge(ev["b_ready"], at("b_ready", c - 1))
                kz, rz = zs[:, KR:2 * KR, :], zs[:, 0:KR, :]
                pool.tensor_tensor(kkT[:], kz, wide("rwkv_k_k"), ALU.mult).then_inc(ev["kk_raw"], 1)
                pool.wait_ge(ev["kk_raw"], at("kk_raw", c, 1))
                pool.tensor_tensor(tmpT[:], kkT[:], kkT[:], ALU.mult).then_inc(ev["kk_raw"], 1)
                if not first:
                    pool_v_rs(c)
                pool.wait_ge(ev["kk_clamped"], at("kk_clamped", c))
                pool.tensor_tensor(kk_rn[:], kk_rn[:], neg_half[:].to_broadcast([P, G]),
                                   ALU.pow).then_inc(ev["kk_rn"], 1)
                if first:
                    pool_v_rs(c)
                pool.wait_ge(ev["a_ready"], at("a_ready", c))
                pool.tensor_tensor(kpT[:], aT[:], wide("rwkv_k_a"), ALU.mult).then_inc(ev["kp"], 1)
                pool.wait_ge(ev["kp"], at("kp", c, 1))
                pool.tensor_tensor(kpT[:], kpT[:], ka_rest[:].unsqueeze(2).to_broadcast([P, KR, C]),
                                   ALU.add).then_inc(ev["kp"], 1)
                pool.wait_ge(ev["kp"], at("kp", c, 2))
                pool.tensor_tensor(kpT[:], kpT[:], kz, ALU.mult).then_inc(ev["kp"], 1)
                pool.wait_ge(ev["kp"], at("kp", c))
                pool.wait_ge(ev["bonus_raw"], at("bonus_raw", c - 1))
                pool.tensor_tensor(rkT[:], rz, kpT[:], ALU.mult).then_inc(ev["rk"], 1)
                pool.wait_ge(ev["v_norm"], at("v_norm", c))
                pool.tensor_tensor(vn[:], vn[:], ln_g[:], ALU.mult).then_inc(ev["v_affine"], 1)
                pool.wait_ge(ev["v_affine"], at("v_affine", c, 1))
                pool.tensor_tensor(vn[:], vn[:], ln_b[:], ALU.add).then_inc(ev["v_affine"], 1)

            def head_wide(x):
                return x.unsqueeze(2).to_broadcast([P, G, HD])

            def heads(x):
                return x.rearrange("p (h d) -> p h d", d=HD)

            def pool_tail(c, par):
                pool.wait_ge(ev["var"], at("var", c))
                pool.tensor_tensor(var[:], var[:], neg_half[:].to_broadcast([P, G]), ALU.pow).then_inc(ev["y_rs"], 1)
                pool.wait_ge(ev["y_rs"], at("y_rs", c))
                pool.tensor_tensor(heads(yc[:]), heads(yc[:]), head_wide(var[:]), ALU.mult).then_inc(ev["y_fin"], 1)
                for k, (op, other) in enumerate(((ALU.mult, gn_g), (ALU.add, gn_b), (ALU.add, bv),
                                                 (ALU.mult, g_nat[par]))):
                    pool.wait_ge(ev["y_fin"], at("y_fin", c, k + 1))
                    pool.tensor_tensor(yc[:], yc[:], other[:], op).then_inc(ev["y_fin"], 1)

            def pool_rest(c, par, first, last):
                if not last:
                    pool_lora(c + 1)
                for g in range(2):
                    pool.wait_ge(ev["gram_used"], at("gram_used", c, 2 * g + 2))
                    x = xq[:, 4 * g:4 * g + 4, 0, :]
                    pool.tensor_tensor(x, x, ident[:].unsqueeze(1).to_broadcast([P, 4, C]),
                                       ALU.add).then_inc(ev["x_init"], 1)
                if not first:
                    pool_tail(c - 1, 1 - par)
                pool.wait_ge(ev["bonus"], at("bonus", c))
                pool.wait_ge(ev["nat_copied"], at("nat_copied", c))
                if not first:
                    pool.wait_ge(ev["y_fin"], at("y_fin", c - 1))
                pool.tensor_tensor(heads(bv[:]), heads(v_nat[:]), head_wide(bonus[:, par, :]),
                                   ALU.mult).then_inc(ev["bv"], 1)
                if not last:
                    pool_front(c + 1)

            for s in stages.values():
                if s.name == "w_out":
                    pool_lora(0)
                    pool_front(0, True)
                    pool.wait_ge(ws_placed, 2)
                    pool.memset(state[:], 0.0).then_inc(mix_made, 1)
                    pool_rest(0, 0, True, False)
                    with pool.Fori(0, CHUNKS // 2 - 1) as i:
                        for b in range(2):
                            pool_rest(i * 2 + (1 + b), 1 - b, False, False)
                    pool_rest(CHUNKS - 1, 1, False, True)
                per = 2 if s.name == "gate" else 1

                def split_tile(i, j, freed):
                    u = i * s.body + (s.first + j)
                    turns = s.body // s.raw_ring
                    landed = (i * turns + (j // s.raw_ring + 1)) * (16 * per)
                    pool.wait_ge(raw_ready[s.name][j % s.raw_ring], landed)
                    pool.wait_ge(w_free, freed)
                    r, w = s.raw_at(j), s.split_at(j)
                    pool.tensor_tensor(wH[:, w:w + s.unit], raw[:, r:r + s.unit],
                                       zero[:].to_broadcast([P, s.unit]), ALU.add).then_inc(high_done, 1)
                    pool.wait_ge(high_done, u + 1)
                    pool.tensor_tensor(wL[:, w:w + s.unit], raw[:, r:r + s.unit],
                                       wH[:, w:w + s.unit].bitcast(F32),
                                       ALU.subtract).then_inc(w_split, 1)

                ahead = 4 if s.name == "ffn2" else 2
                for j in range(ahead):
                    u = s.first + j
                    split_tile(0, j, {"w_in": u + 1, "gate": s.first + 4}.get(
                        s.name, u + 1 + SPLIT_SLOTS - s.ring))
                if s.name == "w_out":
                    pool_tail(CHUNKS - 1, 1)
                if s.name in NORM_OF:
                    norm_part(NORM_OF[s.name])
                for j in range(ahead, s.body):
                    split_tile(0, j, s.first + {2: 4, 3: 6}[j] if s.name == "gate" else s.first + j + 1)
                if s.name == "w_in":
                    mix_constants()
                with pool.Fori(1, s.iters) as i:
                    for j in range(s.body):
                        split_tile(i, j, i * s.body + (s.first + j) + (1 + SPLIT_SLOTS - s.ring))

        @block.tensor
        def _(pe):
            pe.sem_inc(w_free, SPLIT_SLOTS)

            def products(acc, wat, actH, actL, first, last):
                pe.matmul(acc, wH[:, wat:wat + P], actH, start=first, stop=False)
                pe.matmul(acc, wH[:, wat:wat + P], actL, start=False, stop=False)
                return pe.matmul(acc, wL[:, wat:wat + P], actH, start=False, stop=last)

            def half(h):
                return slice(h * NB, (h + 1) * NB)

            def turn_vecs():
                pe.wait_ge(const_ready, 16 * len(VECTORS))
                pe.transpose(psum[:, 0, 0:n_rows], vec_rows[:], ident[0:n_rows, 0:n_rows]).then_inc(vecs_turned, 1)

            def turn_x(h):
                for t in range(h * (TT // 2), (h + 1) * (TT // 2)):
                    if t % 2 == 0:
                        pe.wait_ge(x_ready[t // 2], 16)
                    for q in range(2):
                        if t >= 2:
                            pe.wait_ge(x_used_dve if q == 0 else x_used_act, t - 1)
                        for k in range(4):
                            m = pe.transpose(psum[:, 4 + 2 * (t % 2) + q, k * P:(k + 1) * P],
                                             xs[:, t, (4 * q + k) * P:(4 * q + k + 1) * P], ident[:])
                        m.then_inc(x_turned, 1)

            def spread_sums(name, h):
                if name == "ffn1" and h == 0:
                    pe.wait_ge(x_used_dve, TT)
                    pe.wait_ge(x_used_act, TT)
                if name in ("mix", "ple"):
                    s = ffn["ffn1" if name == "mix" else "ffn2"]
                    pe.wait_ge(s["added"], 4 + FT // 2 * 2 * KD)
                if name == "ffn2":
                    pe.wait_ge(tile_summed, in_tiles(name, tiles))
                elif name == "ffn1" and h == 1:
                    pe.wait_ge(tile_summed, in_tiles(name, KD))
                else:
                    pe.wait_ge(norm["summed"], in_norm(name, "summed", (h + 1) * KD))
                pe.matmul(psum[:, 4 + h, :], inv_width[:].to_broadcast([P, P]), sums[:, h, :],
                          start=True, stop=True).then_inc(norm["spread"], 1)

            def ready(name, h, k):
                pe.wait_ge(norm["ready"], in_norm(name, "ready", h * KD + k + 1))

            def ffn_products(name, st):
                s = ffn[name]
                pe.sem_inc(s["banks_free"], 2)
                pe.sem_inc(s["added"], 4)

                def group(i, first):
                    for f in range(2):
                        for h in range(HALVES):
                            for w in range(2):
                                u = 2 * f + w
                                if h == 0:
                                    pe.wait_ge(w_split, i * 6 + (st.first + u + 1 + RAW_SLOTS))
                                bank = 2 * h + w
                                if w == 0:
                                    pe.wait_ge(s["banks_free"], i * 4 + (2 * f + h + 1))
                                for k in range(KD):
                                    if first and f == 0 and w == 0:
                                        ready(name, h, k)
                                    m = products(psum[:, bank, :], st.split_at(u) + k * P,
                                                 aH[:, k, half(h)], aL[:, k, half(h)],
                                                 k == 0, k == KD - 1)
                                if w == 1:
                                    m.then_inc(s["up"], 1)
                                elif first and name == "ffn1" and f == 0:
                                    if h == 0:
                                        turn_x(1)
                                    else:
                                        spread_sums(name, 0)
                            if first and f == 0 and name != "ffn1":
                                spread_sums(name, h)
                            if first and f == 0 and name == "ffn1" and h == 1:
                                spread_sums(name, 1)
                    for f in range(2):
                        pe.wait_ge(w_split, i * 6 + (st.first + 4 + f + 1 + RAW_SLOTS))
                    for h in range(HALVES):
                        pe.wait_ge(s["hid_ready"], i * 4 + (3 + h))
                        for d in range(KD):
                            bank = 4 + (h * KD + d) % 4
                            pe.wait_ge(s["added"], i * (2 * KD) + (h * KD + d + 1))
                            for f in range(2):
                                m = products(psum[:, bank, :], st.split_at(4 + f) + d * P,
                                             hidH[:, f, half(h)], hidL[:, f, half(h)],
                                             f == 0, f == 1)
                            m.then_inc(s["down"], 1)

                group(0, True)
                with pe.Fori(1, st.iters) as i:
                    group(i, False)

            def turn_p():
                pe.wait_ge(pT["loaded"], 16)
                for t in range(TT):
                    if t >= 2:
                        pe.wait_ge(pT["ready"], t - 1)
                    for k in range(KP):
                        m = pe.transpose(psum[:, 6 + t % 2, k * P:(k + 1) * P],
                                         p_rows[:, t, k * P:(k + 1) * P], ident[:])
                    m.then_inc(pT["turned"], 1)

            def gate_products(st):
                pe.sem_inc(gate["added"], 2)
                for i in range(st.iters):
                    first, last = i == 0, i == st.iters - 1
                    for m, (j, h) in enumerate(gate_items(last)):
                        pe.wait_ge(w_split, i * 4 + (st.first + j + 1 + RAW_SLOTS))
                        pe.wait_ge(gate["added"], i * 8 + (m + 1))
                        w = st.split_at(j)
                        for k in range(KD):
                            if first and j == 0:
                                ready("ple", h, k)
                            products(psum[:, 2 * (m % 2), :], w + k * P, aH[:, k, half(h)],
                                     aL[:, k, half(h)], k == 0, k == KD - 1)
                        for k in range(KP):
                            done = products(psum[:, 2 * (m % 2) + 1, :], w + UNIT + k * P,
                                            pTH[:, k, half(h)], pTL[:, k, half(h)],
                                            k == 0, k == KP - 1)
                        done.then_inc(gate["done"], 1)
                        if first and j == 0:
                            spread_sums("ple", h)
                        if last and m == 4:
                            result_sums(0)
                        if last and m >= 5:
                            turn_result(m - 5)

            def result_sums(h):
                pe.wait_ge(tile_summed, in_tiles("final", tiles - (4 if h == 0 else 0)))
                for t in range(TT // 2):
                    m = pe.matmul(psum[:, 4 if h == 0 else 0, t:t + 1], sums[:, h, t * P:(t + 1) * P],
                                  inv_width[:], start=True, stop=True)
                m.then_inc(norm["spread"], 1)

            def turn_result(t):
                pe.wait_ge(norm["rooted"], in_norm("final", "rooted", 1))
                for q in range(2):
                    bank = 4 + (2 * t + q) % 4
                    if t >= 2:
                        pe.wait_ge(fin["copied"], 2 * t + q - 3)
                    for k in range(4):
                        m = pe.transpose(psum[:, bank, k * P:(k + 1) * P],
                                         hT[:, 4 * q + k, t * P:(t + 1) * P], ident[:])
                    m.then_inc(fin["turned"], 1)

            def w_in_products(st):
                pe.sem_inc(win["copied"], 4)

                def group(i, first):
                    for j in range(2):
                        pe.wait_ge(w_split, i * 2 + (st.first + j + 1 + RAW_SLOTS))
                        for h in range(HALVES):
                            n = 2 * j + h
                            pe.wait_ge(win["copied"], i * 4 + (n + 1))
                            for k in range(KD):
                                if first and j == 0:
                                    ready("mix", h, k)
                                m = products(psum[:, n, :], st.split_at(j) + k * P, aH[:, k, half(h)],
                                             aL[:, k, half(h)], k == 0, k == KD - 1)
                            m.then_inc(win["done"], 1)
                            if first and j == 0:
                                spread_sums("mix", h)

                group(0, True)
                with pe.Fori(1, st.iters - 1) as i:
                    group(i, False)
                turn_spatial()
                group(st.iters - 1, False)

            def w_out_products(st):
                pe.sem_inc(w_out_added, 4)

                def group(i, first, last):
                    for n, (j, h) in enumerate(items(first or last)):
                        pe.wait_ge(w_split, i * 2 + (st.first + j + 1 + RAW_SLOTS))
                        pe.wait_ge(w_out_added, i * 4 + (n + 1))
                        for k in range(KD):
                            if first and j == 0:
                                pe.wait_ge(y_split, h * KD + k + 1)
                            m = products(psum[:, n, :], st.split_at(j) + k * P, aH[:, k, half(h)],
                                         aL[:, k, half(h)], k == 0, k == KD - 1)
                        m.then_inc(w_out_done, 1)
                        if first and n == 1:
                            pe_turn_y(CHUNKS - 1)

                group(0, True, False)
                with pe.Fori(1, st.iters - 1) as i:
                    group(i, False, False)
                turn_p()
                group(st.iters - 1, False, True)

            def turn_spatial():
                pe.wait_ge(mix_consts, 16 * MIX_CONSTS)
                for h in range(8):
                    m = pe.transpose(psum[:, 4 + h // 4, (h % 4) * P:(h % 4 + 1) * P], ws_rows[:, h, :], ident[:])
                    if h % 4 == 3:
                        m.then_inc(ws_turned, 1)

            def rows(h):
                return slice(HD * (h % 2), HD * (h % 2) + HD)

            def cols(h):
                return slice(HD * h, HD * h + HD)

            def head_at(slot):
                return 2 * (slot % 4) + slot // 4

            def mm(out, lhsT, rhs, start=True, stop=True):
                return pe.matmul(out, lhsT, rhs, start=start, stop=stop)

            def pe_front(piece, c, par, rwkv=True, sgu=True):
                if piece == 0 and rwkv:
                    pe.wait_ge(ev["lora_in"], at("lora_in", c, 1))
                    pe.wait_ge(ev["gram_used"], at("gram_used", c - 1, 9))
                    mm(psum[:, 4, :], tanh_w[0:64, :], w_lora[0:64, :]).then_inc(ev["w_raw"], 1)
                    pe.wait_ge(ev["gram_used"], at("gram_used", c - 1))
                    for k in range(KR):
                        m = mm(psum[:, 5, k * P:(k + 1) * P], w_lora[64:128, k * P:(k + 1) * P],
                               zs[64:128, LORA, :])
                    m.then_inc(ev["a_raw"], 1)
                    pe.wait_ge(ev["lora_in"], at("lora_in", c))
                    pe.wait_ge(ev["gmk_copied"], at("gmk_copied", c - 1))
                    mm(psum[:, 6, :], sig_g[:], w_gate[:]).then_inc(ev["g_raw"], 1)
                if piece == 1 and rwkv:
                    pe.wait_ge(ev["w_sig"], at("w_sig", c))
                    pe.wait_ge(ev["a_ready"], at("a_ready", c))
                    for k in range(KR):
                        m = mm(psum[:, 4 + k // 2, (k % 2) * 2 * C:(k % 2 + 1) * 2 * C],
                               sig_w[:, k * P:(k + 1) * P], decay_sums)
                    m.then_inc(ev["decays"], 1)
                if piece == 1 and sgu:
                    pe.wait_ge(ev["gelu"], at("gelu", c))
                    pe.wait_ge(ev["sgu"], at("sgu", c - 1))
                    pe.wait_ge(ev["gmk_copied"], at("gmk_copied", c - 1))
                    for k in range(KR):
                        m = pe.transpose(psum[:, 7, k * P:(k + 1) * P], gc[:, KR + k, :], ident[:])
                    m.then_inc(ev["v_turned"], 1)
                if piece == 2 and rwkv:
                    pe.wait_ge(ev["kk_raw"], at("kk_raw", c))
                    pe.wait_ge(ev["g_ready"], at("g_ready", c))
                    for k in range(KR):
                        m = mm(psum[:, 6, 2 * k:2 * k + 2], tmpT[:, k, :], head_cols)
                    m.then_inc(ev["kk_sums"], 1)
                if piece == 3 and rwkv:
                    pe.wait_ge(ev["kk_rn"], at("kk_rn", c))
                    for h in range(G):
                        m = mm(psum[rows(h), 6, (h // 2) * P:(h // 2 + 1) * P],
                               kk_rn[:, h:h + 1].to_broadcast([P, HD]), ident[:])
                    m.then_inc(ev["kk_spread"], 1)
                if piece == 4 and sgu:
                    pe.wait_ge(ev["v_affine"], at("v_affine", c))
                    for h in range(8):
                        m = mm(psum[rows(h), 7, (h // 2) * P:(h // 2 + 1) * P], vn[:, cols(h)], wsT[:, h, :])
                    m.then_inc(ev["mixed"], 1)
                if piece == 5 and rwkv:
                    pe.wait_ge(ev["rk"], at("rk", c))
                    pe.wait_ge(ev["kk_unit"], at("kk_unit", c))
                    for k in range(KR):
                        m = mm(psum[:, 6, 2 * k:2 * k + 2], rkT[:, k, :], rk_heads[:, k, :])
                    m.then_inc(ev["bonus_raw"], 1)

            def pe_turn_y(c):
                pe.wait_ge(ev["y_fin"], at("y_fin", c))
                for k in range(KR):
                    m = pe.transpose(psum[:, 4, k * P:(k + 1) * P], yc[:, k * P:(k + 1) * P], ident[:])
                m.then_inc(ev["y_turned"], 1)

            def pe_turn_x(c, n):
                g = n % 2
                for h in range(4):
                    m = pe.transpose(psum[:, 2 * g, h * P:(h + 1) * P], xq[:, 4 * g + h, 0, :], ident[:])
                m.then_inc(ev["xt"], 1)

            def pe_rest(c, par, first, last):
                pr = prT[par]
                if first:
                    turn_b_and_k(c)
                for k in range(KR):
                    m = pe.transpose(psum[:, 0, k * P:(k + 1) * P], zs[:, 2 * KR + k, :], ident[:])
                m.then_inc(ev["nat_turned"], 1)
                pe.wait_ge(ev["pr_ready"], at("pr_ready", c))
                for q, bank in enumerate((1, 2, 3, 0)):
                    if q >= 1:
                        pe.wait_ge(ev["nat_copied"], at("nat_copied", c, q))
                    for e in range(2):
                        h = head_at(2 * q + e)
                        m = mm(psum[:, bank, e * 2 * C:(e + 1) * 2 * C], bT[rows(h), h // 2, :],
                               pr[rows(h), h // 2, :, :].rearrange("p a c -> p (a c)"))
                    m.then_inc(ev["gram"], 1)
                pe.wait_ge(ev["bonus"], at("bonus", c))
                pe.wait_ge(ev["mixed_b"], at("mixed_b", c))
                pe.wait_ge(ev["s_sum"], at("s_sum", c - 1))
                for q in range(2):
                    for e in range(4):
                        h = head_at(4 * q + e)
                        m = mm(psum[:, 6 + q, e * P:(e + 1) * P], pr[rows(h), h // 2, 0, :], bT[rows(h), h // 2, :])
                    m.then_inc(ev["gram"], 1)
                pe.wait_ge(ev["exps"], at("exps", c))
                pe.wait_ge(ev["yc"], at("yc", c - 1))
                for q, bank in enumerate((4, 5, 3, 1)):
                    if q == 2:
                        pe.wait_ge(ev["gram_used"], at("gram_used", c, 3))
                    for e in range(2):
                        h = head_at(2 * q + e)
                        m = mm(psum[:, bank, e * 2 * C:(e + 1) * 2 * C], kT[rows(h), h // 2, :],
                               pr[rows(h), h // 2, :, :].rearrange("p a c -> p (a c)"))
                    m.then_inc(ev["gram"], 1)
                for g in range(2):
                    pe.wait_ge(ev["x_init"], at("x_init", c, g + 1))
                    pe.wait_ge(ev["gram_used"], at("gram_used", c, 4))
                    pe_turn_x(c, g)
                pe.wait_ge(ev["gram_used"], at("gram_used", c))
                pe.wait_ge(ev["state"], at("state", c - 1))
                for slot in range(G):
                    h = head_at(slot)
                    mm(psum[:, 6 + h % 2, cols(h // 2)], pr[rows(h), h // 2, 0, :], state[rows(h), h // 2, :],
                       slot % 4 == 0, False)
                for slot in range(G):
                    h = head_at(slot)
                    m = mm(psum[:, 6 + h % 2, cols(h // 2)], mq[:, slot, 0, :], v_nat[:, cols(h)],
                           False, slot % 4 == 3)
                m.then_inc(ev["gmk"], 1)
                for lev in range(LEVELS):
                    for g in range(2):
                        n = 2 * lev + g
                        pe.wait_ge(ev["xt_copied"], at("xt_copied", c, n + 1))
                        for e in range(4):
                            h = 4 * g + e
                            m = mm(psum[:, 2 * g, e * P:(e + 1) * P], nT[:, h, :], xq[:, h, 0, :])
                        m.then_inc(ev["y"], 1)
                    for g in range(2):
                        n = 2 * lev + g
                        pe.wait_ge(ev["y_copied"], at("y_copied", c, n + 1))
                        for e in range(4):
                            h = 4 * g + e
                            m = mm(psum[:, 2 * g + 1, e * P:(e + 1) * P], xT[:, h, :], yb[:, h, :])
                        m.then_inc(ev["delta"], 1)
                    if not last:
                        pe_front(lev, c + 1, 1 - par)
                    if lev == 4 and not first:
                        pe.wait_ge(ev["exps"], at("exps", c + (0 if last else 1)))
                        pe_turn_y(c - 1)
                    if lev == LEVELS - 1:
                        pe.wait_ge(ev["exps"], at("exps", c + (0 if last else 1)))
                        pe.wait_ge(ev["mixed_b"], at("mixed_b", c + (0 if last else 1)))
                        pe.wait_ge(ev["y_placed"], at("y_placed", c - 1))
                        pe_outputs_start(pr)
                    for g in range(2):
                        n = 2 * lev + g
                        pe.wait_ge(ev["x_upd"], at("x_upd", c, n + 1))
                        if lev < LEVELS - 1:
                            pe_turn_x(c, n)
                for slot in range(G):
                    h = head_at(slot)
                    m = mm(psum[:, h % 2, cols(h // 2)], xq[:, slot, 0, :], gv[:, cols(h)])
                m.then_inc(ev["u"], 1)
                if not last:
                    turn_b_and_k(c + 1)
                pe.wait_ge(ev["u_copied"], at("u_copied", c))
                for h in range(G):
                    m = mm(psum[rows(h), 7, (h // 2) * HD:(h // 2 + 1) * HD], b_nat[:, cols(h)], u_nat[:, cols(h)],
                           False, h >= G - 2)
                m.then_inc(ev["s_new"], 1)
                for slot in range(G):
                    h = head_at(slot)
                    m = mm(psum[:, 4 + h % 2, cols(h // 2)], xq[:, slot, 1, :], u_nat[:, cols(h)],
                           False, slot % 4 == 3)
                m.then_inc(ev["y_raw"], 1)

            def turn_b_and_k(c):
                pe.wait_ge(ev["b_ready"], at("b_ready", c))
                pe.wait_ge(ev["k_ready"], at("k_ready", c))
                for bank, src in ((2, bT), (3, kT)):
                    for k in range(KR):
                        m = pe.transpose(psum[:, bank, k * P:(k + 1) * P], src[:, k, :], ident[:])
                    m.then_inc(ev["nat_turned"], 1)

            def pe_outputs_start(pr):
                for slot in range(G):
                    h = head_at(slot)
                    mm(psum[:, 4 + h % 2, cols(h // 2)], pr[rows(h), h // 2, 1, :], state[rows(h), h // 2, :],
                       slot % 4 == 0, False)
                for slot in range(G):
                    h = head_at(slot)
                    mm(psum[:, 4 + h % 2, cols(h // 2)], mq[:, slot, 1, :], v_nat[:, cols(h)], False, False)
                for h in range(G):
                    mm(psum[rows(h), 7, (h // 2) * HD:(h // 2 + 1) * HD], k_nat[:, cols(h)], v_nat[:, cols(h)],
                       h < 2, False)

            def pe_mix():
                pe.wait_ge(ws_placed, 2)
                pe.wait_ge(mix_made, 3)
                for piece, rwkv in ((0, True), (1, True), (2, True), (1, False), (3, True), (5, True), (4, False)):
                    pe_front(piece, 0, 0, rwkv, not rwkv)
                pe.wait_ge(mix_made, 4)
                pe_rest(0, 0, True, False)
                with pe.Fori(0, CHUNKS // 2 - 1) as i:
                    for b in range(2):
                        pe_rest(i * 2 + (1 + b), 1 - b, False, False)
                pe_rest(CHUNKS - 1, 1, False, True)

            pe.wait_ge(made, 7)
            turn_x(0)
            turn_vecs()
            ffn_products("ffn1", stages["ffn1"])
            w_in_products(stages["w_in"])
            pe_mix()
            w_out_products(stages["w_out"])
            ffn_products("ffn2", stages["ffn2"])
            gate_products(stages["gate"])
            turn_result(3)
            result_sums(1)
            for t in range(4, TT):
                turn_result(t)

        @block.scalar
        def _(act):
            def half(h):
                return slice(h * NB, (h + 1) * NB)

            def load_x():
                def load_rows(c):
                    act.dma_start(xs[:, 2 * c:2 * c + 2, :],
                                  x[0, 2 * c * P:(2 * c + 2) * P, :].rearrange("(t q) c -> q t c", q=P)
                                  ).then_inc(x_ready[c], 16)

                load_rows(0)
                load_rows(1)
                for name, row in VECTORS.items():
                    v = io[name]
                    v = (v.rearrange("(k p) -> k p", p=P) if len(v.shape) == 1 else
                         v.rearrange("o (k p) -> (o k) p", p=P) if len(v.shape) == 2 else
                         v.rearrange("o (k a) c -> (o k) (a c)", a=2))
                    act.dma_start(vec_rows[row:row + v.shape[0], :], v).then_inc(const_ready, 16)
                load_rows(2)
                load_rows(3)

            def place_x(h):
                for t in range(h * (TT // 2), (h + 1) * (TT // 2)):
                    act.wait_ge(x_turned, 2 * t + 2)
                    act.activation(hT[:, 4:8, t * P:(t + 1) * P],
                                   psum[:, 4 + 2 * (t % 2) + 1, :].rearrange("p (k c) -> p k c", c=P),
                                   ACT.Copy).then_inc(x_used_act, 1)

            def high(name, gain, h, k):
                act.activation(aH[:, k, half(h)], hT[:, k, half(h)], ACT.Copy,
                               scale=vecs[:, gain + k:gain + k + 1]).then_inc(norm["high"], 1)

            def square(name, h, k):
                n = h * KD + k
                if n >= 4:
                    act.wait_ge(norm["summed"], in_norm(name, "summed", n - 3))
                act.activation(sq[:, n % 4, :], hT[:, k, half(h)], ACT.Square).then_inc(norm["squared"], 1)

            def highs(name, gain, h, final, squares=True):
                for k in range(KD):
                    final(h, k)
                    high(name, gain, h, k)
                    if squares:
                        square(name, h, k)

            def root(name, h):
                act.wait_ge(norm["spread"], in_norm(name, "spread", h + 1))
                act.activation(rs[:, h, :], psum[:, 4 + h, :], ACT.Sqrt, bias=rms_eps[:]).then_inc(norm["rooted"], 1)

            def hidden(name, st):
                s = ffn[name]

                def group(i, first):
                    for f in range(2):
                        for h in range(HALVES):
                            n = 2 * f + h
                            if first and f == 0:
                                root(name, h)
                            act.wait_ge(s["scaled"], i * 4 + (n + 1))
                            act.activation(silu[:, h, :], silu[:, h, :], ACT.Silu).then_inc(s["silued"], 1)
                            act.wait_ge(s["product"], i * 4 + (n + 1))
                            act.activation(hidH[:, f, half(h)], hid[:, h, :], ACT.Copy).then_inc(s["high"], 1)

                group(0, True)
                with act.Fori(1, st.iters) as i:
                    group(i, False)

            def after_adds(name, st):
                base = (st.iters - 1) * 2 * KD + 4
                return lambda h, k: act.wait_ge(ffn[name]["added"], base + h * KD + k + 1)

            def split_p():
                for t in range(TT):
                    act.wait_ge(pT["turned"], t + 1)
                    act.activation(pTH[:, :, t * P:(t + 1) * P],
                                   psum[:, 6 + t % 2, 0:PLE].rearrange("p (k c) -> p k c", c=P),
                                   ACT.Copy).then_inc(pT["high"], 1)

            def gate_sigmoid(st):
                act.wait_ge(ffn["ffn2"]["added"], 4 + st_ffn2.iters * 2 * KD)
                act.dma_start(gain_rows[:], io["norm_final"].unsqueeze(0).to_broadcast([P, D])
                              ).then_inc(gain_ready, 16)
                for i in range(st.iters):
                    for m in range(8):
                        if i == 0 and m < 2:
                            root("ple", m)
                        act.wait_ge(gate["scaled"], i * 8 + (m + 1))
                        act.activation(silu[:, m % 2, :], silu[:, m % 2, :],
                                       ACT.Sigmoid).then_inc(gate["sigmoid"], 1)
                        if i == st.iters - 1 and m == 4:
                            root_final(0)
                root_final(1)

            def root_final(h):
                act.wait_ge(norm["spread"], in_norm("final", "spread", h + 1))
                c = h * (TT // 2)
                act.activation(rstd[:, c:c + TT // 2], psum[:, 4 if h == 0 else 0, 0:TT // 2], ACT.Sqrt,
                               bias=rms_eps[:]).then_inc(norm["rooted"], 1)

            def load_mix_consts():
                act.wait_ge(ffn["ffn1"]["added"], 4 + stages["ffn1"].iters * 2 * KD)
                loads = [(shape_masks[:], io["masks"]),
                         (w_lora[0:64, :], io["rwkv_w_decay"][0]), (w_lora[64:128, :], io["rwkv_w_aaa"][0]),
                         (w_gate[:], io["rwkv_w_gate"][0]),
                         (ws_rows[:], io["sgu_w_s"][0].rearrange("h t s -> t h s"))]
                for dst, name in ((w0_rows, "rwkv_w0"), (gn_g, "rwkv_gn_g"), (gn_b, "rwkv_gn_b"),
                                  (ln_g, "sgu_ln_g"), (ln_b, "sgu_ln_b")):
                    loads.append((dst[:], io[name][0:1, :].to_broadcast([P, NB])))
                for e in range(2):
                    loads.append((b_s[64 * e:64 * e + 64, :, :],
                                  io["sgu_b_s"].rearrange("o (k a) t -> a o k t", a=2)[e]
                                  .to_broadcast([64, KR, P])))
                assert len(loads) == MIX_CONSTS
                for dst, src in loads:
                    act.dma_start(dst, src).then_inc(mix_consts, 16)

            def store_z(st):
                for j in range(2):
                    act.sem_inc(z_stored[j], 16)
                act.wait_ge(mix_made, 1)
                with act.Fori(0, st.iters) as i:
                    for j in range(2):
                        act.wait_ge(z_stored[j], i * 16 + 16)
                        act.sem_inc(zout_free, 1)
                        act.wait_ge(win["copied"], i * 4 + (4 + 2 * j + 2))
                        act.dma_start(z_scratch[bass.ds(i * 2 * P + j * P, P), :],
                                      zout[:, j, :]).then_inc(z_stored[j], 16)

            def act_inputs(c):
                act.wait_ge(ev["shifted"], at("shifted", c, 3))
                act.activation(tanh_w[0:64, :], zs[0:64, LORA, :], ACT.Tanh).then_inc(ev["lora_in"], 1)
                act.activation(sig_g[:], zs[:, GATE, :], ACT.Sigmoid).then_inc(ev["lora_in"], 1)

            def act_gelu(c):
                act.wait_ge(ev["g_loaded"], at("g_loaded", c))
                act.activation(gc[:], gc[:], ACT.Gelu).then_inc(ev["gelu"], 1)

            def act_front(piece, c, par):
                if piece == 0:
                    act.wait_ge(ev["a_raw"], at("a_raw", c))
                    a0 = VECTORS["rwkv_a0"]
                    act.wait_ge(ev["kp"], at("kp", c - 1))
                    act.wait_ge(ev["kk_a"], at("kk_a", c - 1))
                    for k in range(KR):
                        m = act.activation(aT[:, k, :], psum[:, 5, k * P:(k + 1) * P], ACT.Sigmoid,
                                           bias=vecs[:, a0 + k:a0 + k + 1])
                    m.then_inc(ev["a_ready"], 1)
                    act.wait_ge(ev["w_biased"], at("w_biased", c))
                    act.activation(sig_w[:], sig_w[:], ACT.Sigmoid).then_inc(ev["w_sig"], 1)
                if piece == 1:
                    act.wait_ge(ev["g_raw"], at("g_raw", c))
                    act.wait_ge(ev["y_fin"], at("y_fin", c - 2))
                    act.activation(g_nat[par][:], psum[:, 6, :], ACT.Copy).then_inc(ev["g_ready"], 1)
                if piece == 2:
                    act.wait_ge(ev["decays"], at("decays", c))
                    act.wait_ge(ev["pr_ready"], at("pr_ready", c - 1))
                    act.wait_ge(ev["b_ready"], at("b_ready", c - 1))
                    act.wait_ge(ev["k_ready"], at("k_ready", c - 1))
                    sums = psum[:, 4:6, :].rearrange("p b (k w t) -> p b k w t", w=2, t=C)
                    incl, excl = sums[:, :, :, 0, :], sums[:, :, :, 1, :]

                    def tiles(x):
                        return x.rearrange("p (b k) c -> p b k c", k=2)
                    act.activation(tiles(e_in[:]), incl, ACT.Exp).then_inc(ev["exps"], 1)
                    act.activation(tiles(e_ex[:]), excl, ACT.Exp).then_inc(ev["exps"], 1)
                    act.activation(tiles(e_neg[:]), incl, ACT.Exp, scale=-1.0).then_inc(ev["exps"], 1)
                    act.activation(e_mid[:, par, :].rearrange("p (b k) -> p b k", k=2),
                                   excl[:, :, :, 0], ACT.Exp, scale=-1.0).then_inc(ev["exps"], 1)
                    act.activation(e_end[:, par, :].rearrange("p (b k) -> p b k", k=2),
                                   incl[:, :, :, C - 1], ACT.Exp).then_inc(ev["exps"], 1)

            def by_parity(x):
                return x.rearrange("p (k e d) -> p e k d", e=2, d=HD)

            def parities(bank):
                return psum[:, bank:bank + 2, 0:NB // 2].rearrange("p e (k d) -> p e k d", d=HD)

            def act_place_y(c):
                act.wait_ge(ev["y_turned"], at("y_turned", c))
                act.activation(y_out[:, 0:KR, bass.ds(c * C, C)],
                               psum[:, 4, :].rearrange("p (k c) -> p k c", c=P),
                               ACT.Copy).then_inc(ev["y_placed"], 1)

            def act_copy_xt(c, n):
                g = n % 2
                act.wait_ge(ev["xt"], at("xt", c, n + 1))
                act.activation(xT[:, 4 * g:4 * g + 4, :], psum[:, 2 * g, :].rearrange("p (h c) -> p h c", c=P),
                               ACT.Copy).then_inc(ev["xt_copied"], 1)

            def act_copy_nat(c):
                for n, (bank, dst) in enumerate(((2, b_nat), (3, k_nat), (0, v_nat))):
                    act.wait_ge(ev["nat_turned"], at("nat_turned", c, n + 1))
                    if n == 0:
                        act.wait_ge(ev["s_new"], at("s_new", c - 1))
                    if n == 2:
                        act.wait_ge(ev["y_raw"], at("y_raw", c - 1))
                        act.wait_ge(ev["bv"], at("bv", c - 1))
                    act.activation(dst[:], psum[:, bank, :], ACT.Copy).then_inc(ev["nat_copied"], 1)

            def act_rest(c, par, first, last):
                if first:
                    act_copy_nat(c)
                if not last:
                    act_gelu(c + 1)
                    act_inputs(c + 1)
                for g in range(2):
                    act_copy_xt(c, g)
                act.wait_ge(ev["gmk"], at("gmk", c))
                act.activation(by_parity(gv[:]), parities(6), ACT.Copy).then_inc(ev["gmk_copied"], 1)
                for lev in range(LEVELS):
                    for g in range(2):
                        n = 2 * lev + g
                        act.wait_ge(ev["y"], at("y", c, n + 1))
                        act.activation(yb[:, 4 * g:4 * g + 4, :],
                                       psum[:, 2 * g, :].rearrange("p (h c) -> p h c", c=P),
                                       ACT.Copy).then_inc(ev["y_copied"], 1)
                    if not last and lev > 0:
                        act_front(lev, c + 1, 1 - par)
                    if lev == 4 and not first:
                        act_place_y(c - 1)
                    if lev < LEVELS - 1:
                        for g in range(2):
                            act_copy_xt(c, 2 * lev + 2 + g)
                    if not last and lev == 0:
                        act_front(lev, c + 1, 1 - par)
                act.wait_ge(ev["u"], at("u", c))
                act.activation(by_parity(u_nat[:]), parities(0), ACT.Copy).then_inc(ev["u_copied"], 1)
                if not last:
                    act_copy_nat(c + 1)
                act.wait_ge(ev["yc"], at("yc", c))
                act.activation(ysq[:], yc[:], ACT.Square).then_inc(ev["ysq"], 1)

            def act_mix():
                act_inputs(0)
                for piece in range(6):
                    act_front(piece, 0, 0)
                    if piece == 1:
                        act_gelu(0)
                act_rest(0, 0, True, False)
                with act.Fori(0, CHUNKS // 2 - 1) as i:
                    for b in range(2):
                        act_rest(i * 2 + (1 + b), 1 - b, False, False)
                act_rest(CHUNKS - 1, 1, False, True)
                act.wait_ge(ev["y_placed"], at("y_placed", CHUNKS - 2))
                act.wait_ge(ev["sgu"], at("sgu", CHUNKS - 1))
                act.wait_ge(ev["y_raw"], at("y_raw", CHUNKS - 1))
                for h in range(HALVES):
                    if h == 1:
                        act_place_y(CHUNKS - 1)
                        act.wait_ge(ev["y_placed"], at("y_placed", CHUNKS - 1))
                    for k in range(KD):
                        act.activation(aH[:, k, half(h)], y_out[:, k, half(h)], ACT.Copy).then_inc(y_high, 1)

            load_x()
            act.wait_ge(made, 7)
            g = VECTORS["norm_ffn1"]
            for h in range(HALVES):
                place_x(h)
                if h == 0:
                    act.wait_ge(vecs_ready, 1)
                act.wait_ge(x_used_dve, (h + 1) * (TT // 2))
                act.wait_ge(x_used_act, (h + 1) * (TT // 2))
                if h == 1:
                    for k in range(KD // 2, KD):
                        square("ffn1", 0, k)
                for k in range(KD):
                    high("ffn1", g, h, k)
                if h == 0:
                    for k in range(KD // 2):
                        square("ffn1", 0, k)
            hidden("ffn1", stages["ffn1"])
            for h in range(HALVES):
                highs("mix", VECTORS["norm_mix"], h, after_adds("ffn1", stages["ffn1"]))
            load_mix_consts()
            for h in range(HALVES):
                root("mix", h)
            store_z(stages["w_in"])
            act_mix()
            act.dma_start(p_rows[:], p[0, 0].rearrange("(t q) c -> q t c", q=P)).then_inc(pT["loaded"], 16)
            split_p()
            n = 4 * (stages["w_out"].iters - 1) + 4
            for h in range(HALVES):
                highs("ffn2", VECTORS["norm_ffn2"], h,
                      lambda h, k: k == 0 and act.wait_ge(w_out_added, n + 2 * h + 2), squares=False)
            hidden("ffn2", stages["ffn2"])
            st_ffn2 = stages["ffn2"]
            for h in range(HALVES):
                highs("ple", VECTORS["norm_ple"], h, after_adds("ffn2", st_ffn2))
            gate_sigmoid(stages["gate"])

        @block.vector
        def _(dve):
            def half(h):
                return slice(h * NB, (h + 1) * NB)

            def place_x(h):
                for t in range(h * (TT // 2), (h + 1) * (TT // 2)):
                    dve.wait_ge(x_turned, 2 * t + 1)
                    dve.tensor_copy(hT[:, 0:4, t * P:(t + 1) * P],
                                    psum[:, 4 + 2 * (t % 2), :].rearrange("p (k c) -> p k c", c=P)
                                    ).then_inc(x_used_dve, 1)

            def low(name, h, k):
                gain = VECTORS["norm_" + name] + k
                dve.wait_ge(norm["high"], in_norm(name, "high", h * KD + k + 1))
                dve.scalar_tensor_tensor(out=aL[:, k, half(h)], in0=hT[:, k, half(h)],
                                         scalar=vecs[:, gain:gain + 1], in1=aH[:, k, half(h)].bitcast(F32),
                                         op0=ALU.mult, op1=ALU.subtract).then_inc(norm["ready"], 1)

            def sum_square(name, n, hk, slot, h, first, sq=sq):
                if first:
                    dve.sem_inc(tile_squared, 1)
                    dve.tensor_tensor(sums[:, h, :], hk, hk, ALU.mult).then_inc(tile_summed, 1)
                    return
                dve.tensor_tensor(sq[:, slot, :], hk, hk, ALU.mult).then_inc(tile_squared, 1)
                dve.wait_ge(tile_squared, n + in_tiles(name, 0))
                dve.wait_ge(tile_summed, n + in_tiles(name, -1))
                dve.tensor_tensor(sums[:, h, :], sums[:, h, :], sq[:, slot, :], ALU.add).then_inc(tile_summed, 1)

            def invert(name, h):
                dve.wait_ge(norm["rooted"], in_norm(name, "rooted", h + 1))
                dve.reciprocal(rs[:, h, :], rs[:, h, :]).then_inc(norm["inverted"], 1)
                dve.wait_ge(norm["inverted"], in_norm(name, "inverted", h + 1))

            def hidden_and_adds(name, st, next_norm):
                s = ffn[name]

                def group(i, first, last):
                    for f in range(2):
                        for h in range(HALVES):
                            n = 2 * f + h
                            dve.wait_ge(s["up"], i * 4 + (n + 1))
                            if first and f == 0:
                                invert(name, h)
                            dve.tensor_tensor(silu[:, h, :], psum[:, 2 * h, :], rs[:, h, :],
                                              ALU.mult).then_inc(s["scaled"], 1)
                            if h == 1:
                                dve.sem_inc(w_free, 2)
                            dve.tensor_tensor(hid[:, h, :], psum[:, 2 * h + 1, :], rs[:, h, :],
                                              ALU.mult).then_inc(s["banks_free"], 1)
                            dve.wait_ge(s["banks_free"], i * 4 + (n + 3))
                            dve.wait_ge(s["silued"], i * 4 + (n + 1))
                            dve.tensor_tensor(hid[:, h, :], silu[:, h, :], hid[:, h, :],
                                              ALU.mult).then_inc(s["product"], 1)
                            dve.wait_ge(s["high"], i * 4 + (n + 1))
                            dve.tensor_tensor(hidL[:, f, half(h)], hid[:, h, :],
                                              hidH[:, f, half(h)].bitcast(F32),
                                              ALU.subtract).then_inc(s["hid_ready"], 1)
                    for h in range(HALVES):
                        for d in range(KD):
                            n = h * KD + d
                            dve.wait_ge(s["down"], i * (2 * KD) + (n + 1))
                            if n == 2 * KD - 1:
                                dve.sem_inc(w_free, 2)
                            dve.wait_ge(s["added"], i * (2 * KD) + (n + 1))
                            dve.scalar_tensor_tensor(out=hT[:, d, half(h)], in0=psum[:, 4 + n % 4, :],
                                                     scalar=0.5, in1=hT[:, d, half(h)],
                                                     op0=ALU.mult, op1=ALU.add).then_inc(s["added"], 1)
                            if last and n >= 1:
                                low(next_norm, (n - 1) // KD, (n - 1) % KD)
                    if last:
                        low(next_norm, 1, KD - 1)

                group(0, True, False)
                with dve.Fori(1, st.iters - 1) as i:
                    group(i, False, False)
                group(st.iters - 1, False, True)

            def scale_z(st):
                def group(i, first):
                    for j in range(2):
                        dve.wait_ge(zout_free, i * 2 + (j + 1))
                        for h in range(HALVES):
                            n = 2 * j + h
                            dve.wait_ge(win["done"], i * 4 + (n + 1))
                            if h == 1:
                                dve.sem_inc(w_free, 1)
                            if first and j == 0:
                                invert("mix", h)
                            dve.tensor_tensor(zout[:, j, 1 + h * NB:1 + (h + 1) * NB], psum[:, n, :],
                                              rs[:, h, :], ALU.mult).then_inc(win["copied"], 1)

                group(0, True)
                with dve.Fori(1, st.iters - 1) as i:
                    group(i, False)
                place_spatial()
                group(st.iters - 1, False)

            def split_p():
                for t in range(TT):
                    dve.wait_ge(pT["high"], t + 1)
                    dve.tensor_tensor(pTL[:, :, t * P:(t + 1) * P],
                                      psum[:, 6 + t % 2, 0:PLE].rearrange("p (k c) -> p k c", c=P),
                                      pTH[:, :, t * P:(t + 1) * P].bitcast(F32), ALU.subtract).then_inc(pT["ready"], 1)

            def gate_adds(st):
                for i in range(st.iters):
                    first, last = i == 0, i == st.iters - 1
                    for m, (j, h) in enumerate(gate_items(last)):
                        s = silu[:, m % 2, :]
                        dve.wait_ge(gate["done"], i * 8 + (m + 1))
                        if first and h == 1:
                            dve.sem_inc(w_free, 1)
                        if first and j == 0:
                            invert("ple", h)
                        dve.tensor_tensor(s, psum[:, 2 * (m % 2), :], rs[:, h, :],
                                          ALU.mult).then_inc(gate["scaled"], 1)
                        dve.wait_ge(gate["sigmoid"], i * 8 + (m + 1))
                        dve.tensor_tensor(s, s, psum[:, 2 * (m % 2) + 1, :], ALU.mult).then_inc(gate["product"], 1)
                        dve.wait_ge(gate["product"], i * 8 + (m + 1))
                        hk = hT[:, i * 4 + j, half(h)]
                        dve.tensor_tensor(hk, hk, s, ALU.add).then_inc(gate["added"], 1)
                        dve.wait_ge(gate["added"], i * 8 + (m + 3))
                        sum_square("final", i * 8 + (m + 1), hk, m % 4, h, first and j == 0)
                        if last and m >= 5:
                            scale_result(m - 5)

            def scale_result(t):
                if t == 0:
                    dve.wait_ge(gain_ready, 16)
                if t % (TT // 2) == 0:
                    n = 1 + t // (TT // 2)
                    dve.wait_ge(norm["rooted"], in_norm("final", "rooted", n))
                    dve.reciprocal(rstd[:, t:t + TT // 2], rstd[:, t:t + TT // 2]).then_inc(norm["inverted"], 1)
                    dve.wait_ge(norm["inverted"], in_norm("final", "inverted", n))
                if t >= 4:
                    dve.wait_ge(fin[f"stored{t % 4}"], 16 * (t // 4))
                for q in range(2):
                    dve.wait_ge(fin["turned"], 2 * t + q + 1)
                    dve.scalar_tensor_tensor(out=outs[:, t % 4, q * NB:(q + 1) * NB],
                                             in0=psum[:, 4 + (2 * t + q) % 4, :], scalar=rstd[:, t:t + 1],
                                             in1=gain_rows[:, q * NB:(q + 1) * NB],
                                             op0=ALU.mult, op1=ALU.mult).then_inc(fin["copied"], 1)

            def place_spatial():
                for g in range(2):
                    dve.wait_ge(ws_turned, g + 1)
                    dve.tensor_tensor(wsT[:, 4 * g:4 * g + 4, :],
                                      psum[:, 4 + g, :].rearrange("p (h c) -> p h c", c=P),
                                      strict_incl[:, C:2 * C].unsqueeze(1).to_broadcast([P, 4, C]),
                                      ALU.mult).then_inc(ws_placed, 1)

            def dve_front(piece, c, par, rwkv=True, sgu=True):
                kz, rz = zs[:, KR:2 * KR, :], zs[:, 0:KR, :]
                bank7 = psum[:, 7, :].rearrange("p (k c) -> p k c", c=P)
                if piece == 0 and rwkv:
                    dve.wait_ge(ev["w_raw"], at("w_raw", c))
                    dve.wait_ge(ev["decays"], at("decays", c - 1))
                    dve.tensor_tensor(sig_w[:], psum[:, 4, :], w0_rows[:], ALU.add).then_inc(ev["w_biased"], 1)
                if piece == 1 and sgu:
                    dve.wait_ge(ev["v_turned"], at("v_turned", c))
                    dve.bn_stats(v_stats[:], psum[:, 7, :]).then_inc(ev["v_stats"], 1)
                    dve.wait_ge(mix_consts, 16 * MIX_CONSTS)
                    dve.wait_ge(ev["v_stats"], at("v_stats", c))
                    dve.bn_aggr(v_mv[:], v_stats[:]).then_inc(ev["v_mv"], 1)
                    dve.wait_ge(ev["v_mv"], at("v_mv", c))
                    dve.tensor_scalar(v_mv[:, 1:2], v_mv[:, 1:2], 1e-5, None, ALU.add).then_inc(ev["v_ve"], 1)
                if piece == 2 and rwkv:
                    dve.wait_ge(ev["kk_sums"], at("kk_sums", c))
                    dve.tensor_scalar(kk_rn[:], psum[:, 6, 0:G], 1e-24, None, ALU.max).then_inc(ev["kk_clamped"], 1)
                if piece == 2 and sgu:
                    dve.wait_ge(ev["v_rs"], at("v_rs", c))
                    dve.tensor_scalar(vn[:], psum[:, 7, :], v_mv[:, 0:1], v_rs[:], ALU.subtract,
                                      ALU.mult).then_inc(ev["v_norm"], 1)
                if piece == 3 and rwkv:
                    dve.wait_ge(ev["kk_spread"], at("kk_spread", c))
                    dve.tensor_tensor(kkT[:], kkT[:], psum[:, 6, :].rearrange("p (k c) -> p k c", c=P),
                                      ALU.mult).then_inc(ev["kk_unit"], 1)
                    dve.wait_ge(ev["exps"], at("exps", c, 3))
                    dve.tensor_tensor(prT[par][:, :, 1, :], rz, e_in[:], ALU.mult).then_inc(ev["pr_ready"], 1)
                    dve.wait_ge(ev["kk_unit"], at("kk_unit", c))
                    dve.tensor_tensor(prT[par][:, :, 0, :], kkT[:], e_ex[:], ALU.mult).then_inc(ev["pr_ready"], 1)
                    dve.tensor_tensor(tmpT[:], kkT[:], aT[:], ALU.mult).then_inc(ev["kk_a"], 1)
                if piece == 4 and rwkv:
                    dve.wait_ge(ev["kk_a"], at("kk_a", c))
                    dve.wait_ge(ev["gram"], at("gram", c - 1))
                    dve.scalar_tensor_tensor(out=bT[:], in0=tmpT[:], scalar=-1.0, in1=e_neg[:],
                                             op0=ALU.mult, op1=ALU.mult).then_inc(ev["b_ready"], 1)
                    dve.wait_ge(ev["kp"], at("kp", c))
                    dve.tensor_tensor(kT[:], kpT[:], e_neg[:], ALU.mult).then_inc(ev["k_ready"], 1)
                if piece == 4 and sgu:
                    dve.wait_ge(ev["mixed"], at("mixed", c))
                    dve.tensor_tensor(mixed[:], bank7, b_s[:], ALU.add).then_inc(ev["mixed_b"], 1)
                    dve.wait_ge(ev["mixed_b"], at("mixed_b", c))
                    dve.tensor_tensor(y_out[:, KR:2 * KR, bass.ds(c * C, C)], mixed[:], gc[:, 0:KR, :],
                                      ALU.mult).then_inc(ev["sgu"], 1)
                if piece == 5 and rwkv:
                    dve.wait_ge(ev["bonus_raw"], at("bonus_raw", c))
                    dve.tensor_copy(bonus[:, par, :], psum[:, 6, 0:G]).then_inc(ev["bonus"], 1)

            def dve_rest(c, par, first, last):
                k = 0
                for q, bank in enumerate((1, 2, 3, 0)):
                    k += 1
                    dve.wait_ge(ev["gram"], at("gram", c, k))
                    dve.tensor_tensor(xq[:, 2 * q:2 * q + 2, :, :].rearrange("p h a c -> p h (a c)"),
                                      psum[:, bank, :].rearrange("p (h c) -> p h c", h=2),
                                      band_incl.unsqueeze(1).to_broadcast([P, 2, 2 * C]),
                                      ALU.mult).then_inc(ev["gram_used"], 1)
                if not first:
                    dve_variance(c - 1)
                for q in range(2):
                    k += 1
                    dve.wait_ge(ev["gram"], at("gram", c, k))
                    dve.tensor_tensor(nT[:, 4 * q:4 * q + 4, :], psum[:, 6 + q, :].rearrange("p (h c) -> p h c", c=P),
                                      lower.unsqueeze(1).to_broadcast([P, 4, C]),
                                      ALU.mult).then_inc(ev["gram_used"], 1)
                for q, bank in enumerate((4, 5, 3, 1)):
                    k += 1
                    dve.wait_ge(ev["gram"], at("gram", c, k))
                    dve.tensor_tensor(mq[:, 2 * q:2 * q + 2, :, :].rearrange("p h a c -> p h (a c)"),
                                      psum[:, bank, :].rearrange("p (h c) -> p h c", h=2),
                                      strict_incl.unsqueeze(1).to_broadcast([P, 2, 2 * C]),
                                      ALU.mult).then_inc(ev["gram_used"], 1)
                for lev in range(LEVELS):
                    for g in range(2):
                        n = 2 * lev + g
                        dve.wait_ge(ev["delta"], at("delta", c, n + 1))
                        dve.sem_inc(delta_seen, 1)
                        dve.copy_predicated(xq[:, 4 * g:4 * g + 4, 0, :],
                                            merge_masks[:, lev, :].unsqueeze(1).to_broadcast([P, 4, C]),
                                            psum[:, 2 * g + 1, :].rearrange("p (h c) -> p h c", c=P)
                                            ).then_inc(ev["x_upd"], 1)
                    if not last:
                        dve_front(lev, c + 1, 1 - par)
                if not last:
                    dve.wait_ge(ev["exps"], at("exps", c + 1))
                    dve.tensor_tensor(carry[:], e_end[:, par, :], e_mid[:, 1 - par, :],
                                      ALU.mult).then_inc(ev["carry"], 1)
                dve.wait_ge(ev["s_new"], at("s_new", c))
                dve.tensor_tensor(state_sum[:], state[:], psum[:, 7, 0:KR * HD].rearrange("p (k d) -> p k d", d=HD),
                                  ALU.add).then_inc(ev["s_sum"], 1)
                dve.wait_ge(ev["y_raw"], at("y_raw", c))
                if not last:
                    dve.wait_ge(ev["s_sum"], at("s_sum", c))
                    dve.wait_ge(ev["carry"], at("carry", c))
                    dve.tensor_tensor(state[:], state_sum[:], carry[:].unsqueeze(2).to_broadcast([P, KR, HD]),
                                      ALU.mult).then_inc(ev["state"], 1)
                y4 = psum[:, 4:6, 0:NB // 2].rearrange("p e (k d) -> p e k d", d=HD)
                dve.tensor_reduce(mean[:].rearrange("p (e k) -> p e k", e=2), y4, AX_X,
                                  ALU.add).then_inc(ev["mean"], 1)
                dve.wait_ge(ev["mean"], at("mean", c, 1))
                dve.tensor_scalar(mean[:], mean[:], 1.0 / HD, None, ALU.mult).then_inc(ev["mean"], 1)
                dve.wait_ge(ev["mean"], at("mean", c))
                if not first:
                    dve.wait_ge(ev["y_turned"], at("y_turned", c - 1))
                for e in range(2):
                    m = dve.tensor_tensor(yc[:].rearrange("p (k e d) -> p e k d", e=2, d=HD)[:, e],
                                          psum[:, 4 + e, 0:NB // 2].rearrange("p (k d) -> p k d", d=HD),
                                          mean[:, e * KR:(e + 1) * KR].unsqueeze(2).to_broadcast([P, KR, HD]),
                                          ALU.subtract)
                m.then_inc(ev["yc"], 1)
                if last:
                    dve_variance(c)

            def dve_variance(c):
                dve.wait_ge(ev["ysq"], at("ysq", c))
                dve.tensor_reduce(var[:], ysq[:].rearrange("p (h d) -> p h d", d=HD), AX_X, ALU.add
                                  ).then_inc(ev["var"], 1)
                dve.wait_ge(ev["var"], at("var", c, 1))
                dve.tensor_scalar(var[:], var[:], 1.0 / HD, 64e-5, ALU.mult, ALU.add).then_inc(ev["var"], 1)

            def dve_mix():
                for piece, rwkv in ((0, True), (2, True), (1, False), (3, True), (2, False), (4, True), (5, True),
                                    (4, False)):
                    dve_front(piece, 0, 0, rwkv, not rwkv)
                dve.wait_ge(mix_made, 4)
                dve_rest(0, 0, True, False)
                with dve.Fori(0, CHUNKS // 2 - 1) as i:
                    for b in range(2):
                        dve_rest(i * 2 + (1 + b), 1 - b, False, False)
                dve_rest(CHUNKS - 1, 1, False, True)

            def add_w_out(st):
                def y_low(h):
                    for k in range(KD):
                        dve.wait_ge(y_high, h * KD + k + 1)
                        dve.tensor_tensor(aL[:, k, half(h)], y_out[:, k, half(h)],
                                          aH[:, k, half(h)].bitcast(F32), ALU.subtract).then_inc(y_split, 1)

                def group(i, first, last):
                    for n, (j, h) in enumerate(items(first or last)):
                        dve.wait_ge(w_out_done, i * 4 + (n + 1))
                        if frees(n, first or last):
                            dve.sem_inc(w_free, frees(n, first or last))
                        hk = hT[:, bass.ds(i * 2 + j, 1), half(h)].rearrange("p a c -> p (a c)")
                        dve.tensor_tensor(hk, hk, psum[:, n, :], ALU.add).then_inc(w_out_added, 1)
                        dve.wait_ge(w_out_added, i * 4 + (n + 5))
                        sum_square("ffn2", i * 4 + (n + 1), hk, n, h, first and j == 0)
                        if first and n == 0:
                            y_low(1)
                        if last and n == 1:
                            for k in range(KD):
                                low("ffn2", 0, k)

                y_low(0)
                group(0, True, False)
                with dve.Fori(1, st.iters - 1) as i:
                    group(i, False, False)
                split_p()
                group(st.iters - 1, False, True)
                for k in range(KD):
                    low("ffn2", 1, k)

            for h in range(HALVES):
                place_x(h)
                if h == 0:
                    dve.wait_ge(vecs_turned, 1)
                    dve.tensor_copy(vecs[:], psum[:, 0, 0:n_rows]).then_inc(vecs_ready, 1)
                    dve.wait_ge(vecs_ready, 1)
                dve.wait_ge(x_used_act, (h + 1) * (TT // 2))
                for k in range(KD):
                    low("ffn1", h, k)
            for k in range(KD):
                sum_square("ffn1", k + 1, hT[:, k, half(1)], k % 2, 1, k == 0, hid)
            hidden_and_adds("ffn1", stages["ffn1"], "mix")
            scale_z(stages["w_in"])
            dve_mix()
            add_w_out(stages["w_out"])
            hidden_and_adds("ffn2", stages["ffn2"], "ple")
            gate_adds(stages["gate"])
            for t in range(3, TT):
                scale_result(t)


_INS = ['x', 'p', 'norm_ffn1', 'ffn1_w1', 'ffn1_w3', 'ffn1_w2', 'norm_mix', 'w_in', 'shift_mu',
        'rwkv_w0', 'rwkv_w_decay', 'rwkv_a0', 'rwkv_w_aaa', 'rwkv_w_gate', 'rwkv_k_k', 'rwkv_k_a',
        'rwkv_r_k', 'rwkv_gn_g', 'rwkv_gn_b', 'sgu_ln_g', 'sgu_ln_b', 'sgu_w_s', 'sgu_b_s', 'w_out',
        'norm_ffn2', 'ffn2_w1', 'ffn2_w3', 'ffn2_w2', 'norm_ple', 'w_ple_gate', 'w_ple', 'norm_final']


def shape_constants(P=128, levels=6):
    row, col = np.arange(P)[:, None], np.arange(P)[None, :]
    mid = row <= P // 2 - 1
    unit = -np.exp(np.float32(-0.5))
    incl, excl = (row <= col), (row < col)
    pairs = (row // 2 == col // 2) & excl
    head = np.stack([np.arange(P) < P // 2, np.arange(P) >= P // 2], axis=1)
    parts = [unit * (incl.astype(np.float32) - mid), unit * (excl.astype(np.float32) - mid),
             row > col, pairs, incl, excl, incl, head]
    for n in range(1, levels + 1):
        b = 2 ** n
        parts.append((row // (2 * b) == col // (2 * b)) & (row % (2 * b) < b) & (col % (2 * b) >= b))
    return np.ascontiguousarray(np.concatenate([a.astype(np.float32) for a in parts], axis=1))


def kernel(**inputs):
    import concourse.bacc as bacc
    from concourse.bass_utils import run_bass_kernel_spmd

    nc = bacc.Bacc("TRN2", target_bir_lowering=False, num_devices=1,
                   dynamic_dma_scratch_size=1024)
    arrays, io = {}, {}
    for name in _INS:
        a = np.ascontiguousarray(inputs[name])
        arrays[f"in_{name}"] = a
        io[name] = nc.dram_tensor(f"in_{name}", a.shape, mybir.dt.from_np(a.dtype), kind="ExternalInput").ap()
    arrays["in_masks"] = shape_constants()
    io["masks"] = nc.dram_tensor("in_masks", arrays["in_masks"].shape, F32, kind="ExternalInput").ap()
    out = nc.dram_tensor("out", inputs["x"].shape, F32, kind="ExternalOutput").ap()
    build(nc, io, out)
    return run_bass_kernel_spmd(nc, [arrays], core_ids=[0]).results[0]["out"]
```
